# Optimizing a Trainium2 kernel written in Bass

```python
import math
import jax, jax.numpy as jnp
from jax import lax
import numpy as np

D_MODEL = 1024
BATCH = 1
SEQ = 256
DEPTH = 4
DEC_BATCH = 8
DEC_SEQ = 1
PAST_LEN = 256
PAGE_SIZE = 128

N_MIXERS = 3
EPS = 1e-6
NEG = -1e30
TINY = 1e-30
D_FF = 2816
CONV_W = 3
HEAD_DIM = 64
NSA_HEADS = 16
NSA_GROUPS = 4
NSA_HPG = NSA_HEADS // NSA_GROUPS
CMP_BLOCK = 32
SEL_BLOCK = 64
CMP_PER_SEL = SEL_BLOCK // CMP_BLOCK
N_SEL = 8
WINDOW = 512
NSA_QB = 64
FORCE_SCORE = 1e4
NSA_QW = NSA_HEADS * HEAD_DIM
NSA_KVW = NSA_GROUPS * 6 * HEAD_DIM
NSA_IN = NSA_QW + NSA_KVW + NSA_HEADS * 3
DIFF_HEADS = 8
DIFF_KV_HEADS = 4
DIFF_REP = DIFF_HEADS // DIFF_KV_HEADS
DIFF_QW = DIFF_HEADS * 2 * HEAD_DIM
DIFF_IN = DIFF_QW + DIFF_KV_HEADS * 4 * HEAD_DIM
DIFF_QB = 128
N_CONV = (DEPTH + 2) // 3
N_NSA = (DEPTH + 1) // 3
N_DIFF = DEPTH // 3

kernel_name = 'hybrid_conv_nsa_diffattn_decoder_step'

def rms_norm(x, g):
    xf = x.astype(jnp.float32)
    y = xf * lax.rsqrt(jnp.mean(xf * xf, axis=-1, keepdims=True) + EPS)
    return (y * g.astype(jnp.float32)).astype(x.dtype)

def masked_softmax(s, mask):
    s = jnp.where(mask, s.astype(jnp.float32), NEG)
    m = jnp.max(s, axis=-1, keepdims=True)
    p = jnp.where(mask, jnp.exp(s - m), 0.0)
    return p / jnp.maximum(jnp.sum(p, axis=-1, keepdims=True), TINY)

def half_ffn(x, g_pre, g_post, w_in, w_out):
    gate, up = jnp.split(rms_norm(x, g_pre) @ w_in, 2, axis=-1)
    return x + 0.5 * rms_norm((jax.nn.silu(gate) * up) @ w_out, g_post)

def short_conv(h, buf, w_in, w_conv, w_out):
    T = h.shape[1]
    c, b, v = jnp.split(h @ w_in, 3, axis=-1)
    u = jnp.concatenate([buf.astype(h.dtype), c * v], axis=1)
    y = w_conv[0] * u[:, 0:T]
    for j in range(1, CONV_W):
        y = y + w_conv[j] * u[:, j:j + T]
    return (b * y) @ w_out, u[:, T:]

def nsa_project(h, w_in):
    B, T, _ = h.shape
    p = h @ w_in
    q = p[..., :NSA_QW].reshape(B, T, NSA_GROUPS, NSA_HPG, HEAD_DIM)
    kv = p[..., NSA_QW:NSA_QW + NSA_KVW].reshape(B, T, NSA_GROUPS, 6 * HEAD_DIM)
    gates = jax.nn.sigmoid(p[..., NSA_QW + NSA_KVW:]).reshape(B, T, NSA_GROUPS, NSA_HPG, 3)
    return q, kv, gates

def nsa_blocks(rows, w_cmp):
    B, L, G, _ = rows.shape
    n_sel = -(-L // SEL_BLOCK)
    n_cmp = n_sel * CMP_PER_SEL
    rows = jnp.pad(rows, ((0, 0), (0, n_sel * SEL_BLOCK - L), (0, 0), (0, 0)))
    k_c, v_c, k_s, v_s = jnp.split(rows, 4, axis=-1)
    kc = jnp.einsum('bnlgd,ld->bngd', k_c.reshape(B, n_cmp, CMP_BLOCK, G, HEAD_DIM), w_cmp[0])
    vc = jnp.einsum('bnlgd,ld->bngd', v_c.reshape(B, n_cmp, CMP_BLOCK, G, HEAD_DIM), w_cmp[1])
    ks = k_s.reshape(B, n_sel, SEL_BLOCK, G, HEAD_DIM).transpose(0, 3, 1, 2, 4)
    vs = v_s.reshape(B, n_sel, SEL_BLOCK, G, HEAD_DIM).transpose(0, 3, 1, 2, 4)
    return kc, vc, ks, vs

def nsa_attend(q, gates, q_pos, blocks, win, w_pos):
    kc, vc, ks, vs = blocks
    B, Tq = q.shape[:2]
    scale = HEAD_DIM ** -0.5
    n_cmp = kc.shape[1]
    cmp_end = (jnp.arange(n_cmp, dtype=jnp.int32) + 1) * CMP_BLOCK - 1
    mask_c = (cmp_end[None, :] <= q_pos[:, None])[None, :, None, None, :]
    p_c = masked_softmax(jnp.einsum('bqghd,bngd->bqghn', q, kc) * scale, mask_c)
    o_c = jnp.einsum('bqghn,bngd->bqghd', p_c.astype(vc.dtype), vc)
    n_sel = ks.shape[2]
    imp = p_c.sum(axis=3).reshape(B, Tq, NSA_GROUPS, n_sel, CMP_PER_SEL).sum(-1)
    blk = jnp.arange(n_sel, dtype=jnp.int32)
    forced = ((q_pos[:, None] // SEL_BLOCK) == blk[None, :]) | (blk == 0)[None, :]
    valid = (blk * SEL_BLOCK)[None, :] <= q_pos[:, None]
    imp = jnp.where(forced[None, :, None, :], FORCE_SCORE,
                    jnp.where(valid[None, :, None, :], imp, NEG))
    k_top = min(N_SEL, n_sel)
    _, idx = lax.top_k(imp, k_top)
    idx = idx.transpose(0, 2, 1, 3)
    bi = jnp.arange(B)[:, None, None, None]
    gi = jnp.arange(NSA_GROUPS)[None, :, None, None]
    k_g = ks[bi, gi, idx]
    v_g = vs[bi, gi, idx].reshape(B, NSA_GROUPS, Tq, k_top * SEL_BLOCK, HEAD_DIM)
    key_pos = idx[..., None] * SEL_BLOCK + jnp.arange(SEL_BLOCK, dtype=jnp.int32)
    mask_s = (key_pos <= q_pos[None, None, :, None, None]).transpose(0, 2, 1, 3, 4)
    mask_s = mask_s.reshape(B, Tq, NSA_GROUPS, 1, k_top * SEL_BLOCK)
    s_s = jnp.einsum('bqghd,bgqkld->bqghkl', q, k_g) * scale
    p_s = masked_softmax(s_s.reshape(B, Tq, NSA_GROUPS, NSA_HPG, k_top * SEL_BLOCK), mask_s)
    o_s = jnp.einsum('bqghn,bgqnd->bqghd', p_s.astype(v_g.dtype), v_g)
    kw, vw = jnp.split(win, 2, axis=-1)
    mask_w = ((w_pos[None, :] <= q_pos[:, None]) & (w_pos[None, :] > q_pos[:, None] - WINDOW)
              & (w_pos[None, :] >= 0))[None, :, None, None, :]
    p_w = masked_softmax(jnp.einsum('bqghd,bkgd->bqghk', q, kw) * scale, mask_w)
    o_w = jnp.einsum('bqghk,bkgd->bqghd', p_w.astype(vw.dtype), vw)
    return gates[..., 0:1] * o_c + gates[..., 1:2] * o_s + gates[..., 2:3] * o_w

def nsa_prompt(h, w_in, w_cmp, w_out):
    B, T, _ = h.shape
    q, kv, gates = nsa_project(h, w_in)
    rows, win = kv[..., :4 * HEAD_DIM], kv[..., 4 * HEAD_DIM:]
    blocks = nsa_blocks(rows, w_cmp)
    win_pad = jnp.pad(win, ((0, 0), (WINDOW, 0), (0, 0), (0, 0)))

    def chunk(ci):
        c0 = ci * NSA_QB
        qc = lax.dynamic_slice_in_dim(q, c0, NSA_QB, axis=1)
        gc = lax.dynamic_slice_in_dim(gates, c0, NSA_QB, axis=1)
        wc = lax.dynamic_slice_in_dim(win_pad, c0, WINDOW + NSA_QB, axis=1)
        q_pos = c0 + jnp.arange(NSA_QB, dtype=jnp.int32)
        w_pos = c0 - WINDOW + jnp.arange(WINDOW + NSA_QB, dtype=jnp.int32)
        return nsa_attend(qc, gc, q_pos, blocks, wc, w_pos)

    o = lax.map(chunk, jnp.arange(T // NSA_QB, dtype=jnp.int32))
    o = jnp.moveaxis(o, 0, 1).reshape(B, T, NSA_QW)
    return o @ w_out, rows, win[:, T - min(WINDOW, T):]

def nsa_sample(h, cache, win_buf, page_table, w_in, w_cmp, w_out):
    B, T, _ = h.shape
    q, kv, gates = nsa_project(h, w_in)
    rows, win_new = kv[..., :4 * HEAD_DIM], kv[..., 4 * HEAD_DIM:]
    past_len = page_table.shape[1] * cache.shape[1]
    past = cache[page_table].reshape(B, past_len, NSA_GROUPS, 4 * HEAD_DIM).astype(rows.dtype)
    blocks = nsa_blocks(jnp.concatenate([past, rows], axis=1), w_cmp)
    w_buf = win_buf.shape[1]
    win = jnp.concatenate([win_buf.astype(win_new.dtype), win_new], axis=1)
    q_pos = past_len + jnp.arange(T, dtype=jnp.int32)
    w_pos = past_len - w_buf + jnp.arange(w_buf + T, dtype=jnp.int32)
    o = nsa_attend(q, gates, q_pos, blocks, win, w_pos)
    return o.reshape(B, T, NSA_QW) @ w_out, rows, win[:, T:]

def diff_project(h, w_in):
    B, T, _ = h.shape
    p = h @ w_in
    q = p[..., :DIFF_QW].reshape(B, T, DIFF_KV_HEADS, DIFF_REP, 2, HEAD_DIM)
    kv = p[..., DIFF_QW:].reshape(B, T, DIFF_KV_HEADS, 4 * HEAD_DIM)
    return q, kv

def diff_lambda_value(lam_p, lam_init):
    lp = lam_p.astype(jnp.float32)
    return jnp.exp(jnp.sum(lp[0] * lp[1])) - jnp.exp(jnp.sum(lp[2] * lp[3])) + lam_init

def diff_attend(q, q_pos, kv, k_pos, lam):
    B, Tk = kv.shape[:2]
    k = kv[..., :2 * HEAD_DIM].reshape(B, Tk, DIFF_KV_HEADS, 2, HEAD_DIM)
    v = kv[..., 2 * HEAD_DIM:]
    s = jnp.einsum('bqgrmd,bkgmd->bgrmqk', q, k) * HEAD_DIM ** -0.5
    p = masked_softmax(s, k_pos[None, :] <= q_pos[:, None])
    a = (p[:, :, :, 0] - lam * p[:, :, :, 1]).astype(v.dtype)
    return jnp.einsum('bgrqk,bkgd->bqgrd', a, v)

def diff_output(o, lam_init, subln_g, w_out):
    B, T = o.shape[:2]
    o = rms_norm(o, subln_g) * (1.0 - lam_init)
    return o.reshape(B, T, DIFF_HEADS * 2 * HEAD_DIM) @ w_out

def diff_prompt(h, w_in, lam_p, lam_init, subln_g, w_out):
    B, T, _ = h.shape
    q, kv = diff_project(h, w_in)
    lam = diff_lambda_value(lam_p, lam_init)
    k_pos = jnp.arange(T, dtype=jnp.int32)

    def block(ci):
        c0 = ci * DIFF_QB
        qb = lax.dynamic_slice_in_dim(q, c0, DIFF_QB, axis=1)
        return diff_attend(qb, c0 + jnp.arange(DIFF_QB, dtype=jnp.int32), kv, k_pos, lam)

    o = lax.map(block, jnp.arange(T // DIFF_QB, dtype=jnp.int32))
    o = jnp.moveaxis(o, 0, 1).reshape(B, T, DIFF_KV_HEADS, DIFF_REP, 2 * HEAD_DIM)
    return diff_output(o, lam_init, subln_g, w_out), kv

def diff_sample(h, cache, page_table, w_in, lam_p, lam_init, subln_g, w_out):
    B, T, _ = h.shape
    q, kv = diff_project(h, w_in)
    past_len = page_table.shape[1] * cache.shape[1]
    past = cache[page_table].reshape(B, past_len, DIFF_KV_HEADS, 4 * HEAD_DIM).astype(kv.dtype)
    keys = jnp.concatenate([past, kv], axis=1)
    k_pos = jnp.arange(past_len + T, dtype=jnp.int32)
    q_pos = past_len + jnp.arange(T, dtype=jnp.int32)
    o = diff_attend(q, q_pos, keys, k_pos, diff_lambda_value(lam_p, lam_init))
    return diff_output(o, lam_init, subln_g, w_out), kv

def setup_inputs(seed: int = 0) -> dict:
    key = jax.random.key(seed)
    ks = jax.random.split(key, 24)
    f32 = jnp.float32

    def nrm(k, shape, scale):
        return jax.random.normal(k, shape, f32) * scale

    n_pages = PAST_LEN // PAGE_SIZE
    n_used = DEC_BATCH * n_pages
    n_phys = n_used + (n_used + 3) // 4
    w_buf = min(WINDOW, PAST_LEN)
    page_table = jax.random.permutation(ks[6], n_phys)[:n_used].reshape(DEC_BATCH, n_pages).astype(jnp.int32)
    return {
        'x_prompt': nrm(ks[0], (BATCH, SEQ, D_MODEL), 1.0),
        'x_sample': nrm(ks[1], (DEC_BATCH, DEC_SEQ, D_MODEL), 1.0),
        'state_conv': nrm(ks[2], (N_CONV, DEC_BATCH, CONV_W - 1, D_MODEL), 1.0),
        'cache_nsa': nrm(ks[3], (N_NSA, n_phys, PAGE_SIZE, NSA_GROUPS, 4 * HEAD_DIM), 1.0),
        'state_nsa_win': nrm(ks[4], (N_NSA, DEC_BATCH, w_buf, NSA_GROUPS, 2 * HEAD_DIM), 1.0),
        'cache_diff': nrm(ks[5], (N_DIFF, n_phys, PAGE_SIZE, DIFF_KV_HEADS, 4 * HEAD_DIM), 1.0),
        'page_table': page_table,
        'norm_g': 1.0 + nrm(ks[7], (DEPTH, 6, D_MODEL), 0.02),
        'ffn_w_in': nrm(ks[8], (DEPTH, 2, D_MODEL, 2 * D_FF), D_MODEL ** -0.5),
        'ffn_w_out': nrm(ks[9], (DEPTH, 2, D_FF, D_MODEL), D_FF ** -0.5),
        'conv_w_in': nrm(ks[10], (N_CONV, D_MODEL, 3 * D_MODEL), D_MODEL ** -0.5),
        'conv_w': nrm(ks[11], (N_CONV, CONV_W, D_MODEL), CONV_W ** -0.5),
        'conv_w_out': nrm(ks[12], (N_CONV, D_MODEL, D_MODEL), D_MODEL ** -0.5),
        'nsa_w_in': nrm(ks[13], (N_NSA, D_MODEL, NSA_IN), D_MODEL ** -0.5),
        'nsa_w_cmp': nrm(ks[14], (N_NSA, 2, CMP_BLOCK, HEAD_DIM), CMP_BLOCK ** -0.5),
        'nsa_w_out': nrm(ks[15], (N_NSA, NSA_QW, D_MODEL), NSA_QW ** -0.5),
        'diff_w_in': nrm(ks[16], (N_DIFF, D_MODEL, DIFF_IN), D_MODEL ** -0.5),
        'diff_lambda': nrm(ks[17], (N_DIFF, 4, HEAD_DIM), 0.1),
        'diff_subln_g': 1.0 + nrm(ks[18], (N_DIFF, 2 * HEAD_DIM), 0.02),
        'diff_w_out': nrm(ks[19], (N_DIFF, DIFF_QW, D_MODEL), DIFF_QW ** -0.5),
    }

def reference(x_prompt, x_sample, state_conv, cache_nsa, state_nsa_win, cache_diff, page_table,
              norm_g, ffn_w_in, ffn_w_out, conv_w_in, conv_w, conv_w_out,
              nsa_w_in, nsa_w_cmp, nsa_w_out, diff_w_in, diff_lambda, diff_subln_g, diff_w_out):
    xp, xs = x_prompt, x_sample
    conv_p, conv_s, nsa_p, nsa_s, win_p, win_s, diff_p, diff_s = [], [], [], [], [], [], [], []
    for i in range(DEPTH):
        g = norm_g[i]
        kind, j = i % N_MIXERS, i // N_MIXERS
        xp = half_ffn(xp, g[0], g[1], ffn_w_in[i, 0], ffn_w_out[i, 0])
        xs = half_ffn(xs, g[0], g[1], ffn_w_in[i, 0], ffn_w_out[i, 0])
        hp, hs = rms_norm(xp, g[2]), rms_norm(xs, g[2])
        if kind == 0:
            zero_buf = jnp.zeros((hp.shape[0], CONV_W - 1, hp.shape[2]), hp.dtype)
            yp, st = short_conv(hp, zero_buf, conv_w_in[j], conv_w[j], conv_w_out[j])
            conv_p.append(st)
            ys, st = short_conv(hs, state_conv[j], conv_w_in[j], conv_w[j], conv_w_out[j])
            conv_s.append(st)
        elif kind == 1:
            yp, rows, win = nsa_prompt(hp, nsa_w_in[j], nsa_w_cmp[j], nsa_w_out[j])
            nsa_p.append(rows)
            win_p.append(win)
            ys, rows, win = nsa_sample(hs, cache_nsa[j], state_nsa_win[j], page_table,
                                       nsa_w_in[j], nsa_w_cmp[j], nsa_w_out[j])
            nsa_s.append(rows)
            win_s.append(win)
        else:
            lam_init = 0.8 - 0.6 * math.exp(-0.3 * i)
            yp, rows = diff_prompt(hp, diff_w_in[j], diff_lambda[j], lam_init, diff_subln_g[j], diff_w_out[j])
            diff_p.append(rows)
            ys, rows = diff_sample(hs, cache_diff[j], page_table, diff_w_in[j], diff_lambda[j],
                                   lam_init, diff_subln_g[j], diff_w_out[j])
            diff_s.append(rows)
        xp = xp + rms_norm(yp, g[3])
        xs = xs + rms_norm(ys, g[3])
        xp = half_ffn(xp, g[4], g[5], ffn_w_in[i, 1], ffn_w_out[i, 1])
        xs = half_ffn(xs, g[4], g[5], ffn_w_in[i, 1], ffn_w_out[i, 1])
    new_conv_prompt = jnp.stack(conv_p)
    new_conv_sample = jnp.stack(conv_s)
    new_nsa_kv_prompt = jnp.stack(nsa_p)
    new_nsa_kv_sample = jnp.stack(nsa_s)
    new_nsa_win_prompt = jnp.stack(win_p)
    new_nsa_win_sample = jnp.stack(win_s)
    new_diff_kv_prompt = jnp.stack(diff_p)
    new_diff_kv_sample = jnp.stack(diff_s)
    return (xp, xs, new_conv_prompt, new_conv_sample, new_nsa_kv_prompt, new_nsa_kv_sample,
            new_nsa_win_prompt, new_nsa_win_sample, new_diff_kv_prompt, new_diff_kv_sample)


_drawn_inputs = setup_inputs


def setup_inputs(seed=0):
    import zlib

    import numpy as np

    out = dict(_drawn_inputs(seed))
    spreads = {}
    factors = {}
    for name, (base, spread) in spreads.items():
        noise = np.random.default_rng([zlib.crc32(name.encode()), seed]).standard_normal(out[name].shape)
        drawn = base * np.exp(spread * noise) if base else spread * noise
        out[name] = __import__('jax').numpy.asarray(drawn.astype(out[name].dtype))
    for name, factor in factors.items():
        out[name] = (out[name] * factor).astype(out[name].dtype)
    return out
```

```python
import math
from contextlib import ExitStack

import concourse.bass as bass
from concourse import mybir

F32 = mybir.dt.float32
F32R = mybir.dt.float32r
BF16 = mybir.dt.bfloat16
I32 = mybir.dt.int32
ALU = mybir.AluOpType
ACT = mybir.ActivationFunctionType
AX_X = mybir.AxisListType.X

P = 128
D_MODEL = 1024
SEQ = 256
DEC = 8
T = SEQ + DEC
DEPTH = 4
PAGE = 128
N_PAGES = 2
D_FF = 2816
HEAD = 64
GROUPS = 4
CMP_BLOCK = 32
N_CMP = SEQ // CMP_BLOCK
EPS = 1e-6
NEG = -1e30
TINY = 1e-30
NC = D_MODEL // P
NF = D_FF // P
HC = 4
GT = 4
GC = GT * P
RING = 4
NSA_QW = 1024
NSA_KVW = GROUPS * 6 * HEAD
NSA_IN = NSA_QW + NSA_KVW + 48
NSA_KVT = NSA_KVW // P
DIFF_KVT = 8
SCALE = HEAD ** -0.5
TOK = [(0, P), (P, P), (SEQ, DEC)]


def lam_init(layer):
    return 0.8 - 0.6 * math.exp(-0.3 * layer)


class Group:

    def __init__(self, kind, n, unit0, units, sub, index, tiles=GT):
        self.kind, self.n, self.unit0, self.units, self.sub, self.index, self.tiles = \
            kind, n, unit0, units, sub, index, tiles
        self.set = index % 2
        self.end = unit0 + len(units)


class Sublayer:
    pass


def make_plan():
    subs, unit, index, attends, convs, hlow = [], 0, 0, 0, 0, 0
    stage = []
    cache_unit = 0
    for layer in range(DEPTH):
        for part in range(3):
            s = Sublayer()
            s.i, s.layer, s.part = len(subs), layer, part
            mixer = ("conv", "nsa", "diff")[layer % 3]
            s.kind = mixer if part == 1 else "ffn"
            kinds = {"ffn": ["ffn_in"] * (NF // 2), "conv": ["conv_cv"] * 4 + ["conv_b"] * 2,
                     "nsa": ["q"] * 2 + ["kv"] * 3 + ["gate"], "diff": ["q"] * 2 + ["kv"] * 2}[s.kind]
            s.ins = []
            for n, kind in enumerate(kinds):
                s.ins.append(Group(kind, n, unit, [HC] * (NC // HC), s.i, index, 1 if kind == "gate" else GT))
                unit, index = unit + NC // HC, index + 1
            k_chunks = NF if s.kind == "ffn" else NC
            per = [HC] * (k_chunks // HC) + ([k_chunks % HC] if k_chunks % HC else [])
            s.outs = []
            for n in range(2):
                s.outs.append(Group("out", n, unit, per, s.i, index))
                unit, index = unit + len(per), index + 1
            s.h_piece = {"ffn": 2, "conv": 4, "nsa": 8, "diff": 8}[s.kind]
            s.h_before = hlow
            hlow += 0 if s.kind in ("nsa", "diff") else k_chunks // s.h_piece
            s.ffn = 2 * layer + part // 2
            s.conv, s.attend = convs, attends
            attends += s.kind in ("nsa", "diff")
            convs += s.kind == "conv"
            s.cache_units = {"nsa": 2 * DEC, "diff": DEC}.get(s.kind, 0)
            s.cache0 = cache_unit
            order = [("w", u) for g in s.ins for u in range(g.unit0, g.end)]
            outs = [("w", u) for g in s.outs for u in range(g.unit0, g.end)]
            order += outs[:2] + [("c", cache_unit + n) for n in range(s.cache_units)] + outs[2:]
            cache_unit += s.cache_units
            stage += order
            subs.append(s)
    return subs, stage


def trunk_kernel(nc, x_prompt, x_sample, state_conv, cache_nsa, state_nsa_win, cache_diff, page_table,
                 norm_g, ffn_w_in, ffn_w_out, conv_w_in, conv_w, conv_w_out,
                 nsa_w_in, nsa_w_cmp, nsa_w_out, diff_w_in, diff_lambda, diff_subln_g, diff_w_out,
                 y_prompt, y_sample, new_conv_prompt, new_conv_sample, new_nsa_kv_prompt, new_nsa_kv_sample,
                 new_nsa_win_prompt, new_nsa_win_sample, new_diff_kv_prompt, new_diff_kv_sample):
    subs, stage_order = make_plan()
    stage_of = {item: n for n, item in enumerate(stage_order)}
    n_norm = DEPTH * 6 * NC
    n_convw = 2 * 3 * NC
    gain_rows = n_norm + n_convw + 1
    cols_b = gain_rows - P

    ctx = ExitStack()
    with ctx:
        base = (nc.sbuf_base + 31) // 32 * 32
        cursor = [base]

        def place(name, shape, dt=F32, at=None):
            size = (math.prod(shape[1:]) * (2 if dt == BF16 else 4) + 31) // 32 * 32
            if at is None:
                at = cursor[0]
                cursor[0] += size
            return nc.alloc_sbuf_tensor_at(name, shape, dt, offset=at)

        def sem(name):
            return ctx.enter_context(nc.semaphore(name))

        wstage = place("wstage", [P, RING, HC, GC])
        w_at = cursor[0]
        w_high_ring = place("w_high_ring", [P, RING, HC, GC], F32R)
        w_low_ring = place("w_low_ring", [P, RING, HC, GC], F32R)
        slot_bytes = HC * GC * 4
        x = place("x", [P, NC, T])
        x_hi_at = cursor[0]
        x_hi = place("x_hi", [P, NC, T], F32R)
        x_lo = place("x_lo", [P, NC, T], F32R)
        y_at = cursor[0]
        y = place("y", [P, NC, T])
        sq_at = cursor[0]
        sq = place("sq", [P, NC, T])
        tmp_at = cursor[0]
        tmp = place("tmp", [P, NC, T])
        arena = cursor[0]
        h_hi = place("h_hi", [P, NF, T], F32R)
        arena_low = cursor[0]
        h_lo = place("h_lo", [P, NF, T], F32R)
        sum_pre = place("sum_pre", [P, T])
        sum_post = place("sum_post", [P, T])
        r_pre = place("r_pre", [P, T])
        ident = place("ident", [P, P])
        ident_r = place("ident_r", [P, P], F32R)
        ident_b = place("ident_b", [P, P], BF16)
        causal = place("causal", [P, P], BF16)
        gains = place("gains", [P, gain_rows])
        conv_state = place("conv_state", [P, NC, 32])
        cmp_w = place("cmp_w", [P, CMP_BLOCK])
        cmp_w_tok = place("cmp_w_tok", [P, P])
        cmp_ok = place("cmp_ok", [P, 2, N_CMP])
        cmp_bias = place("cmp_bias", [P, 2, N_CMP])
        head_of_row = place("head_of_row", [P, 16])
        own_cmp = place("own_cmp", [P, 32, N_CMP], BF16)
        own_new = place("own_new", [P, 4, DEC], BF16)
        block_of_row = place("block_of_row", [P, 4])
        mean_col = place("mean_col", [P, 2])
        var = place("var", [P, 3])
        rs = place("rs", [P, 3])
        rs_hi = place("rs_hi", [P, 3], F32R)
        rs_lo = place("rs_lo", [P, 3], F32R)
        minus_half = place("minus_half", [P, 32])
        pages = place("pages", [1, 16], I32)
        conv_tok = place("conv_tok", [18, D_MODEL], at=cursor[0])
        kv_sample = place("kv_sample", [DEC, NSA_KVW])
        small = place("small", [P, 288])
        assert cursor[0] <= nc.sbuf_usable_end, (cursor[0], nc.sbuf_usable_end)

        gate_t, up_t, tanh_t, prod_t = (tmp[:, 2 * k:2 * k + 2, :] for k in range(4))
        tmp4 = tmp[:, 4:8, :]
        gates = small[:, 0:144].rearrange("p (t c) -> p t c", t=3)
        gate_rows = small[:, 144:147]
        lam = small[:, 147:148]
        neg_lam = small[:, 148:149]
        even_row = small[:, 149:150]
        dec_sign = small[:, 150:151]
        s_mx, s_nmx, s_sum, s_coef = ([small[:, 161 + 3 * k + r:162 + 3 * k + r] for r in range(3)] for k in range(4))
        lam_s = small[:, 156:158]
        lam_e = small[:, 158:160]
        sub_gain = small[:, 160:161]
        sub_v, sub_r = small[:, 16:32], small[:, 0:16]
        mx, nmx, esum, coef = (small[:, 176 + 16 * k:192 + 16 * k].rearrange("p (b c) -> p b c", b=4)
                               for k in range(4))
        tok_in = place("tok_in", [P, 3, D_MODEL], at=arena)
        gain_a = place("gain_a", [P, P], at=arena + 12288)
        gain_b = place("gain_b", [cols_b, P], at=arena + 12800)
        state_tok = place("state_tok", [32, D_MODEL], at=arena + 13312)
        cmp_tok = place("cmp_tok", [CMP_BLOCK, P], at=arena + 17408)
        lam_in = place("lam_in", [P, 4, HEAD], at=arena + 17920)
        lam_p = place("lam_p", [P, 2, HEAD], at=arena + 18944)
        y_tok = place("y_tok", [P, 3, D_MODEL], at=arena)
        u_prompt = place("u_prompt", [P, NC, SEQ + 2], at=arena + NC * T * 4)
        u_sample = place("u_sample", [P, NC, 3, DEC], at=arena + NC * T * 4 + NC * (SEQ + 2) * 4)
        conv_new = place("conv_new", [P, NC, 18], at=arena_low + NC * T * 4)
        q_t = place("q_t", [P, NC, T], at=y_at)
        o_tok = place("o_tok", [P, 2, D_MODEL], at=sq_at)
        k_odd = place("k_odd", [P, GROUPS, 2, SEQ], at=tmp_at)
        kv_t = place("kv_t", [P, NSA_KVT, T], at=arena)
        kv_tok = place("kv_tok", [P, 2, NSA_KVW], at=arena + 12672)
        probs = place("probs", [P, 2, 4, SEQ], at=arena + 24960)
        probs_t = place("probs_t", [P, 2, 4, 2, P], at=arena + 33152)
        vc_diag = place("vc_diag", [P, 16, HEAD], at=arena + 41344)
        kc_t = place("kc_t", [P, GROUPS, N_CMP], at=arena + 45440)
        kc_odd = place("kc_odd", [P, GROUPS, N_CMP], at=arena + 45568)
        vc_rep = place("vc_rep", [P, GROUPS, 4, N_CMP], at=arena + 45696)
        gate_t1 = place("gate_t1", [P, T], at=sq_at)
        cmp_prod = place("cmp_prod", [P, GROUPS, N_CMP, CMP_BLOCK], at=arena + 24960)
        cmp_s = place("cmp_s", [P, 2, 16, N_CMP], at=arena + 33152)
        cmp_e = place("cmp_e", [P, 2, 16, N_CMP], at=arena + 34176)
        cmp_m = place("cmp_m", [P, 2, 16], at=arena + 35200)
        cmp_pt = place("cmp_pt", [P, 2, P], at=arena + 36224)
        o_scaled = place("o_scaled", [P, 2, 512], at=arena + 41344)
        o_square = place("o_square", [P, 2, D_MODEL], at=tmp_at)
        even_tmp = place("even_tmp", [P, 64], at=arena + 19968)
        kt_dec = place("kt_dec", [P, 2, 2, P], at=x_hi_at)
        prod_dec = place("prod_dec", [P, 2, GROUPS, P], at=x_hi_at + 2048)
        st_dec = place("st_dec", [P, 2, 2, P], at=x_hi_at + 6144)
        kc_dec = place("kc_dec", [P, SEQ], at=x_hi_at + 8448)
        q_dec = place("q_dec", [P, P], at=x_hi_at + 9472)
        q_pair = place("q_pair", [P, P], at=x_hi_at + 9984)
        k_pairs = place("k_pairs", [P, 2, 2, GROUPS, HEAD], at=x_hi_at + 10496)
        dec = arena + 33152
        p_dec = place("p_dec", [P, 3, SEQ + 32], at=dec)
        pt_dec = place("pt_dec", [P, 2, 2, P], at=dec + 3456)
        ptn_dec = place("ptn_dec", [DEC, 2, GROUPS, P], at=dec + 5504)
        vc_dec = place("vc_dec", [P, 2, HEAD], at=dec + 9600)
        o_dec = place("o_dec", [P, P], at=dec + 10112)
        z_dec = place("z_dec", [P, NC, DEC], at=dec + 10624)

        ps = ctx.enter_context(nc.psum_tensor("ps", [P, 8, 512], F32))

        loaded = [sem(f"stage_loaded{k}") for k in range(RING)]
        w_high = sem("w_high")
        w_low = sem("w_low")
        unit_used = sem("unit_used")
        psum_drained = sem("psum_drained")
        x_updated = sem("x_updated")
        x_high = sem("x_high")
        x_low = sem("x_low")
        x_squared = sem("x_squared")
        pre_summed = sem("pre_summed")
        stats_done = sem("stats_done")
        var_ready = sem("var_ready")
        rs_ready = sem("rs_ready")
        bcast_done = sem("bcast_done")
        rstd_ready = sem("rstd_ready")
        gate_scaled = sem("gate_scaled")
        tanh_done = sem("tanh_done")
        prod_ready = sem("prod_ready")
        h_full = sem("h_full")
        h_high = sem("h_high")
        h_low = sem("h_low")
        y_copied = sem("y_copied")
        y_squared = sem("y_squared")
        tile_done = sem("tile_done")
        post_added = sem("post_added")
        y_scaled = sem("y_scaled")
        conv_step = sem("conv_step")
        conv_gathered = sem("conv_gathered")
        conv_turned = sem("conv_turned")
        conv_copied = sem("conv_copied")
        small_loaded = sem("small_loaded")
        xs_loaded = sem("xs_loaded")
        consts_ready = sem("consts_ready")
        pool_step = sem("pool_step")
        init_turned = sem("init_turned")
        init_copied = sem("init_copied")
        x_turned = sem("x_turned")
        lam_exp = sem("lam_exp")
        tok_turned = sem("tok_turned")
        tok_copied = sem("tok_copied")
        gates_turned = sem("gates_turned")
        gates_tanh = sem("gates_tanh")
        gates_ready = sem("gates_ready")
        gate_rows_loaded = sem("gate_rows_loaded")
        att_step = sem("att_step")
        cmp_keys = sem("cmp_keys")
        cmp_vals = sem("cmp_vals")
        o_normed = sem("o_normed")
        cmp_turned = sem("cmp_turned")
        cmp_scores = sem("cmp_scores")
        cmp_shifted = sem("cmp_shifted")
        cmp_exp = sem("cmp_exp")
        cmp_probs = sem("cmp_probs")
        cmp_pt_done = sem("cmp_pt_done")
        cmp_pt_copied = sem("cmp_pt_copied")
        cmp_out = sem("cmp_out")
        cmp_added = sem("cmp_added")
        keys_odd = sem("keys_odd")
        at_scores = sem("at_scores")
        at_max = sem("at_max")
        at_exp = sem("at_exp")
        at_turned = sem("at_turned")
        at_copied = sem("at_copied")
        at_pv = sem("at_pv")
        at_scaled = sem("at_scaled")
        at_added = sem("at_added")
        dec_q = sem("dec_q")
        keys_paired = sem("keys_paired")
        cache_turned = sem("cache_turned")
        cache_keys = sem("cache_keys")
        cache_kept = sem("cache_kept")
        cache_scored = sem("cache_scored")
        cache_prod = sem("cache_prod")
        cache_summed = sem("cache_summed")
        kc_copied = sem("kc_copied")
        st_copied = sem("st_copied")
        dec_scores = sem("dec_scores")
        dec_max = sem("dec_max")
        dec_exp = sem("dec_exp")
        dec_probs = sem("dec_probs")
        dec_turned = sem("dec_turned")
        dec_copied = sem("dec_copied")
        dec_pv = sem("dec_pv")
        dec_added = sem("dec_added")
        dec_placed = sem("dec_placed")
        sub_squared = sem("sub_squared")
        sub_stats = sem("sub_stats")
        sub_var = sem("sub_var")
        sub_rs = sem("sub_rs")
        sub_bcast = sem("sub_bcast")
        z_turned = sem("z_turned")
        z_high = sem("z_high")
        y_turned = sem("y_turned")
        y_out = sem("y_out")
        z_low = sem("z_low")
        dve_const = sem("dve_const")
        lam_summed = sem("lam_summed")
        sub_added = sem("sub_added")
        gates_out = sem("gates_out")
        tok_stored = sem("tok_stored")
        conv_stored = sem("conv_stored")
        win_moved = sem("win_moved")
        y_stored = sem("y_stored")

        gate_scratch = nc.dram_tensor("gate_scratch", (DEC, 48), F32, kind="Internal").ap()

        block = ctx.enter_context(nc.Block())

        def rows(w):
            return w.rearrange("(c p) n -> p c n", p=P)

        def b3(ap, n):
            return ap.unsqueeze(1).broadcast_to([P, n, T])

        def gset(group, tiles=GT):
            b = 4 * (group.set if isinstance(group, Group) else group)
            return ps[:, b:b + tiles, 0:T]

        def gain(layer, j, c):
            k = (layer * 6 + j) * NC + c
            return gains[:, k:k + 1]

        def pre_gain(s, c):
            return gain(s.layer, 2 * s.part, c)

        def post_gain(s, c):
            return gain(s.layer, 2 * s.part + 1, c)

        stores = {}

        def store(dma, signal, key):
            stores[key] = stores.get(key, 0) + 1
            dma.then_inc(signal, 16)

        KV_TILES = {"nsa": NSA_KVT, "diff": DIFF_KVT}
        BATCHES = {k: [(tt, j) for tt in range(3) for j in range(KV_TILES[k] // 4)] for k in KV_TILES}
        TASKS = {"nsa": [(qt, br, g) for qt in range(2) for br in (0, 1) for g in range(GROUPS)],
                 "diff": [(qt, 0, g) for qt in range(2) for g in range(GROUPS)]}
        ROUNDS = {"nsa": ["cmp", "sel", "win"], "diff": ["diff"]}
        PIECES = {"nsa": 2, "diff": 4}
        PLACES = {"nsa": (1, 3), "diff": (0, 1, 2, 3)}
        piece0 = {"nsa": 0, "diff": PIECES["nsa"] * 2 * DEC}

        def piece_at(kind, n, place_in_task):
            if n >= len(TASKS[kind]) or place_in_task not in PLACES[kind]:
                return None
            return n * PIECES[kind] + PLACES[kind].index(place_in_task)

        def pieces_to(n):
            past = 2 * DEC
            return PIECES["nsa"] * (n + 1) if n < past else piece0["diff"] + PIECES["diff"] * (n - past + 1)

        batch0 = {"nsa": 0, "diff": len(BATCHES["nsa"])}
        task0 = {"nsa": 0, "diff": len(TASKS["nsa"])}
        round0 = {"nsa": 0, "diff": len(ROUNDS["nsa"])}
        n_units = subs[-1].outs[-1].end
        unit_shape = {}
        for s in subs:
            for g in s.ins + s.outs:
                for k, n in enumerate(g.units):
                    unit_shape[g.unit0 + k] = (n, g.tiles * P)

        def norm_bank(norm):
            s = subs[norm // 2]
            return 4 * s.outs[1].set if norm % 2 else 4 * s.ins[1].set + 3

        def round_bank(name):
            return {"cmp": 4, "sel": 5, "win": 6, "diff": 5}[name]

        def round_cols(name):
            return DEC * GROUPS * N_CMP if name == "cmp" else SEQ + DEC * GROUPS

        def value_tile(kind, br):
            return (64 + 128 * (br + 1), 384, HEAD) if kind == "nsa" else (128, 256, P)

        def value_home(s):
            free = (s.outs[0].unit0 + 2) % RING
            assert free % 2 == 0
            return w_at + free * slot_bytes, w_at + (RING + free) * slot_bytes

        homes = {}
        for s in subs:
            if s.kind == "nsa":
                a, b = value_home(s)
                homes["sel"] = place("v_sel", [P, DEC, 2, GROUPS, HEAD], at=a)
                homes["win"] = place("v_win", [P, DEC, 2, GROUPS, HEAD], at=b)
            if s.kind == "diff":
                a, b = value_home(s)
                homes["diff"] = [place("v_diff_a", [P, 4, 2, GROUPS, P], at=a),
                                 place("v_diff_b", [P, 4, 2, GROUPS, P], at=b)]

        @block.gpsimd
        def _(pool):
            fill = lambda t, v: nc.gpsimd.memset(t, v).then_inc(pool_step, 1)
            fill(ident[:, :], 0.0)
            fill(cmp_ok[:, :, :], 1.0)
            fill(head_of_row[:, :], 1.0)
            fill(block_of_row[:, :], 1.0)
            fill(tmp[:, 0, 0:256], 0.0)
            fill(tmp[:, 1, 0:256], 0.0)
            fill(tmp[:, 2, 0:32], 0.0)
            fill(mean_col[:, 0:1], 1.0 / D_MODEL)
            fill(mean_col[:, 1:2], 1.0 / P)
            fill(minus_half[:, :], -0.5)
            fill(var[:, :], 1.0)
            fill(small[:, :], 1.0)
            fill(even_tmp[:, :], 0.0)
            n = [13]
            pool.wait_ge(pool_step, n[0])

            def select(t, pattern, op, fill, base, mult):
                nc.gpsimd.affine_select(out=t, in_=t, compare_op=op, fill=fill, base=base,
                                        pattern=pattern, channel_multiplier=mult).then_inc(pool_step, 1)
                n[0] += 1
                pool.wait_ge(pool_step, n[0])

            def copy(dst, src):
                nc.gpsimd.tensor_copy(dst, src).then_inc(consts_ready, 1)

            select(ident[:, :], [[-1, P]], ALU.not_equal, 1.0, 0, 1)
            copy(ident_b[:, :], ident[:, :])
            copy(ident_r[:, :], ident[:, :])
            select(tmp[:, 0, 0:P], [[-1, P]], ALU.is_ge, NEG, 0, 1)
            copy(causal[:, :], tmp[:, 0, 0:P])
            select(cmp_ok[:, :, :], [[P, 2], [-CMP_BLOCK, N_CMP]], ALU.is_ge, 0.0, -(CMP_BLOCK - 1), 1)
            nc.gpsimd.tensor_scalar(cmp_bias[:, :, :], cmp_ok[:, :, :], -1.0, -NEG, ALU.add, ALU.mult)\
                .then_inc(consts_ready, 1)
            select(head_of_row[:, :], [[-N_CMP, 16]], ALU.is_ge, 0.0, 0, 1)
            select(head_of_row[:, :], [[N_CMP, 16]], ALU.is_ge, 0.0, N_CMP - 1, -1)
            select(block_of_row[:, :], [[-CMP_BLOCK, 4]], ALU.is_ge, 0.0, 0, 1)
            select(block_of_row[:, :], [[CMP_BLOCK, 4]], ALU.is_ge, 0.0, CMP_BLOCK - 1, -1)
            select(even_tmp[:, :], [[-2, 64]], ALU.not_equal, 1.0, 0, 1)
            view = tmp[:, 1, 0:256].rearrange("p (j n) -> p j n", n=N_CMP)
            select(view, [[-4, 32], [0, N_CMP]], ALU.is_ge, NEG, 0, 1)
            select(view, [[4, 32], [0, N_CMP]], ALU.is_ge, NEG, 3, -1)
            copy(own_cmp[:, :, :], view)
            view = tmp[:, 2, 0:32].rearrange("p (g b) -> p g b", b=DEC)
            select(view, [[-4, GROUPS], [-16, DEC]], ALU.is_ge, NEG, 0, 1)
            select(view, [[4, GROUPS], [16, DEC]], ALU.is_ge, NEG, 3, -1)
            copy(own_new[:, :, :], view)
            for norm in range(2 * len(subs)):
                s = subs[norm // 2]
                if norm % 2 == 0:
                    for c in range(1, NC):
                        pool.wait_ge(x_squared, NC * s.i + c + 1)
                        if c > 1:
                            pool.wait_ge(pre_summed, (NC - 1) * s.i + c - 1)
                        nc.gpsimd.tensor_tensor(sum_pre[:, :], sum_pre[:, :] if c > 1 else sq[:, 0, :], sq[:, c, :],
                                                ALU.add).then_inc(pre_summed, 1)
                if s.kind == "nsa" and norm % 2:
                    for b in range(s.cache_units):
                        t = stage_of["c", s.cache0 + b]
                        pool.wait_ge(loaded[t % RING], 32 * (t // RING + 1))
                        if b == 0:
                            pool.wait_ge(dec_q, s.attend + 1)
                        if b >= 2:
                            pool.wait_ge(cache_turned, pieces_to(s.cache0 + b - 2))
                        if b < DEC:
                            page = wstage[:, t % RING, :, :].rearrange("p (t g) (h c) -> p t (g h) c", t=2, c=256)
                            keys = page[:, :, :, 128:192]
                        else:
                            keys = wstage[:, t % RING, 0:2, :].rearrange("p t (g c) -> p t g c", g=GROUPS)[:, :, :, 0:HEAD]
                        nc.gpsimd.tensor_copy(k_pairs[:, b % 2, :, :, :], keys).then_inc(keys_paired, 1)
                if s.kind == "diff" and norm % 2:
                    pool.wait_ge(sub_var, 1)
                    nc.gpsimd.tensor_tensor(sub_r, sub_v, minus_half[:, 0:16], ALU.pow).then_inc(sub_rs, 1)
                    pool.wait_ge(sub_var, 2)
                    nc.gpsimd.tensor_tensor(s_nmx[0][0:64, :], s_mx[0][0:64, :], minus_half[0:64, 0:1], ALU.pow)\
                        .then_inc(sub_rs, 1)
                pool.wait_ge(var_ready, 2 * norm + 2)
                nc.gpsimd.tensor_tensor(rs[:, :], var[:, :], minus_half[:, 0:3], ALU.pow).then_inc(rs_ready, 1)
                pool.wait_ge(rs_ready, 3 * norm + 1)
                nc.gpsimd.tensor_copy(rs_hi[:, :], rs[:, :]).then_inc(rs_ready, 1)
                pool.wait_ge(rs_ready, 3 * norm + 2)
                nc.gpsimd.tensor_tensor(rs_lo[:, :], rs[:, :], rs_hi[:, :].bitcast(F32), ALU.subtract)\
                    .then_inc(rs_ready, 1)

        @block.scalar
        def _(act):
            split = [0]

            def split_to(upto):
                while split[0] < upto:
                    u = split[0]
                    t = stage_of["w", u]
                    act.wait_ge(loaded[t % RING], 32 * (t // RING + 1))
                    if u >= RING:
                        act.wait_ge(unit_used, u - RING + 1)
                    n, cols = unit_shape[u]
                    nc.scalar.activation(w_high_ring[:, u % RING, 0:n, 0:cols], wstage[:, t % RING, 0:n, 0:cols],
                                         ACT.Copy).then_inc(w_high, 1)
                    split[0] += 1

            def ffn_drain(gate, piece, chunk):
                act.wait_ge(gate_scaled, gate)
                nc.scalar.activation(tanh_t, gate_t, ACT.Tanh, scale=0.5).then_inc(tanh_done, 1)
                act.wait_ge(h_full, piece)
                nc.scalar.activation(h_hi[:, chunk, :], prod_t, ACT.Copy).then_inc(h_high, 1)

            def new_x(s):
                for c in range(NC):
                    act.wait_ge(x_updated, NC * s.i + c + 1)
                    nc.scalar.activation(x_hi[:, c, :], x[:, c, :], ACT.Copy, scale=pre_gain(s, c)).then_inc(x_high, 1)
                    nc.scalar.activation(sq[:, c, :], x[:, c, :], ACT.Square).then_inc(x_squared, 1)

            def attend(s):
                kind = s.kind
                tiles, b0, n0 = KV_TILES[kind], batch0[kind], task0[kind]
                if kind == "nsa":
                    act.wait_ge(gates_turned, 1)
                    g_ps = ps[:, 7, 0:3 * P].rearrange("p (t c) -> p t c", t=3)[:, :, P - 48:P]
                    nc.scalar.activation(gates[:, 0:2, :], g_ps[:, 0:2, :], ACT.Tanh, scale=0.5).then_inc(gates_tanh, 1)
                    nc.scalar.activation(gates[0:DEC, 2, :], g_ps[0:DEC, 2, :], ACT.Tanh, scale=0.5)\
                        .then_inc(gates_tanh, 1)
                act.wait_ge(conv_stored, 16 * stores["conv_stored"])
                for n, (tt, j) in enumerate(BATCHES[kind]):
                    rows_n = TOK[tt][1]
                    dst = kv_tok[:, tt, 512 * j:512 * j + 512] if tt < 2 else kv_sample[:, 512 * j:512 * j + 512]
                    act.wait_ge(tok_turned, b0 + n + 1)
                    nc.scalar.activation(dst, ps[0:rows_n, n % 6, :], ACT.Copy).then_inc(tok_copied, 1)
                act.wait_ge(tok_copied, b0 + len(BATCHES[kind]))
                if kind == "nsa":
                    act.wait_ge(gates_ready, 2)
                    store(act.dma_start(gate_scratch, gates[0:DEC, 2, :]), gates_out, "gates_out")
                width = 384 if kind == "nsa" else 256
                outs = (new_nsa_kv_prompt, new_nsa_kv_sample) if kind == "nsa" else (new_diff_kv_prompt, new_diff_kv_sample)
                for tt in range(2):
                    kv = kv_tok[:, tt, 0:4 * width].rearrange("p (g c) -> p g c", g=GROUPS)
                    store(act.dma_start(outs[0][0, 0, P * tt:P * tt + P], kv[:, :, 0:256]), tok_stored, "tok_stored")
                    if kind == "nsa":
                        store(act.dma_start(new_nsa_win_prompt[0, 0, P * tt:P * tt + P], kv[:, :, 256:384]), tok_stored, "tok_stored")
                kv = kv_sample[:, 0:4 * width].rearrange("p (g c) -> p g c", g=GROUPS)
                store(act.dma_start(outs[1][0].rearrange("b t g c -> (b t) g c"), kv[:, :, 0:256]), tok_stored, "tok_stored")
                if kind == "nsa":
                    store(act.dma_start(new_nsa_win_sample[0, :, SEQ - 1], kv[:, :, 256:384]), tok_stored, "tok_stored")
                    act.wait_ge(gates_out, 16)
                    act.dma_start(gate_rows, gate_scratch.rearrange("b (r k) -> (b r) k", k=3))\
                        .then_inc(gate_rows_loaded, 16)
                    act.wait_ge(cmp_shifted, 1)
                    nc.scalar.activation(cmp_e[:, :, :, :], cmp_s[:, :, :, :], ACT.Exp, scale=SCALE).then_inc(cmp_exp, 1)
                    act.wait_ge(cmp_pt_done, 1)
                    nc.scalar.activation(cmp_pt[:, :, :].rearrange("p a b -> p (a b)"), ps[:, 7, 0:2 * P],
                                         ACT.Copy).then_inc(cmp_pt_copied, 1)
                    act.wait_ge(cmp_out, 1)
                    nc.scalar.activation(o_tok[:, :, :].rearrange("p a b -> p (a b)"),
                                         ps[:, 0:4, :].rearrange("p a b -> p (a b)"), ACT.Copy).then_inc(cmp_added, 1)

                r0 = round0[kind]

                def keep_values(b):
                    n = s.cache0 + b
                    t = stage_of["c", n]
                    act.wait_ge(loaded[t % RING], 32 * (t // RING + 1))
                    page = wstage[:, t % RING, :, :].rearrange("p (t g) (h c) -> p t (g h) c", t=2, c=256)
                    if kind == "diff":
                        dst, src = homes["diff"][b // 4][:, b % 4, :, :, :], page[:, :, :, 128:256]
                    elif b < DEC:
                        dst, src = homes["sel"][:, b, :, :, :], page[:, :, :, 192:256]
                    else:
                        win = wstage[:, t % RING, 0:2, :].rearrange("p t (g c) -> p t g c", g=GROUPS)
                        dst, src = homes["win"][:, b - DEC, :, :, :], win[:, :, :, 64:128]
                    nc.scalar.activation(dst, src, ACT.Copy).then_inc(cache_kept, 1)

                def copy_scores(k):
                    act.wait_ge(cache_scored, pieces_to(s.cache0 + DEC * (k + 1) - 1))
                    nc.scalar.activation(st_dec[:, k, :, :].rearrange("p a b -> p (a b)"), ps[:, 7, 256:512], ACT.Copy)\
                        .then_inc(st_copied, 1)

                tasks = TASKS[kind]
                for n in range(len(tasks) + 1):
                    if kind == "nsa" and n == DEC:
                        copy_scores(0)
                    if n < len(tasks):
                        m, keys = n0 + n, P * (tasks[n][0] + 1)
                        act.wait_ge(at_max, m + 1)
                        if m >= 2:
                            act.wait_ge(at_turned, m - 1)
                        for i in range(4):
                            nc.scalar.activation(probs[:, m % 2, i, 0:keys],
                                                 ps[:, 2 * (m % 2) + i // 2, 256 * (i % 2):256 * (i % 2) + keys],
                                                 ACT.Exp, bias=nmx[:, m % 4, i:i + 1], scale=SCALE,
                                                 accum_out=esum[:, m % 4, i:i + 1]).then_inc(at_exp, 1)
                    if n >= 1:
                        m, tiles_n = n0 + n - 1, tasks[n - 1][0] + 1
                        act.wait_ge(at_turned, m + 1)
                        if m >= 2:
                            act.wait_ge(at_pv, m - 1)
                        nc.scalar.activation(probs_t[:, m % 2, :, 0:tiles_n, :],
                                             ps[:, 4:6, :].rearrange("p a (i t q) -> p (a i) t q", i=2, t=2)[:, :, 0:tiles_n, :],
                                             ACT.Copy).then_inc(at_copied, 1)
                    if n < len(tasks):
                        keep_values(n)
                rounds = ROUNDS[kind]
                copy_scores(len(rounds) // 2)
                if kind == "nsa":
                    act.wait_ge(cache_summed, DEC)
                    act.wait_ge(at_scaled, n0 + len(tasks))
                    nc.scalar.activation(kc_dec[:, :], ps[:, 6, 256:512], ACT.Copy).then_inc(kc_copied, 1)
                for k, name in enumerate(rounds):
                    bank, cols = round_bank(name), round_cols(name)
                    act.wait_ge(dec_max, r0 + k + 1)
                    nc.scalar.activation(p_dec[:, k, 0:cols], ps[:, bank, 0:cols], ACT.Exp, bias=s_nmx[k], scale=SCALE,
                                         accum_out=s_sum[k]).then_inc(dec_exp, 1)
                scale = 1.0 if kind == "nsa" else sub_gain
                act.wait_ge(tok_stored, 16 * stores["tok_stored"])
                stores["tok_stored" + kind] = stores["tok_stored"]
                act.wait_ge(z_turned, s.attend + 1)
                nc.scalar.activation(h_hi[:, 0:NC, 0:SEQ], ps[:, 0:4, :].rearrange("p a (b t) -> p (a b) t", b=2),
                                     ACT.Copy, scale=scale).then_inc(z_high, 1)
                act.wait_ge(dec_placed, s.attend + 1)
                nc.scalar.activation(h_hi[:, 0:NC, SEQ:T], z_dec[:, :, :], ACT.Copy, scale=scale).then_inc(z_high, 1)

            act.wait_ge(small_loaded, 192)
            split_to(2)
            act.wait_ge(lam_summed, 2)
            nc.scalar.activation(lam_e, lam_s, ACT.Exp).then_inc(lam_exp, 1)
            act.wait_ge(init_copied, 5)
            new_x(subs[0])
            for s in subs:
                if s.kind == "ffn":
                    gates0, pieces0 = s.ffn * (NF // 2), s.h_before
                    split_to(s.ins[0].end + 2)
                    ffn_drain(gates0 + 1, pieces0 + 1, slice(0, 2))
                    u0 = split[0]
                    with act.Fori(0, (NF // 2 - 1) // 2) as i:
                        for k in range(2):
                            for j in range(2):
                                u = u0 + 2 * k + j
                                t = stage_of["w", u]
                                act.wait_ge(loaded[t % RING], i * 32 + 32 * (t // RING + 1))
                                act.wait_ge(unit_used, i * 4 + (u - RING + 1))
                                nc.scalar.activation(w_high_ring[:, u % RING, :, :], wstage[:, t % RING, :, :],
                                                     ACT.Copy).then_inc(w_high, 1)
                            ffn_drain(i * 2 + (gates0 + 2 + k), i * 2 + (pieces0 + 2 + k), bass.ds(i * 4 + (2 + 2 * k), 2))
                    split[0] = u0 + 4 * ((NF // 2 - 1) // 2)
                else:
                    for g in s.ins:
                        split_to(g.end + 2)
                        if g.kind == "conv_b":
                            act.wait_ge(h_full, s.h_before + g.n - 3)
                            nc.scalar.activation(h_hi[:, 4 * (g.n - 4):4 * (g.n - 4) + 4, :], tmp4, ACT.Copy)\
                                .then_inc(h_high, 1)
                if s.cache_units:
                    attend(s)
                g = s.outs[0]
                split_to(g.end + 2)
                act.wait_ge(unit_used, g.end)
                nc.scalar.activation(y[:, 0:GT, :], gset(g), ACT.Copy).then_inc(y_copied, 1)
                nc.scalar.activation(sq[:, 0:GT, :], gset(g), ACT.Square).then_inc(y_squared, 1)
                g = s.outs[1]
                split_to(min(g.end + 2, n_units))
                for tile in range(GT):
                    if tile < GT - 1:
                        act.wait_ge(tile_done, (GT - 1) * s.i + tile + 1)
                    else:
                        act.wait_ge(unit_used, g.end)
                    nc.scalar.activation(sq[:, GT + tile, :], gset(g)[:, tile, :], ACT.Square).then_inc(y_squared, 1)
                    nc.scalar.activation(y[:, GT + tile, :], gset(g)[:, tile, :], ACT.Copy).then_inc(y_copied, 1)
                if s.kind == "conv":
                    act.wait_ge(conv_turned, s.conv + 1)
                    b = 4 * s.outs[0].set
                    nc.scalar.activation(conv_tok[:, :].rearrange("p (a n) -> p a n", a=2), ps[0:18, b:b + 2, :],
                                         ACT.Copy).then_inc(conv_copied, 1)
                    act.wait_ge(conv_copied, s.conv + 1)
                    store(act.dma_start(new_conv_prompt[s.conv, 0], conv_tok[0:2, :]), conv_stored, "conv_stored")
                    store(act.dma_start(new_conv_sample[s.conv].rearrange("b s n -> (b s) n"), conv_tok[2:18, :]),
                          conv_stored, "conv_stored")
                if s.i + 1 < len(subs):
                    new_x(subs[s.i + 1])
            for c in range(6):
                tt, half = c // 2, c % 2
                n = TOK[tt][1]
                act.wait_ge(y_turned, c + 1)
                nc.scalar.activation(y_tok[0:n, tt, 512 * half:512 * half + 512], ps[0:n, c, :], ACT.Copy)\
                    .then_inc(y_out, 1)
            act.wait_ge(y_out, 6)
            store(act.dma_start(y_prompt[0].rearrange("(t p) n -> p t n", p=P), y_tok[:, 0:2, :]), y_stored, "y_stored")
            store(act.dma_start(y_sample.rearrange("b t n -> (b t) n"), y_tok[0:DEC, 2, :]), y_stored, "y_stored")
        @block.vector
        def _(dve):
            V = nc.vector
            split = [0]

            def low_part(u, n, cols):
                V.tensor_tensor(w_low_ring[:, u % RING, 0:n, 0:cols],
                                wstage[:, stage_of["w", u] % RING, 0:n, 0:cols],
                                w_high_ring[:, u % RING, 0:n, 0:cols].bitcast(F32), ALU.subtract).then_inc(w_low, 1)

            def split_to(upto):
                while split[0] < upto:
                    u = split[0]
                    dve.wait_ge(w_high, u + 1)
                    low_part(u, *unit_shape[u])
                    split[0] += 1

            steps = {}

            def chain(ins, signal):
                steps[signal.name] = steps.get(signal.name, 0) + 1
                ins.then_inc(signal, 1)
                dve.wait_ge(signal, steps[signal.name])

            def ffn_drain(psum_set, end, before, gates, pieces, chunk):
                dve.wait_ge(unit_used, end)
                V.tensor_tensor(gate_t, ps[:, 4 * psum_set:4 * psum_set + 2, 0:T], b3(r_pre[:, :], 2), ALU.mult)\
                    .then_inc(gate_scaled, 1)
                V.scalar_tensor_tensor(out=up_t, in0=ps[:, 4 * psum_set + 2:4 * psum_set + 4, 0:T], scalar=0.5,
                                       in1=b3(r_pre[:, :], 2), op0=ALU.mult, op1=ALU.mult).then_inc(psum_drained, 1)
                dve.wait_ge(gate_scaled, gates + 1)
                dve.wait_ge(psum_drained, before + 1)
                V.tensor_tensor(up_t, gate_t, up_t, ALU.mult).then_inc(prod_ready, 1)
                dve.wait_ge(tanh_done, gates + 1)
                dve.wait_ge(prod_ready, gates + 1)
                V.scalar_tensor_tensor(out=prod_t, in0=tanh_t, scalar=1.0, in1=up_t, op0=ALU.add, op1=ALU.mult)\
                    .then_inc(h_full, 1)
                dve.wait_ge(h_high, pieces + 1)
                V.tensor_tensor(h_lo[:, chunk, :], prod_t, h_hi[:, chunk, :].bitcast(F32), ALU.subtract)\
                    .then_inc(h_low, 1)

            def norm_var(norm):
                dve.wait_ge(stats_done, norm + 1)
                b = norm_bank(norm)
                V.tensor_scalar(var[:, 0:2], ps[:, b, 0:2], EPS, None, ALU.add).then_inc(var_ready, 1)
                V.tensor_scalar(var[0:DEC, 2:3], ps[0:DEC, b, 2:3], EPS, None, ALU.add).then_inc(var_ready, 1)

            def norm_copy(s):
                dve.wait_ge(bcast_done, 2 * s.i + 1)
                V.tensor_copy(r_pre[:, :], ps[:, norm_bank(2 * s.i), 8:8 + T]).then_inc(rstd_ready, 1)
                dve.wait_ge(rstd_ready, s.i + 1)

            def low_x(s, c):
                dve.wait_ge(x_updated, NC * s.i + c + 1)
                dve.wait_ge(x_high, NC * s.i + c + 1)
                V.scalar_tensor_tensor(out=x_lo[:, c, :], in0=x[:, c, :], scalar=pre_gain(s, c),
                                       in1=x_hi[:, c, :].bitcast(F32), op0=ALU.mult, op1=ALU.subtract)\
                    .then_inc(x_low, 1)

            dve.wait_ge(small_loaded, 192)
            dve.wait_ge(consts_ready, 6)
            V.tensor_tensor(lam_p[:, :, :], lam_in[:, 0:4:2, :], lam_in[:, 1:4:2, :], ALU.mult).then_inc(lam_summed, 1)
            dve.wait_ge(lam_summed, 1)
            V.tensor_reduce(lam_s, lam_p[:, :, :], AX_X, ALU.add).then_inc(lam_summed, 1)
            V.tensor_reduce(even_row, even_tmp[:, :], AX_X, ALU.max).then_inc(dve_const, 1)
            steps["dve_const"] = 1
            dve.wait_ge(init_turned, 1)
            V.tensor_copy(gains[:, :], ps[:, 0, 0:gain_rows]).then_inc(init_copied, 1)
            V.tensor_copy(cmp_w[:, :], ps[:, 0, 256:288]).then_inc(init_copied, 1)
            V.tensor_copy(conv_state[:, :, :], ps[:, 1, 0:256].rearrange("p (c r) -> p c r", c=NC))\
                .then_inc(init_copied, 1)
            dve.wait_ge(init_copied, 3)
            halves = gains[:, 0:n_norm].rearrange("p (l j c) -> p l j c", l=DEPTH, j=6)
            V.tensor_scalar(halves[:, :, 1, :], halves[:, :, 1, :], 0.5, None, ALU.mult).then_inc(init_copied, 1)
            V.tensor_scalar(halves[:, :, 5, :], halves[:, :, 5, :], 0.5, None, ALU.mult).then_inc(init_copied, 1)
            dve.wait_ge(init_copied, 5)
            dve.wait_ge(lam_exp, 1)
            chain(V.tensor_tensor(lam, lam_e[:, 0:1], lam_e[:, 1:2], ALU.subtract), dve_const)
            chain(V.tensor_scalar(lam, lam, lam_init(2), None, ALU.add), dve_const)
            chain(V.tensor_scalar(dec_sign, lam, 1.0, None, ALU.add), dve_const)
            chain(V.tensor_tensor(dec_sign, dec_sign, even_row, ALU.mult), dve_const)
            chain(V.tensor_tensor(dec_sign, dec_sign, lam, ALU.subtract), dve_const)
            chain(V.tensor_scalar(sub_gain, gains[:, gain_rows - 1:gain_rows], 1.0 - lam_init(2), None, ALU.mult),
                  dve_const)
            for c in range(NC):
                dve.wait_ge(x_turned, c + 1)
                V.tensor_copy(x[:, c, :], ps[:, c, 0:T]).then_inc(x_updated, 1)
            split_to(2)
            for c in range(NC):
                dve.wait_ge(x_updated, NC)
                low_x(subs[0], c)

            def conv_tap(s, j, c):
                k = n_norm + (3 * s.conv + j) * NC + c
                return gains[:, k:k + 1]

            def conv_filter(s, c):
                for dst, taps in ((y[:, c, 0:SEQ], [u_prompt[:, c, j:j + SEQ] for j in range(3)]),
                                  (y[:, c, SEQ:T], [u_sample[:, c, j, :] for j in range(3)])):
                    chain(V.tensor_scalar(dst, taps[0], conv_tap(s, 0, c), None, ALU.mult), conv_step)
                    for j in (1, 2):
                        chain(V.scalar_tensor_tensor(out=dst, in0=taps[j], scalar=conv_tap(s, j, c), in1=dst,
                                                     op0=ALU.mult, op1=ALU.add), conv_step)

            def drain(s, g):
                dve.wait_ge(unit_used, g.end)
                if g.kind in ("q", "kv"):
                    dst = (q_t if g.kind == "q" else kv_t)
                    n = g.n if g.kind == "q" else g.n - 2
                    V.tensor_tensor(dst[:, 4 * n:4 * n + 4, :], gset(g), b3(r_pre[:, :], 4), ALU.mult)\
                        .then_inc(psum_drained, 1)
                elif g.kind == "gate":
                    V.tensor_tensor(gate_t1[:, :], gset(g)[:, 0, :], r_pre[:, :], ALU.mult).then_inc(psum_drained, 1)
                elif g.kind == "conv_cv":
                    if g.n == 0:
                        chain(V.memset(u_prompt[:, :, 0:2], 0.0), conv_step)
                        kept = conv_state[:, :, 16 * s.conv:16 * s.conv + 16].rearrange("p c (b s) -> p c s b", s=2)
                        for j in range(2):
                            chain(V.tensor_copy(u_sample[:, :, j, :], kept[:, :, j, :]), conv_step)
                    view = gset(g)
                    chain(V.tensor_tensor(gate_t, view[:, 0:2, :], b3(r_pre[:, :], 2), ALU.mult), conv_step)
                    V.tensor_tensor(up_t, view[:, 2:4, :], b3(r_pre[:, :], 2), ALU.mult).then_inc(psum_drained, 1)
                    dve.wait_ge(psum_drained, g.index + 1)
                    c = 2 * g.n
                    chain(V.tensor_tensor(u_prompt[:, c:c + 2, 2:SEQ + 2], gate_t[:, :, 0:SEQ], up_t[:, :, 0:SEQ],
                                          ALU.mult), conv_step)
                    chain(V.tensor_tensor(u_sample[:, c:c + 2, 2, :], gate_t[:, :, SEQ:T], up_t[:, :, SEQ:T],
                                          ALU.mult), conv_step)
                    conv_filter(s, c)
                    conv_filter(s, c + 1)
                    if g.n == 3:
                        if s.conv:
                            dve.wait_ge(conv_turned, s.conv)
                        chain(V.tensor_copy(conv_new[:, :, 0:2], u_prompt[:, :, SEQ:SEQ + 2]), conv_step)
                        V.tensor_copy(conv_new[:, :, 2:18].rearrange("p c (b s) -> p c s b", s=2),
                                      u_sample[:, :, 1:3, :]).then_inc(conv_gathered, 1)
                elif g.kind == "conv_b":
                    c = 4 * (g.n - 4)
                    if g.n > 4:
                        dve.wait_ge(h_low, s.h_before + g.n - 4)
                    V.tensor_tensor(tmp4, gset(g), b3(r_pre[:, :], 4), ALU.mult).then_inc(psum_drained, 1)
                    dve.wait_ge(psum_drained, g.index + 1)
                    V.tensor_tensor(tmp4, tmp4, y[:, c:c + 4, :], ALU.mult).then_inc(h_full, 1)
                    dve.wait_ge(h_high, s.h_before + g.n - 3)
                    V.tensor_tensor(h_lo[:, c:c + 4, :], tmp4, h_hi[:, c:c + 4, :].bitcast(F32), ALU.subtract)\
                        .then_inc(h_low, 1)

            def attend(s):
                kind = s.kind
                n0, tasks = task0[kind], TASKS[kind]

                def step(ins):
                    chain(ins, att_step)

                def decode_queries():
                    src = q_t[:, :, SEQ:T]
                    dst = q_dec[:, :].rearrange("p (b c k) -> p c b k", b=DEC, k=2)
                    if kind == "diff":
                        step(V.memset(q_dec[:, :], 0.0))
                        step(V.tensor_copy(dst[0:64, :, :, 0], src[0:64]))
                        V.tensor_copy(dst[64:128, :, :, 1], src[64:128]).then_inc(dec_q, 1)
                    else:
                        step(V.memset(q_pair[:, :], 0.0))
                        step(V.tensor_copy(dst[0:64, :, :, 0], src[0:64]))
                        step(V.tensor_copy(dst[0:64, :, :, 1], src[64:128]))
                        by_pair = lambda t: t.rearrange("p (j e h) -> p j e h", e=2, h=4)
                        step(V.tensor_copy(by_pair(q_pair[0:64, :])[:, :, 0, :], by_pair(q_dec[0:64, :])[:, :, 0, :]))
                        V.tensor_copy(by_pair(q_pair[64:128, :])[:, :, 1, :], by_pair(q_dec[0:64, :])[:, :, 1, :])\
                            .then_inc(dec_q, 1)

                dve.wait_ge(psum_drained, s.ins[-1].index + 1)
                if kind == "nsa":
                    groups_t = kv_t[:, :, :].rearrange("p (g k) t -> p g k t", k=3)
                    step(V.tensor_tensor(cmp_prod[:, :, :, :],
                                         groups_t[:, :, 0, 0:SEQ].rearrange("p g (n l) -> p g n l", l=CMP_BLOCK),
                                         cmp_w[:, :].unsqueeze(1).unsqueeze(1).broadcast_to(
                                             [P, GROUPS, N_CMP, CMP_BLOCK]), ALU.mult))
                    step(V.tensor_reduce(kc_t[:, :, :], cmp_prod[:, :, :, :], AX_X, ALU.add))
                    step(V.tensor_copy(kc_odd[64:128, :, :], kc_t[0:64, :, :]))
                    V.tensor_copy(vc_rep[64:128, :, :, :], kc_t[64:128, :, :].unsqueeze(2).broadcast_to(
                        [64, GROUPS, 4, N_CMP])).then_inc(cmp_keys, 1)
                    V.tensor_copy(k_odd[64:128, :, 0, :], groups_t[0:64, :, 1, 0:SEQ]).then_inc(keys_odd, 1)
                    V.tensor_copy(k_odd[64:128, :, 1, :], groups_t[0:64, :, 2, 0:SEQ]).then_inc(keys_odd, 1)
                    dve.wait_ge(gates_tanh, 2)
                    for t, n in ((slice(0, 2), P), (slice(2, 3), DEC)):
                        V.tensor_scalar(gates[0:n, t, :], gates[0:n, t, :], 0.5, 0.5, ALU.mult, ALU.add)\
                            .then_inc(gates_ready, 1)
                    dve.wait_ge(cmp_turned, 1)
                    V.tensor_tensor(vc_diag[:, :, :], ps[:, 6, 0:HEAD].unsqueeze(1).broadcast_to([P, 16, HEAD]),
                                    head_of_row[:, :].unsqueeze(2).broadcast_to([P, 16, HEAD]), ALU.mult)\
                        .then_inc(cmp_vals, 1)
                    dve.wait_ge(cmp_scores, 1)
                    for qt in range(2):
                        step(V.tensor_tensor(
                            cmp_s[:, qt, :, :].rearrange("p (a k) n -> p a k n", k=2),
                            ps[:, 4:6, 64 * qt:64 * qt + 64].rearrange("p k (a n) -> p a k n", n=N_CMP),
                            cmp_bias[:, qt, :].unsqueeze(1).unsqueeze(1).broadcast_to([P, 8, 2, N_CMP]), ALU.add))
                    step(V.tensor_reduce(cmp_m[:, :, :], cmp_s[:, :, :, :], AX_X, ALU.max))
                    m_all = cmp_m[:, :, :].unsqueeze(3).broadcast_to([P, 2, 16, N_CMP])
                    V.tensor_tensor(cmp_s[:, :, :, :], cmp_s[:, :, :, :], m_all, ALU.subtract)\
                        .then_inc(cmp_shifted, 1)
                    dve.wait_ge(cmp_exp, 1)
                    step(V.tensor_tensor(cmp_e[:, :, :, :], cmp_e[:, :, :, :],
                                         cmp_ok[:, :, :].unsqueeze(2).broadcast_to([P, 2, 16, N_CMP]), ALU.mult))
                    step(V.tensor_reduce(cmp_m[:, :, :], cmp_e[:, :, :, :], AX_X, ALU.add))
                    step(V.tensor_scalar(cmp_m[:, :, :], cmp_m[:, :, :], TINY, None, ALU.max))
                    step(V.reciprocal(cmp_m[:, :, :], cmp_m[:, :, :]))
                    dve.wait_ge(gates_ready, 2)
                    step(V.tensor_tensor(cmp_m[:, :, :], cmp_m[:, :, :],
                                         gates[:, 0:2, :].rearrange("p q (h k) -> p q h k", k=3)[:, :, :, 0], ALU.mult))
                    V.tensor_tensor(cmp_e[:, :, :, :], cmp_e[:, :, :, :], m_all, ALU.mult).then_inc(cmp_probs, 1)

                def task_max(n):
                    m, keys = n0 + n, P * (tasks[n][0] + 1)
                    dve.wait_ge(at_scores, m + 1)
                    b = 2 * (m % 2)
                    step(V.tensor_reduce(mx[:, m % 4, :].rearrange("p (a i) -> p a i", a=2),
                                         ps[:, b:b + 2, :].rearrange("p a (i k) -> p a i k", i=2)[:, :, :, 0:keys],
                                         AX_X, ALU.max))
                    V.tensor_scalar(nmx[:, m % 4, :], mx[:, m % 4, :], -SCALE, None, ALU.mult).then_inc(at_max, 1)

                def task_add(n):
                    m, (qt, br, g) = n0 + n, tasks[n]
                    dve.wait_ge(at_exp, 4 * (m + 1))
                    cf = coef[:, m % 4, :]
                    step(V.reciprocal(cf, esum[:, m % 4, :]))
                    if kind == "nsa":
                        k = 12 * g
                        step(V.tensor_tensor(cf.rearrange("p (k a) -> p k a", k=2), cf.rearrange("p (k a) -> p k a", k=2),
                                             gates[:, qt, k:k + 12].rearrange("p (a k t) -> p k a t", k=2, t=3)[:, :, :, br + 1],
                                             ALU.mult))
                    else:
                        step(V.tensor_scalar(cf[:, 2:4], cf[:, 2:4], lam, -1.0, ALU.mult, ALU.mult))
                    dve.wait_ge(at_pv, m + 1)
                    if kind == "nsa":
                        V.tensor_tensor(o_scaled[:, m % 2, 0:256].rearrange("p (a k d) -> p a k d", a=2, k=2),
                                        ps[:, 6, 0:256].rearrange("p (a k d) -> p a k d", a=2, k=2),
                                        cf.rearrange("p (k a) -> p a k", k=2).unsqueeze(3).broadcast_to([P, 2, 2, HEAD]),
                                        ALU.mult).then_inc(at_scaled, 1)
                        dve.wait_ge(at_scaled, m + 1)
                        if n == 0:
                            dve.wait_ge(cmp_added, 1)
                        o = o_tok[:, qt, 256 * g:256 * g + 256]
                        V.tensor_tensor(o, o, o_scaled[:, m % 2, 0:256], ALU.add).then_inc(at_added, 1)
                    else:
                        V.tensor_tensor(o_scaled[:, m % 2, :].rearrange("p (i d) -> p i d", i=4),
                                        ps[:, 6, :].rearrange("p (i d) -> p i d", i=4),
                                        cf.unsqueeze(2).broadcast_to([P, 4, P]), ALU.mult).then_inc(at_scaled, 1)
                        dve.wait_ge(at_scaled, m + 1)
                        V.tensor_tensor(o_tok[:, qt, 256 * g:256 * g + 256], o_scaled[:, m % 2, 0:256],
                                        o_scaled[:, m % 2, 256:512], ALU.add).then_inc(at_added, 1)

                decode_queries()
                p0, r0 = piece0[kind], round0[kind]

                def copy_piece(n, where):
                    piece = piece_at(kind, n, where)
                    if piece is None:
                        return
                    m = p0 + piece
                    dve.wait_ge(cache_turned, m + 1)
                    V.tensor_copy(kt_dec[:, m % 2, :, :].rearrange("p a k -> p (a k)"), ps[:, 7, 0:2 * P])\
                        .then_inc(cache_keys, 1)

                def compress(n):
                    t = stage_of["c", n]
                    dve.wait_ge(loaded[t % RING], 32 * (t // RING + 1))
                    if n:
                        dve.wait_ge(cache_summed, n)
                    page = wstage[:, t % RING, :, :].rearrange("p (t g) (h c) -> p (t g h) c", t=2, c=256)
                    V.tensor_tensor(prod_dec[:, :, :, :].rearrange("p t g c -> p (t g) c"), page[:, :, 0:P],
                                    cmp_w_tok[:, :].unsqueeze(1).broadcast_to([P, 8, P]), ALU.mult)\
                        .then_inc(cache_prod, 1)

                for n in range(len(tasks) + 2):
                    copy_piece(n, 0)
                    if n < len(tasks):
                        task_max(n)
                    copy_piece(n, 1)
                    copy_piece(n, 2)
                    if n >= 2:
                        task_add(n - 2)
                    copy_piece(n, 3)
                    if kind == "nsa" and n < DEC:
                        compress(s.cache0 + n)
                rounds = ROUNDS[kind]
                for k, name in enumerate(rounds):
                    dve.wait_ge(dec_scores, r0 + k + 1)
                    step(V.tensor_reduce(s_mx[k], ps[:, round_bank(name), 0:round_cols(name)], AX_X, ALU.max))
                    V.tensor_scalar(s_nmx[k], s_mx[k], -SCALE, None, ALU.mult).then_inc(dec_max, 1)
                for k, name in enumerate(rounds):
                    cols = round_cols(name)
                    factor = gate_rows[:, k:k + 1] if kind == "nsa" else dec_sign
                    if name == "cmp":
                        dve.wait_ge(gate_rows_loaded, 16)
                    dve.wait_ge(dec_exp, r0 + k + 1)
                    step(V.tensor_scalar(s_sum[k], s_sum[k], TINY, None, ALU.max))
                    step(V.reciprocal(s_coef[k], s_sum[k]))
                    step(V.tensor_tensor(s_coef[k], s_coef[k], factor, ALU.mult))
                    V.tensor_scalar(p_dec[:, k, 0:cols], p_dec[:, k, 0:cols], s_coef[k], None, ALU.mult)\
                        .then_inc(dec_probs, 1)
                    dve.wait_ge(dec_turned, r0 + k + 1)
                    if k == 2:
                        dve.wait_ge(dec_pv, r0 + k - 1)
                    V.tensor_copy(pt_dec[:, k % 2, :, :].rearrange("p a b -> p (a b)"), ps[:, 7, 0:2 * P])\
                        .then_inc(dec_copied, 1)
                    if name == "cmp":
                        V.tensor_copy(vc_dec[:, :, :].rearrange("p a b -> p (a b)"), ps[:, 4, 0:P])\
                            .then_inc(dec_copied, 1)
                    else:
                        V.tensor_copy(ptn_dec[:, k % 2, :, :].rearrange("p a b -> p (a b)"), ps[0:DEC, 4, :])\
                            .then_inc(dec_copied, 1)

                def z_low_part(k, src, t):
                    dve.wait_ge(z_high, 2 * s.attend + k + 1)
                    hi, lo = h_hi[:, 0:NC, t].bitcast(F32), h_lo[:, 0:NC, t]
                    if kind == "nsa":
                        V.tensor_tensor(lo, src, hi, ALU.subtract).then_inc(z_low, 1)
                    else:
                        V.scalar_tensor_tensor(out=lo, in0=src, scalar=sub_gain, in1=hi, op0=ALU.mult,
                                               op1=ALU.subtract).then_inc(z_low, 1)

                def prompt_low():
                    dve.wait_ge(tok_stored, 16 * stores["tok_stored" + kind])
                    z_low_part(0, ps[:, 0:4, :].rearrange("p a (b t) -> p (a b) t", b=2), slice(0, SEQ))

                dve.wait_ge(at_added, n0 + len(tasks))
                if kind == "nsa":
                    prompt_low()
                    dve.wait_ge(dec_pv, r0 + 3)
                    pairs = ps[0:64, 5, 0:P].rearrange("p (b c k) -> p c b k", b=DEC, k=2)
                    step(V.tensor_copy(z_dec[0:64, :, :], pairs[:, :, :, 0]))
                    V.tensor_copy(z_dec[64:128, :, :], pairs[:, :, :, 1]).then_inc(dec_placed, 1)
                else:
                    heads = lambda t: t.rearrange("p q (h d) -> p (q h) d", d=P)
                    step(V.tensor_tensor(o_square[:, :, :], o_tok[:, :, :], o_tok[:, :, :], ALU.mult))
                    step(V.tensor_reduce(sub_v, heads(o_square[:, :, :]), AX_X, ALU.add))
                    V.tensor_scalar(sub_v, sub_v, 1.0 / P, EPS, ALU.mult, ALU.add).then_inc(sub_var, 1)
                    dve.wait_ge(sub_rs, 1)
                    V.tensor_tensor(heads(o_tok[:, :, :]), heads(o_tok[:, :, :]),
                                    sub_r.unsqueeze(2).broadcast_to([P, 16, P]), ALU.mult).then_inc(o_normed, 1)
                    dve.wait_ge(dec_pv, r0 + 1)
                    V.tensor_copy(o_dec[:, :], ps[:, 5, 0:P]).then_inc(dec_added, 1)
                    dve.wait_ge(dec_added, 1)
                    pairs = o_dec[:, :].rearrange("p (b c k) -> p c b k", b=DEC, k=2)
                    step(V.tensor_tensor(z_dec[:, :, :], pairs[:, :, :, 0], pairs[:, :, :, 1], ALU.add))
                    z_rows = z_dec[:, :, :].rearrange("p c b -> p (c b)")
                    V.tensor_tensor(o_dec[:, 0:64], z_rows, z_rows, ALU.mult).then_inc(sub_squared, 1)
                    dve.wait_ge(sub_stats, 1)
                    V.tensor_scalar(s_mx[0][0:64, :], ps[0:64, 6, 0:1], EPS, None, ALU.add).then_inc(sub_var, 1)
                    prompt_low()
                    dve.wait_ge(sub_bcast, 1)
                    V.tensor_tensor(z_rows, ps[:, 6, 64:128], z_rows, ALU.mult).then_inc(dec_placed, 1)
                dve.wait_ge(dec_placed, s.attend + 1)
                z_low_part(1, z_dec[:, :, :], slice(SEQ, T))

            for s in subs:
                pre, post = 2 * s.i, 2 * s.i + 1
                split_to(s.ins[0].end + 1)
                norm_var(pre)
                split_to(s.ins[0].end + 2)
                norm_copy(s)
                if s.kind == "ffn":
                    gates0, pieces0, g1 = s.ffn * (NF // 2), s.h_before, s.ins[1]
                    ffn_drain(s.ins[0].set, s.ins[0].end, s.ins[0].index, gates0, pieces0, slice(0, 2))
                    u0 = split[0]
                    with dve.Fori(0, (NF // 2 - 1) // 2) as i:
                        for k in range(2):
                            for j in range(2):
                                u = u0 + 2 * k + j
                                dve.wait_ge(w_high, i * 4 + (u + 1))
                                low_part(u, HC, GC)
                            ffn_drain(s.ins[1 + k].set, i * 4 + s.ins[1 + k].end, i * 2 + (g1.index + k), i * 2 + (gates0 + 1 + k),
                                      i * 2 + (pieces0 + 1 + k), bass.ds(i * 4 + (2 + 2 * k), 2))
                    split[0] = u0 + 4 * ((NF // 2 - 1) // 2)
                else:
                    drain(s, s.ins[0])
                    for g in s.ins[1:]:
                        split_to(g.end + 2)
                        drain(s, g)
                if s.cache_units:
                    attend(s)
                split_to(s.outs[0].end + 2)
                dve.wait_ge(y_squared, (GT + 1) * s.i + 1)
                V.tensor_reduce(sum_post[:, :], sq[:, 0:GT, :].rearrange("p c t -> p t c"),
                                AX_X, ALU.add).then_inc(psum_drained, 1)
                dve.wait_ge(psum_drained, s.outs[0].index + 1)
                split_to(min(s.outs[1].end + 2, n_units))
                for tile in range(GT):
                    dve.wait_ge(y_squared, (GT + 1) * s.i + tile + 2)
                    if tile:
                        dve.wait_ge(post_added, (GT - 1) * s.i + tile)
                    V.tensor_tensor(sum_post[:, :], sum_post[:, :], sq[:, GT + tile, :], ALU.add)\
                        .then_inc(post_added if tile < GT - 1 else psum_drained, 1)
                norm_var(post)
                dve.wait_ge(y_copied, (GT + 1) * (s.i + 1))
                dve.wait_ge(bcast_done, post + 1)
                r_post = ps[:, norm_bank(post), 8:8 + T]
                def scale_y(c):
                    V.scalar_tensor_tensor(out=y[:, c, :], in0=y[:, c, :], scalar=post_gain(s, c),
                                           in1=r_post, op0=ALU.mult, op1=ALU.mult).then_inc(y_scaled, 1)

                scale_y(0)
                for c in range(NC):
                    dve.wait_ge(y_scaled, NC * s.i + c + 1)
                    V.tensor_tensor(x[:, c, :], x[:, c, :], y[:, c, :], ALU.add).then_inc(x_updated, 1)
                    if c + 1 < NC:
                        scale_y(c + 1)
                    if c and s.i + 1 < len(subs):
                        low_x(subs[s.i + 1], c - 1)
                if s.i + 1 < len(subs):
                    dve.wait_ge(x_updated, NC * (s.i + 2))
                    low_x(subs[s.i + 1], NC - 1)

        @block.tensor
        def _(pe):
            MM = nc.tensor.matmul
            TR = nc.tensor.transpose

            def products(psum_bank, u, k, tile, hi, lo, first, last):
                wh = w_high_ring[:, u % RING, k, tile * P:tile * P + P]
                wl = w_low_ring[:, u % RING, k, tile * P:tile * P + P]
                out = ps[:, psum_bank, 0:T]
                MM(out, wh, hi, start=first, stop=False)
                MM(out, wh, lo, start=False, stop=False)
                return MM(out, wl, hi, start=False, stop=last)

            def norm_stats(norm, squares):
                b = norm_bank(norm)
                for tt, (t0, n) in enumerate(TOK):
                    mm = MM(ps[0:n, b, tt:tt + 1], squares[:, t0:t0 + n], mean_col[:, 0:1], start=(tt == 0),
                            stop=True, skip_group_check=True)
                mm.then_inc(stats_done, 1)

            def norm_bcast(norm):
                pe.wait_ge(rs_ready, 3 * (norm + 1))
                b = norm_bank(norm)
                for tt, (t0, n) in enumerate(TOK):
                    out = ps[:, b, 8 + t0:8 + t0 + n]
                    MM(out, rs_hi[0:n, tt:tt + 1].broadcast_to([n, P]), ident_r[0:n, 0:n], start=(tt == 0), stop=False,
                       skip_group_check=True)
                    mm = MM(out, rs_lo[0:n, tt:tt + 1].broadcast_to([n, P]), ident_r[0:n, 0:n], start=False, stop=True,
                            skip_group_check=True)
                mm.then_inc(bcast_done, 1)

            def group_units(s, g):
                first_of_sub, second = g is s.ins[0], g is s.ins[1]
                if g.index >= 2:
                    pe.wait_ge(psum_drained, g.index - 1)
                for k, u in enumerate(range(g.unit0, g.end)):
                    pe.wait_ge(w_low, u + 1)
                    if second and k == 0:
                        for tile in range(GT):
                            if tile == 1:
                                norm_bcast(2 * s.i)
                            if tile == GT - 1:
                                pe.wait_ge(rstd_ready, s.i + 1)
                            for c in range(HC):
                                mm = products(4 * g.set + tile, u, c, tile, x_hi[:, c, :], x_lo[:, c, :], c == 0, False)
                    else:
                        for j in range(HC):
                            c = HC * k + j
                            if first_of_sub:
                                w = lambda ring, tile: ring[:, u % RING, j, tile * P:tile * P + P]
                                out = lambda tile: ps[:, 4 * g.set + tile, 0:T]
                                pe.wait_ge(x_high, NC * s.i + c + 1)
                                for tile in range(g.tiles):
                                    MM(out(tile), w(w_high_ring, tile), x_hi[:, c, :], start=(c == 0), stop=False)
                                    MM(out(tile), w(w_low_ring, tile), x_hi[:, c, :], start=False, stop=False)
                                pe.wait_ge(x_low, NC * s.i + c + 1)
                                for tile in range(g.tiles):
                                    mm = MM(out(tile), w(w_high_ring, tile), x_lo[:, c, :], start=False,
                                            stop=(c == NC - 1))
                                continue
                            for tile in range(g.tiles):
                                mm = products(4 * g.set + tile, u, j, tile, x_hi[:, c, :], x_lo[:, c, :],
                                              c == 0, c == NC - 1)
                    mm.then_inc(unit_used, 1)

            pe.wait_ge(small_loaded, 192)
            pe.wait_ge(consts_ready, 6)
            TR(ps[:, 0, 0:P], gain_a[:, :], ident[:, :])
            TR(ps[:, 0, P:P + cols_b], gain_b[:, :], ident[0:cols_b, 0:cols_b])
            TR(ps[:, 0, 256:288], cmp_tok[:, :], ident[0:32, 0:32])
            for c in range(NC):
                mm = TR(ps[:, 1, 32 * c:32 * c + 32], state_tok[:, c * P:c * P + P], ident[0:32, 0:32])
            mm.then_inc(init_turned, 1)
            pe.wait_ge(xs_loaded, 32)
            pe.wait_ge(init_copied, 3)
            for c in range(NC):
                for tt, (t0, n) in enumerate(TOK):
                    mm = TR(ps[:, c, t0:t0 + n], tok_in[0:n, tt, c * P:c * P + P], ident[0:n, 0:n])
                mm.then_inc(x_turned, 1)
            pe.wait_ge(x_updated, NC)

            def attend(s):
                kind = s.kind
                n0, b0, tasks = task0[kind], batch0[kind], TASKS[kind]
                pe.wait_ge(psum_drained, s.ins[-1].index + 1)
                if kind == "nsa":
                    for tt, (t0, n) in enumerate(TOK):
                        mm = TR(ps[0:n, 7, P * tt:P * tt + P], gate_t1[:, t0:t0 + n], ident[:, :])
                    mm.then_inc(gates_turned, 1)
                for n, (tt, j) in enumerate(BATCHES[kind]):
                    t0, rows_n = TOK[tt]
                    if n >= 6:
                        pe.wait_ge(tok_copied, b0 + n - 5)
                    for i in range(4):
                        mm = TR(ps[0:rows_n, n % 6, P * i:P * i + P], kv_t[:, 4 * j + i, t0:t0 + rows_n], ident[:, :])
                    mm.then_inc(tok_turned, 1)
                pe.wait_ge(tok_copied, b0 + len(BATCHES[kind]))
                if kind == "nsa":
                    pe.wait_ge(cmp_keys, 1)
                    TR(ps[:, 6, 0:HEAD], vc_rep[64:128, :, :, :].rearrange("p g h n -> p (g h n)"),
                       ident[64:128, 64:128]).then_inc(cmp_turned, 1)
                    for qt in range(2):
                        for h in range(16):
                            g, odd = h // 4, h % 2
                            keys = kc_odd[64:128, g, :] if odd else kc_t[0:64, g, :]
                            col = 64 * qt + N_CMP * (h // 2)
                            mm = MM(ps[:, 4 + odd, col:col + N_CMP],
                                    q_t[64 * odd:64 * odd + 64, h // 2, P * qt:P * qt + P], keys,
                                    start=(qt == 0 and h < 2), stop=True, skip_group_check=True)
                    mm.then_inc(cmp_scores, 1)
                    pe.wait_ge(cmp_probs, 1)
                    pe.wait_ge(gates_tanh, 2)
                    for qt in range(2):
                        mm = TR(ps[:, 7, P * qt:P * qt + P], cmp_e[:, qt, :, :].rearrange("p h n -> p (h n)"), ident[:, :])
                    mm.then_inc(cmp_pt_done, 1)
                    pe.wait_ge(cmp_pt_copied, 1)
                    pe.wait_ge(cmp_vals, 1)
                    for qt in range(2):
                        for half in range(2):
                            mm = MM(ps[:, 2 * qt + half, :], cmp_pt[:, qt, :],
                                    vc_diag[:, 8 * half:8 * half + 8, :].rearrange("p h d -> p (h d)"),
                                    start=True, stop=True)
                    mm.then_inc(cmp_out, 1)
                    pe.wait_ge(cmp_added, 1)
                    pe.wait_ge(keys_odd, 2)

                def task_scores(n):
                    m, (qt, br, g) = n0 + n, tasks[n]
                    if n >= 2:
                        pe.wait_ge(at_exp, 4 * (m - 1))
                    keys = P * (qt + 1)
                    for i in range(4):
                        odd, a = i // 2, i % 2
                        if kind == "nsa":
                            k = k_odd[64:128, g, br, 0:keys] if odd else kv_t[0:64, 3 * g + 1 + br, 0:keys]
                        else:
                            k = kv_t[64 * odd:64 * odd + 64, 2 * g, 0:keys]
                        bank, col = 2 * (m % 2) + odd, 256 * a
                        MM(ps[:, bank, col:col + keys], q_t[64 * odd:64 * odd + 64, 2 * g + a, P * qt:P * qt + P], k,
                           start=(a == 0), stop=False, skip_group_check=True)
                    for i in range(4):
                        bank, col = 2 * (m % 2) + i // 2, 256 * (i % 2) + P * qt
                        mm = MM(ps[:, bank, col:col + P], ident_b[:, :], causal[:, :], start=False, stop=True,
                                skip_group_check=True)
                    mm.then_inc(at_scores, 1)

                def task_turn(n):
                    m, (qt, br, g) = n0 + n, tasks[n]
                    pe.wait_ge(at_exp, 4 * (m + 1))
                    if n >= 1:
                        pe.wait_ge(at_copied, m)
                    for i in range(4):
                        for kt in range(qt + 1):
                            col = 256 * (i % 2) + P * kt
                            mm = TR(ps[:, 4 + i // 2, col:col + P], probs[:, m % 2, i, P * kt:P * kt + P], ident[:, :])
                    mm.then_inc(at_turned, 1)

                def task_values(n):
                    m, (qt, br, g) = n0 + n, tasks[n]
                    v0, vstep, d = value_tile(kind, br)
                    pe.wait_ge(at_copied, m + 1)
                    if n >= 1:
                        pe.wait_ge(at_scaled, m)
                    first = True
                    for i in range(4):
                        slot = 2 * (i % 2) + i // 2 if kind == "nsa" else i
                        for kt in range(qt + 1):
                            mm = MM(ps[:, 6, d * slot:d * slot + d], probs_t[:, m % 2, i, kt, :],
                                    kv_tok[:, kt, v0 + vstep * g:v0 + vstep * g + d], start=first, stop=(kt == qt),
                                    skip_group_check=True)
                            first = False
                    mm.then_inc(at_pv, 1)

                p0, kd = piece0[kind], (64 if kind == "nsa" else P)

                def piece_tiles(piece):
                    u, q = piece // PIECES[kind], piece % PIECES[kind]
                    tiles = [(q, 0), (q, 1)] if kind == "nsa" else [(q // 2, 2 * (q % 2)), (q // 2, 2 * (q % 2) + 1)]
                    return u, stage_of["c", s.cache0 + u], tiles

                def turn_piece(piece):
                    u, t, tiles = piece_tiles(piece)
                    if kind == "nsa":
                        pe.wait_ge(keys_paired, u + 1)
                    else:
                        pe.wait_ge(loaded[t % RING], 32 * (t // RING + 1))
                    for i, (kt, e) in enumerate(tiles):
                        if kind == "nsa":
                            keys = k_pairs[:, u % 2, kt, 2 * e:2 * e + 2, :].rearrange("p g d -> p (g d)")
                        else:
                            page = wstage[:, t % RING, 2 * kt:2 * kt + 2, :].rearrange("p a (g c) -> p (a g) c", g=2)
                            keys = page[:, e, 0:P]
                        mm = TR(ps[:, 7, P * i:P * i + P], keys, ident[:, :])
                    mm.then_inc(cache_turned, 1)

                def score_piece(piece):
                    u, t, tiles = piece_tiles(piece)
                    pe.wait_ge(cache_keys, p0 + piece + 1)
                    queries, n = (q_pair, 8) if kind == "nsa" else (q_dec, 4)
                    for i, (kt, e) in enumerate(tiles):
                        col = 16 * (u % DEC) + n * e
                        mm = MM(ps[:, 7, 256 + P * kt + col:256 + P * kt + col + n], kt_dec[:, (p0 + piece) % 2, i, :],
                                queries[:, col:col + n], start=True, stop=True, skip_group_check=True)
                    mm.then_inc(cache_scored, 1)

                def piece_step(n, where):
                    piece = piece_at(kind, n, where)
                    if piece is None:
                        return
                    if piece:
                        score_piece(piece - 1)
                    else:
                        pe.wait_ge(dec_q, s.attend + 1)
                    if kind == "nsa" and piece == PIECES[kind] * DEC:
                        pe.wait_ge(st_copied, 1)
                    turn_piece(piece)

                def sum_blocks(b):
                    pe.wait_ge(cache_prod, b + 1)
                    for i in range(8):
                        kt, g = i // 4, i % 4
                        col = 256 + 32 * b + 8 * g + 4 * kt
                        mm = MM(ps[:, 6, col:col + 4], prod_dec[:, kt, g, :], block_of_row[:, :],
                                start=True, stop=True, skip_group_check=True)
                    mm.then_inc(cache_summed, 1)

                for n in range(len(tasks) + 2):
                    piece_step(n, 0)
                    if n < len(tasks):
                        task_scores(n)
                    piece_step(n, 1)
                    if 1 <= n <= len(tasks):
                        task_turn(n - 1)
                    piece_step(n, 2)
                    if kind == "nsa" and 1 <= n <= DEC:
                        if n >= 3:
                            pe.wait_ge(at_scaled, n0 + n - 2)
                        sum_blocks(n - 1)
                    if n >= 2:
                        task_values(n - 2)
                    piece_step(n, 3)
                    if n == len(tasks):
                        score_piece(PIECES[kind] * n - 1)
                pe.wait_ge(at_scaled, n0 + len(tasks))

                r0, rounds = round0[kind], ROUNDS[kind]

                def page_scores(k, bank, new_tile):
                    pe.wait_ge(st_copied, 2 * s.attend + k + 1)
                    for kt in range(2):
                        TR(ps[:, bank, P * kt:P * kt + P], st_dec[:, k, kt, :], ident[:, :])
                    for g in range(GROUPS):
                        MM(ps[:, bank, 256 + DEC * g:256 + DEC * g + DEC], q_dec[0:kd, :], kv_t[0:kd, new_tile(g), SEQ:T],
                           start=False, stop=False, skip_group_check=True)
                    MM(ps[:, bank, 256:288], ident_b[:, :], own_new[:, :, :].rearrange("p g b -> p (g b)"),
                       start=False, stop=True, skip_group_check=True).then_inc(dec_scores, 1)

                def turn_probs(k):
                    pe.wait_ge(dec_probs, r0 + k + 1)
                    if k:
                        pe.wait_ge(dec_copied, 2 * (r0 + k))
                    for kt in range(2):
                        mm = TR(ps[:, 7, P * kt:P * kt + P], p_dec[:, k, P * kt:P * kt + P], ident[:, :])
                    if rounds[k] == "cmp":
                        for kt in range(2):
                            mm = TR(ps[:, 4, HEAD * kt:HEAD * kt + HEAD], kc_dec[64:128, P * kt:P * kt + P],
                                    ident[64:128, 64:128])
                    else:
                        for g in range(GROUPS):
                            mm = TR(ps[0:DEC, 4, P * g:P * g + P], p_dec[:, k, 256 + DEC * g:256 + DEC * g + DEC], ident[:, :])
                    mm.then_inc(dec_turned, 1)

                def round_values(k, br, values):
                    v0, vstep, d = value_tile(kind, br)
                    pe.wait_ge(dec_copied, 2 * (r0 + k + 1))
                    for g in range(GROUPS):
                        MM(ps[0:d, 5, 0:P], kv_sample[:, v0 + vstep * g:v0 + vstep * g + d], ptn_dec[:, k % 2, g, :],
                           start=(g == 0 and k == 0), stop=False, skip_group_check=True)
                    for b in range(DEC):
                        for kt in range(2):
                            for g in range(GROUPS):
                                c = 16 * b + 4 * g
                                mm = MM(ps[0:d, 5, c:c + 4], values(b, kt, g), pt_dec[:, k % 2, kt, c:c + 4],
                                        start=False, stop=True, skip_group_check=True)
                    mm.then_inc(dec_pv, 1)

                def turn_prompt():
                    for qt in range(2):
                        for c in range(NC):
                            col = 256 * (c % 2) + P * qt
                            mm = TR(ps[:, c // 2, col:col + P], o_tok[:, qt, P * c:P * c + P], ident[:, :])
                    mm.then_inc(z_turned, 1)

                if kind == "nsa":
                    pe.wait_ge(kc_copied, 1)
                    MM(ps[:, 4, 0:256], q_dec[0:64, :], kc_dec[0:64, :], start=True, stop=False, skip_group_check=True)
                    MM(ps[:, 4, 0:256], ident_b[:, :], own_cmp[:, :, :].rearrange("p j n -> p (j n)"),
                       start=False, stop=True, skip_group_check=True).then_inc(dec_scores, 1)
                    page_scores(0, 5, lambda g: 3 * g + 1)
                    page_scores(1, 6, lambda g: 3 * g + 2)
                    pe.wait_ge(at_added, n0 + len(tasks))
                    turn_prompt()
                    turn_probs(0)
                    turn_probs(1)
                    pe.wait_ge(dec_exp, r0 + 2)
                    for kt in range(2):
                        mm = MM(ps[0:HEAD, 5, 0:P], vc_dec[:, kt, :], pt_dec[:, 0, kt, :], start=(kt == 0), stop=False,
                                skip_group_check=True)
                    mm.then_inc(dec_pv, 1)
                    turn_probs(2)
                    round_values(1, 0, lambda b, kt, g: homes["sel"][:, b, kt, g, :])
                    round_values(2, 1, lambda b, kt, g: homes["win"][:, b, kt, g, :])
                else:
                    page_scores(0, 5, lambda g: 2 * g)
                    turn_probs(0)
                    round_values(0, 0, lambda b, kt, g: homes["diff"][b // 4][:, b % 4, kt, g, :])
                    pe.wait_ge(o_normed, 1)
                    turn_prompt()
                    pe.wait_ge(sub_squared, 1)
                    MM(ps[0:64, 6, 0:1], o_dec[:, 0:64], mean_col[:, 1:2], start=True, stop=True).then_inc(sub_stats, 1)
                    pe.wait_ge(sub_rs, 2)
                    MM(ps[:, 6, 64:128], s_nmx[0][0:64, :].broadcast_to([64, P]), ident[0:64, 0:64], start=True, stop=True)\
                        .then_inc(sub_bcast, 1)

            for s in subs:
                g0, g1 = s.ins[0], s.ins[1]
                group_units(s, g0)
                pe.wait_ge(pre_summed, (NC - 1) * (s.i + 1))
                pe.wait_ge(psum_drained, g0.index)
                norm_stats(2 * s.i, sum_pre)
                group_units(s, g1)
                if s.kind == "ffn":
                    with pe.Fori(0, (NF // 2 - 3) // 2) as i:
                        for k in range(2):
                            g = s.ins[2 + k]
                            pe.wait_ge(psum_drained, i * 2 + (g.index - 1))
                            for j in range(2):
                                u = g.unit0 + j
                                pe.wait_ge(w_low, i * 4 + (u + 1))
                                for cc in range(HC):
                                    c = HC * j + cc
                                    for tile in range(GT):
                                        mm = products(4 * g.set + tile, u, cc, tile, x_hi[:, c, :], x_lo[:, c, :],
                                                      c == 0, c == NC - 1)
                                mm.then_inc(unit_used, 1)
                    group_units(s, s.ins[-1])
                else:
                    for g in s.ins[2:]:
                        group_units(s, g)
                if s.cache_units:
                    attend(s)
                for g in s.outs:
                    pe.wait_ge(psum_drained, g.index - 1)
                    if s.cache_units:
                        pe.wait_ge(z_low, 2 * (s.attend + 1))
                    chunk0, n_chunks = 0, sum(g.units)
                    for k, u in enumerate(range(g.unit0, g.end)):
                        pe.wait_ge(w_low, u + 1)
                        if g.n == 1 and u == g.end - 1:
                            for tile in range(GT):
                                for j in range(g.units[k]):
                                    c = chunk0 + j
                                    mm = products(4 * g.set + tile, u, j, tile, h_hi[:, c, :], h_lo[:, c, :],
                                                  c == 0, c == n_chunks - 1)
                                mm.then_inc(tile_done if tile < GT - 1 else unit_used, 1)
                            break
                        for j in range(g.units[k]):
                            c = chunk0 + j
                            if not s.cache_units and g.n == 0 and c % s.h_piece == 0:
                                pe.wait_ge(h_low, s.h_before + c // s.h_piece + 1)
                            for tile in range(GT):
                                mm = products(4 * g.set + tile, u, j, tile, h_hi[:, c, :], h_lo[:, c, :],
                                              c == 0, c == n_chunks - 1)
                        mm.then_inc(unit_used, 1)
                        chunk0 += g.units[k]
                pe.wait_ge(psum_drained, s.outs[1].index + 1)
                pe.wait_ge(y_copied, (GT + 1) * s.i + 2)
                norm_stats(2 * s.i + 1, sum_post)
                norm_bcast(2 * s.i + 1)
                if s.kind == "conv":
                    pe.wait_ge(conv_gathered, s.conv + 1)
                    b = 4 * s.outs[0].set
                    pe.wait_ge(psum_drained, s.outs[0].index + 1)
                    for c in range(NC):
                        mm = TR(ps[0:18, b + c // 4, P * (c % 4):P * (c % 4) + P], conv_new[:, c, :], ident[:, :])
                    mm.then_inc(conv_turned, 1)
                    pe.wait_ge(conv_copied, s.conv + 1)
            pe.wait_ge(x_updated, NC * (len(subs) + 1))
            for c in range(6):
                tt, half = c // 2, c % 2
                t0, n = TOK[tt]
                for j in range(4):
                    mm = TR(ps[0:n, c, P * j:P * j + P], x[:, 4 * half + j, t0:t0 + n], ident[:, :])
                mm.then_inc(y_turned, 1)

        @block.sync
        def _(sp):
            sp.dma_start(pages[:, :], page_table.rearrange("(a b) n -> a (b n)", a=1)).then_inc(small_loaded, 16)
            g2 = norm_g.rearrange("l j (c p) -> (l j c) p", p=P)
            sp.dma_start(gain_a[:, :], g2[0:P, :]).then_inc(small_loaded, 16)
            sp.dma_start(gain_b[0:n_norm - P, :], g2[P:n_norm, :]).then_inc(small_loaded, 16)
            sp.dma_start(gain_b[n_norm - P:cols_b - 1, :], conv_w.rearrange("v j (c p) -> (v j c) p", p=P))\
                .then_inc(small_loaded, 16)
            sp.dma_start(gain_b[cols_b - 1:cols_b, :], diff_subln_g).then_inc(small_loaded, 16)
            sp.dma_start(state_tok[:, :], state_conv.rearrange("v b s n -> (v b s) n")).then_inc(small_loaded, 16)
            sp.dma_start(cmp_tok[:, :].rearrange("l (k d) -> l k d", k=2), nsa_w_cmp[0].rearrange("k l d -> l k d"))\
                .then_inc(small_loaded, 16)
            for n in range(4):
                sp.dma_start(cmp_w_tok[32 * n:32 * n + 32, :].rearrange("l (k d) -> l k d", k=2),
                             nsa_w_cmp[0].rearrange("k l d -> l k d")).then_inc(small_loaded, 16)
            sp.dma_start(lam_in[:, :, :].rearrange("p a d -> p (a d)"),
                         diff_lambda.rearrange("a b d -> a (b d)").broadcast_to([P, 4 * HEAD])).then_inc(small_loaded, 16)
            sp.dma_start(tok_in[:, 0:2, :], x_prompt[0].rearrange("(t p) n -> p t n", p=P)).then_inc(xs_loaded, 16)
            sp.dma_start(tok_in[0:DEC, 2, :], x_sample.rearrange("b t n -> (b t) n")).then_inc(xs_loaded, 16)

            def slot_free(t):
                if t < RING:
                    return
                kind, n = stage_order[t - RING]
                if kind == "w":
                    sp.wait_ge(w_low, n + 1)
                else:
                    if n < 2 * DEC:
                        sp.wait_ge(keys_paired, n + 1)
                    else:
                        sp.wait_ge(cache_turned, pieces_to(n))
                    sp.wait_ge(cache_kept, n + 1)
                    if n < DEC:
                        sp.wait_ge(cache_prod, n + 1)

            def load(t, *parts):
                for dst, src in parts:
                    sp.dma_start(dst, src).then_inc(loaded[t % RING], 16)

            def chunks(t, w, k0, n, c0, cols=GC):
                h, v = n // 2, rows(w)
                load(t, (wstage[:, t % RING, 0:h, 0:cols], v[:, k0:k0 + h, c0:c0 + cols]),
                     (wstage[:, t % RING, h:n, 0:cols], v[:, k0 + h:k0 + n, c0:c0 + cols]))

            def pair(t, w, k0, c0, c1):
                v = rows(w)
                load(t, (wstage[:, t % RING, :, 0:256], v[:, k0:k0 + HC, c0:c0 + 256]),
                     (wstage[:, t % RING, :, 256:512], v[:, k0:k0 + HC, c1:c1 + 256]))

            for s in subs:
                w_in = {"ffn": ffn_w_in[s.layer, s.part // 2] if s.kind == "ffn" else None,
                        "conv": conv_w_in[s.conv % 2], "nsa": nsa_w_in[0], "diff": diff_w_in[0]}[s.kind]
                w_out = {"ffn": ffn_w_out[s.layer, s.part // 2] if s.kind == "ffn" else None,
                         "conv": conv_w_out[s.conv % 2], "nsa": nsa_w_out[0], "diff": diff_w_out[0]}[s.kind]

                def load_in(g):
                    for k, u in enumerate(range(g.unit0, g.end)):
                        t = stage_of["w", u]
                        slot_free(t)
                        if g.kind == "ffn_in":
                            pair(t, w_in, HC * k, 256 * g.n, D_FF + 256 * g.n)
                        elif g.kind == "conv_cv":
                            pair(t, w_in, HC * k, 256 * g.n, 2 * D_MODEL + 256 * g.n)
                        elif g.kind == "conv_b":
                            chunks(t, w_in, HC * k, HC, D_MODEL + GC * (g.n - 4))
                        elif g.kind == "gate":
                            chunks(t, w_in, HC * k, HC, NSA_IN - P, P)
                        else:
                            chunks(t, w_in, HC * k, HC, GC * g.n)

                if s.kind == "ffn":
                    load_in(s.ins[0])
                    load_in(s.ins[1])
                    g2 = s.ins[2]
                    cols = w_in.rearrange("(c p) (m n) -> m p c n", p=P, n=256)
                    with sp.Fori(0, (NF // 2 - 3) // 2) as i:
                        for k in range(4):
                            t0 = stage_of["w", g2.unit0 + k]
                            sp.wait_ge(w_low, i * 4 + (g2.unit0 + k - RING + 1))
                            for half, off in ((0, 0), (1, NF // 2)):
                                m = i * 2 + (2 + k // 2 + off)
                                sp.dma_start(wstage[:, t0 % RING, :, 256 * half:256 * half + 256],
                                             cols[bass.ds(m, 1), :, HC * (k % 2):HC * (k % 2) + HC, :]
                                             .rearrange("m p c n -> (m p) c n")).then_inc(loaded[t0 % RING], 16)
                    load_in(s.ins[-1])
                else:
                    for g in s.ins:
                        load_in(g)

                def load_out(g, k):
                    u = g.unit0 + k
                    t = stage_of["w", u]
                    slot_free(t)
                    chunks(t, w_out, HC * k, g.units[k], GC * g.n)

                outs = [(g, k) for g in s.outs for k in range(len(g.units))]
                for g, k in outs[:2]:
                    load_out(g, k)
                if s.cache_units:
                    cache = cache_nsa[0] if s.kind == "nsa" else cache_diff[0]
                    cv = cache.rearrange("g p h n -> g p (h n)")
                    if s.kind == "nsa":
                        sp.wait_ge(small_loaded, 192)
                    for b in range(DEC):
                        t = stage_of["c", s.cache0 + b]
                        slot_free(t)
                        for pg in range(N_PAGES):
                            page = sp.value_load(pages[0:1, 2 * b + pg:2 * b + pg + 1], min_val=0,
                                                 max_val=cache.shape[0] - 1)
                            sp.dma_start(wstage[:, t % RING, 2 * pg:2 * pg + 2, :].rearrange("p a n -> p (a n)"),
                                         cv[bass.ds(page, 1), :, :].rearrange("g p n -> (g p) n"))\
                                .then_inc(loaded[t % RING], 16)
                    for b in range(DEC if s.kind == "nsa" else 0):
                        t = stage_of["c", s.cache0 + DEC + b]
                        slot_free(t)
                        win = state_nsa_win[0, b].rearrange("(t p) h n -> p t (h n)", p=P)
                        for kt in range(2):
                            sp.dma_start(wstage[:, t % RING, kt, :], win[:, kt, :]).then_inc(loaded[t % RING], 16)
                for g, k in outs[2:]:
                    load_out(g, k)
                if s.kind == "nsa":
                    store(sp.dma_start(new_nsa_win_sample[0, :, 0:SEQ - 1].rearrange("b t h n -> b (t h n)"),
                                       state_nsa_win[0, :, 1:SEQ].rearrange("b t h n -> b (t h n)")),
                          win_moved, "win_moved")
            for signal in (gates_out, tok_stored, conv_stored, win_moved, y_stored):
                sp.wait_ge(signal, 16 * stores[signal.name])


_INS = ['x_prompt', 'x_sample', 'state_conv', 'cache_nsa', 'state_nsa_win', 'cache_diff', 'page_table', 'norm_g',
        'ffn_w_in', 'ffn_w_out', 'conv_w_in', 'conv_w', 'conv_w_out', 'nsa_w_in', 'nsa_w_cmp', 'nsa_w_out',
        'diff_w_in', 'diff_lambda', 'diff_subln_g', 'diff_w_out']
_OUTS = [(1, SEQ, D_MODEL), (DEC, 1, D_MODEL), (2, 1, 2, D_MODEL), (2, DEC, 2, D_MODEL), (1, 1, SEQ, 4, 256),
         (1, DEC, 1, 4, 256), (1, 1, SEQ, 4, 128), (1, DEC, SEQ, 4, 128), (1, 1, SEQ, 4, 256), (1, DEC, 1, 4, 256)]


def kernel(**inputs):
    import numpy as _np
    import concourse.bacc as _bacc
    from concourse import mybir as _mybir
    from concourse.bass_utils import run_bass_kernel_spmd as _run

    nc = _bacc.Bacc("TRN2", target_bir_lowering=False, num_devices=1)
    arrays, args = {}, []
    for name in _INS:
        a = _np.ascontiguousarray(inputs[name])
        arrays[f"in_{name}_dram"] = a
        args.append(nc.dram_tensor(f"in_{name}_dram", a.shape, _mybir.dt.from_np(a.dtype), kind="ExternalInput").ap())
    for i, shape in enumerate(_OUTS):
        args.append(nc.dram_tensor(f"out_{i}_dram", shape, _mybir.dt.float32, kind="ExternalOutput").ap())
    trunk_kernel(nc, *args)
    r = _run(nc, [arrays], core_ids=[0])
    return tuple(r.results[0][f"out_{i}_dram"] for i in range(len(_OUTS)))
```

```python
import math
from contextlib import ExitStack

import concourse.bass as bass
from concourse import mybir

F32 = mybir.dt.float32
F32R = mybir.dt.float32r
BF16 = mybir.dt.bfloat16
I32 = mybir.dt.int32
ALU = mybir.AluOpType
ACT = mybir.ActivationFunctionType
AX_X = mybir.AxisListType.X

P = 128
D_MODEL = 1024
SEQ = 256
DEC = 8
T = SEQ + DEC
DEPTH = 4
PAGE = 128
N_PAGES = 2
D_FF = 2816
HEAD = 64
GROUPS = 4
CMP_BLOCK = 32
N_CMP = SEQ // CMP_BLOCK
EPS = 1e-6
NEG = -1e30
TINY = 1e-30
NC = D_MODEL // P
NF = D_FF // P
HC = 4
GT = 4
GC = GT * P
RING = 4
NSA_QW = 1024
NSA_KVW = GROUPS * 6 * HEAD
NSA_IN = NSA_QW + NSA_KVW + 48
NSA_KVT = NSA_KVW // P
DIFF_KVT = 8
SCALE = HEAD ** -0.5
TOK = [(0, P), (P, P), (SEQ, DEC)]


def lam_init(layer):
    return 0.8 - 0.6 * math.exp(-0.3 * layer)


class Group:

    def __init__(self, kind, n, unit0, units, sub, index, tiles=GT):
        self.kind, self.n, self.unit0, self.units, self.sub, self.index, self.tiles = \
            kind, n, unit0, units, sub, index, tiles
        self.set = index % 2
        self.end = unit0 + len(units)


class Sublayer:
    pass


def make_plan():
    subs, unit, index, attends, convs, hlow = [], 0, 0, 0, 0, 0
    stage = []
    cache_unit = 0
    for layer in range(DEPTH):
        for part in range(3):
            s = Sublayer()
            s.i, s.layer, s.part = len(subs), layer, part
            mixer = ("conv", "nsa", "diff")[layer % 3]
            s.kind = mixer if part == 1 else "ffn"
            kinds = {"ffn": ["ffn_in"] * (NF // 2), "conv": ["conv_cv"] * 4 + ["conv_b"] * 2,
                     "nsa": ["q"] * 2 + ["kv"] * 3 + ["gate"], "diff": ["q"] * 2 + ["kv"] * 2}[s.kind]
            s.ins = []
            for n, kind in enumerate(kinds):
                s.ins.append(Group(kind, n, unit, [HC] * (NC // HC), s.i, index, 1 if kind == "gate" else GT))
                unit, index = unit + NC // HC, index + 1
            k_chunks = NF if s.kind == "ffn" else NC
            per = [HC] * (k_chunks // HC) + ([k_chunks % HC] if k_chunks % HC else [])
            s.outs = []
            for n in range(2):
                s.outs.append(Group("out", n, unit, per, s.i, index))
                unit, index = unit + len(per), index + 1
            s.h_piece = {"ffn": 2, "conv": 4, "nsa": 8, "diff": 8}[s.kind]
            s.h_before = hlow
            hlow += 0 if s.kind in ("nsa", "diff") else k_chunks // s.h_piece
            s.ffn = 2 * layer + part // 2
            s.conv, s.attend = convs, attends
            attends += s.kind in ("nsa", "diff")
            convs += s.kind == "conv"
            s.cache_units = {"nsa": 2 * DEC, "diff": DEC}.get(s.kind, 0)
            s.cache0 = cache_unit
            order = [("w", u) for g in s.ins for u in range(g.unit0, g.end)]
            outs = [("w", u) for g in s.outs for u in range(g.unit0, g.end)]
            order += outs[:2] + [("c", cache_unit + n) for n in range(s.cache_units)] + outs[2:]
            cache_unit += s.cache_units
            stage += order
            subs.append(s)
    return subs, stage


def trunk_kernel(nc, x_prompt, x_sample, state_conv, cache_nsa, state_nsa_win, cache_diff, page_table,
                 norm_g, ffn_w_in, ffn_w_out, conv_w_in, conv_w, conv_w_out,
                 nsa_w_in, nsa_w_cmp, nsa_w_out, diff_w_in, diff_lambda, diff_subln_g, diff_w_out,
                 y_prompt, y_sample, new_conv_prompt, new_conv_sample, new_nsa_kv_prompt, new_nsa_kv_sample,
                 new_nsa_win_prompt, new_nsa_win_sample, new_diff_kv_prompt, new_diff_kv_sample):
    subs, stage_order = make_plan()
    stage_of = {item: n for n, item in enumerate(stage_order)}
    n_norm = DEPTH * 6 * NC
    n_convw = 2 * 3 * NC
    gain_rows = n_norm + n_convw + 1
    cols_b = gain_rows - P

    ctx = ExitStack()
    with ctx:
        base = (nc.sbuf_base + 31) // 32 * 32
        cursor = [base]

        def place(name, shape, dt=F32, at=None):
            size = (math.prod(shape[1:]) * (2 if dt == BF16 else 4) + 31) // 32 * 32
            if at is None:
                at = cursor[0]
                cursor[0] += size
            return nc.alloc_sbuf_tensor_at(name, shape, dt, offset=at)

        def sem(name):
            return ctx.enter_context(nc.semaphore(name))

        wstage = place("wstage", [P, RING, HC, GC])
        w_at = cursor[0]
        w_high_ring = place("w_high_ring", [P, RING, HC, GC], F32R)
        w_low_ring = place("w_low_ring", [P, RING, HC, GC], F32R)
        slot_bytes = HC * GC * 4
        x = place("x", [P, NC, T])
        x_hi_at = cursor[0]
        x_hi = place("x_hi", [P, NC, T], F32R)
        x_lo = place("x_lo", [P, NC, T], F32R)
        y_at = cursor[0]
        y = place("y", [P, NC, T])
        sq_at = cursor[0]
        sq = place("sq", [P, NC, T])
        tmp_at = cursor[0]
        tmp = place("tmp", [P, NC, T])
        arena = cursor[0]
        h_hi = place("h_hi", [P, NF, T], F32R)
        arena_low = cursor[0]
        h_lo = place("h_lo", [P, NF, T], F32R)
        norm_at = cursor[0]
        sum_pre = place("sum_pre", [P, T])
        sum_post = place("sum_post", [P, T])
        r_pre = place("r_pre", [P, T])
        ident = place("ident", [P, P])
        ident_r = place("ident_r", [P, P], F32R)
        ident_b = place("ident_b", [P, P], BF16)
        causal = place("causal", [P, P], BF16)
        gains = place("gains", [P, gain_rows])
        conv_state = place("conv_state", [P, NC, 32])
        cmp_w = place("cmp_w", [P, CMP_BLOCK])
        cmp_w_tok = place("cmp_w_tok", [P, P])
        cmp_ok = place("cmp_ok", [P, 2, N_CMP])
        cmp_bias = place("cmp_bias", [P, 2, N_CMP])
        head_of_row = place("head_of_row", [P, 16])
        own_cmp = place("own_cmp", [P, 32, N_CMP], BF16)
        own_new = place("own_new", [P, 4, DEC], BF16)
        block_of_row = place("block_of_row", [P, 4])
        block_strip = place("block_strip", [P, 60])
        mean_col = place("mean_col", [P, 2])
        var = place("var", [P, 3])
        rs = place("rs", [P, 3])
        rs_hi = place("rs_hi", [P, 3], F32R)
        rs_lo = place("rs_lo", [P, 3], F32R)
        minus_half = place("minus_half", [P, 32])
        pages = place("pages", [1, 16], I32)
        conv_tok = place("conv_tok", [18, D_MODEL], at=cursor[0])
        kv_sample = place("kv_sample", [DEC, NSA_KVW])
        small = place("small", [P, 288])
        assert cursor[0] <= nc.sbuf_usable_end, (cursor[0], nc.sbuf_usable_end)

        gate_t, up_t, tanh_t, prod_t = (tmp[:, 2 * k:2 * k + 2, :] for k in range(4))
        tmp4 = tmp[:, 4:8, :]
        gates = small[:, 0:144].rearrange("p (t c) -> p t c", t=3)
        gate_rows = small[:, 144:147]
        lam = small[:, 147:148]
        even_row = small[:, 149:150]
        dec_sign = small[:, 150:151]
        s_mx, s_nmx, s_sum, s_coef = ([small[:, 161 + 3 * k + r:162 + 3 * k + r] for r in range(3)] for k in range(4))
        warm = small[:, 151:152]
        lam_s = small[:, 156:158]
        lam_e = small[:, 158:160]
        sub_gain = small[:, 160:161]
        sub_v, sub_r = small[:, 16:32], small[:, 0:16]
        mx, nmx, esum, coef = (small[:, 176 + 16 * k:192 + 16 * k].rearrange("p (b c) -> p b c", b=4)
                               for k in range(4))
        tok_in = place("tok_in", [P, 3, D_MODEL], at=arena)
        gain_a = place("gain_a", [P, P], at=arena + 12288)
        gain_b = place("gain_b", [cols_b, P], at=arena + 12800)
        state_tok = place("state_tok", [32, D_MODEL], at=arena + 13312)
        cmp_tok = place("cmp_tok", [CMP_BLOCK, P], at=arena + 17408)
        lam_in = place("lam_in", [P, 4, HEAD], at=arena + 17920)
        lam_p = place("lam_p", [P, 2, HEAD], at=arena + 18944)
        y_tok = place("y_tok", [P, 3, D_MODEL], at=arena)
        u_prompt = place("u_prompt", [P, NC, SEQ + 2], at=arena + NC * T * 4)
        u_sample = place("u_sample", [P, NC, 3, DEC], at=arena + NC * T * 4 + NC * (SEQ + 2) * 4)
        conv_new = place("conv_new", [P, NC, 18], at=arena_low + NC * T * 4)
        q_t = place("q_t", [P, NC, T], at=y_at)
        o_tok = place("o_tok", [P, 2, D_MODEL], at=sq_at)
        z_prompt = place("z_prompt", [P, NC, SEQ], at=sq_at)
        k_odd = place("k_odd", [P, GROUPS, 2, SEQ], at=tmp_at)
        kv_t = place("kv_t", [P, NSA_KVT, T], at=arena)
        kv_tok = place("kv_tok", [P, 2, NSA_KVW], at=arena + 12672)
        probs = place("probs", [P, 2, 4, SEQ], at=arena + 24960)
        probs_t = place("probs_t", [P, 2, 4, 2, P], at=arena + 33152)
        vc_diag = place("vc_diag", [P, 16, HEAD], at=arena + 41344)
        kc_t = place("kc_t", [P, GROUPS, N_CMP], at=arena + 45440)
        kc_diag = place("kc_diag", [P, GROUPS, 2, N_CMP], at=arena + 46208)
        vc_rep = place("vc_rep", [P, GROUPS, 4, N_CMP], at=arena + 45696)
        gate_t1 = place("gate_t1", [P, T], at=sq_at)
        cmp_prod = place("cmp_prod", [P, GROUPS, N_CMP, CMP_BLOCK], at=arena + 24960)
        cmp_s = place("cmp_s", [P, 2, 16, N_CMP], at=arena + 33152)
        cmp_e = place("cmp_e", [P, 2, 16, N_CMP], at=arena + 34176)
        cmp_m = place("cmp_m", [P, 2, 16], at=arena + 35200)
        cmp_pt = place("cmp_pt", [P, 2, P], at=arena + 36224)
        o_square = place("o_square", [P, 2, D_MODEL], at=tmp_at)
        even_tmp = place("even_tmp", [P, 64], at=arena + 19968)
        kt_dec = place("kt_dec", [P, 2, 2, P], at=x_hi_at)
        prod_dec = place("prod_dec", [P, 2, GROUPS, P], at=x_hi_at + 2048)
        q_wide = {"nsa": place("q_wide_pair", [P, 4, 160], at=x_hi_at + 6144),
                  "diff": place("q_wide", [P, 4, 288], at=x_hi_at + 6144)}
        s_rows = place("s_rows", [P, 2, SEQ], at=x_hi_at + 14592)
        kc_dec = place("kc_dec", [P, SEQ], at=norm_at)
        q_dec = place("q_dec", [P, P], at=norm_at + 1024)
        q_pair = place("q_pair", [P, P], at=norm_at + 1536)
        kc_rows = place("kc_rows", [P, 2, P], at=norm_at + 2048)
        k_pairs = place("k_pairs", [P, 2, 2, GROUPS, HEAD], at=x_hi_at + 10496)
        dec = arena + 33152
        p_dec = place("p_dec", [P, 3, SEQ + 32], at=dec)
        pt_dec = place("pt_dec", [P, 2, P], at=dec + 3456)
        ptn_dec = place("ptn_dec", [DEC, 2, GROUPS, P], at=dec + 5504)
        vc_dec = place("vc_dec", [P, 2, HEAD], at=dec + 9600)
        o_dec = place("o_dec", [P, P], at=dec + 10112)
        z_dec = place("z_dec", [P, NC, DEC], at=dec + 10624)
        o_rows = place("o_rows", [P, P], at=dec + 10880)
        pt_wide = [place("pt_wide_a", [P, 8, 288], at=arena + 12672), place("pt_wide_b", [P, 8, 288], at=x_hi_at)]

        ps = ctx.enter_context(nc.psum_tensor("ps", [P, 8, 512], F32))

        loaded = [sem(f"stage_loaded{k}") for k in range(RING)]
        w_high = sem("w_high")
        w_low = sem("w_low")
        unit_used = sem("unit_used")
        psum_drained = sem("psum_drained")
        x_updated = sem("x_updated")
        x_high = sem("x_high")
        x_low = sem("x_low")
        x_squared = sem("x_squared")
        pre_summed = sem("pre_summed")
        stats_done = sem("stats_done")
        var_ready = sem("var_ready")
        rs_ready = sem("rs_ready")
        bcast_done = sem("bcast_done")
        rstd_ready = sem("rstd_ready")
        gate_scaled = sem("gate_scaled")
        tanh_done = sem("tanh_done")
        prod_ready = sem("prod_ready")
        h_full = sem("h_full")
        h_high = sem("h_high")
        h_low = sem("h_low")
        y_copied = sem("y_copied")
        y_squared = sem("y_squared")
        tile_done = sem("tile_done")
        post_added = sem("post_added")
        y_scaled = sem("y_scaled")
        conv_step = sem("conv_step")
        conv_gathered = sem("conv_gathered")
        conv_turned = sem("conv_turned")
        conv_copied = sem("conv_copied")
        ident_ready = sem("ident_ready")
        gains_loaded = sem("gains_loaded")
        gains_turned = sem("gains_turned")
        gains_copied = sem("gains_copied")
        small_loaded = sem("small_loaded")
        xs_loaded = sem("xs_loaded")
        consts_ready = sem("consts_ready")
        pool_step = sem("pool_step")
        init_turned = sem("init_turned")
        init_copied = sem("init_copied")
        x_turned = sem("x_turned")
        lam_exp = sem("lam_exp")
        tok_turned = sem("tok_turned")
        tok_copied = sem("tok_copied")
        gates_turned = sem("gates_turned")
        gates_tanh = sem("gates_tanh")
        gates_ready = sem("gates_ready")
        gate_rows_loaded = sem("gate_rows_loaded")
        att_step = sem("att_step")
        cmp_keys = sem("cmp_keys")
        cmp_vals = sem("cmp_vals")
        o_normed = sem("o_normed")
        cmp_turned = sem("cmp_turned")
        cmp_scores = sem("cmp_scores")
        cmp_shifted = sem("cmp_shifted")
        cmp_exp = sem("cmp_exp")
        cmp_probs = sem("cmp_probs")
        cmp_pt_done = sem("cmp_pt_done")
        cmp_pt_copied = sem("cmp_pt_copied")
        cmp_out = sem("cmp_out")
        cmp_added = sem("cmp_added")
        keys_odd = sem("keys_odd")
        at_scores = sem("at_scores")
        at_max = sem("at_max")
        at_exp = sem("at_exp")
        at_turned = sem("at_turned")
        at_copied = sem("at_copied")
        at_pv = sem("at_pv")
        at_scaled = sem("at_scaled")
        dec_q = sem("dec_q")
        keys_paired = sem("keys_paired")
        cache_turned = sem("cache_turned")
        cache_keys = sem("cache_keys")
        cache_kept = sem("cache_kept")
        cache_scored = sem("cache_scored")
        cache_prod = sem("cache_prod")
        cache_summed = sem("cache_summed")
        blocks_added = sem("blocks_added")
        kc_turned = sem("kc_turned")
        kc_copied = sem("kc_copied")
        rows_added = sem("rows_added")
        dec_scores = sem("dec_scores")
        dec_max = sem("dec_max")
        dec_exp = sem("dec_exp")
        dec_probs = sem("dec_probs")
        dec_turned = sem("dec_turned")
        dec_copied = sem("dec_copied")
        dec_pv = sem("dec_pv")
        dec_added = sem("dec_added")
        dec_placed = sem("dec_placed")
        wide_zeroed = sem("wide_zeroed")
        dec_rows = sem("dec_rows")
        dec_back = sem("dec_back")
        at_mixed = sem("at_mixed")
        sub_squared = sem("sub_squared")
        sub_stats = sem("sub_stats")
        sub_var = sem("sub_var")
        sub_rs = sem("sub_rs")
        sub_bcast = sem("sub_bcast")
        z_turned = sem("z_turned")
        z_high = sem("z_high")
        y_turned = sem("y_turned")
        y_out = sem("y_out")
        z_low = sem("z_low")
        dve_const = sem("dve_const")
        lam_summed = sem("lam_summed")
        gates_out = sem("gates_out")
        tok_stored = sem("tok_stored")
        conv_stored = sem("conv_stored")
        win_moved = sem("win_moved")
        y_stored = sem("y_stored")

        gate_scratch = nc.dram_tensor("gate_scratch", (DEC, 48), F32, kind="Internal").ap()

        block = ctx.enter_context(nc.Block())

        def rows(w):
            return w.rearrange("(c p) n -> p c n", p=P)

        def b3(ap, n):
            return ap.unsqueeze(1).broadcast_to([P, n, T])

        def gset(group, tiles=GT):
            b = 4 * (group.set if isinstance(group, Group) else group)
            return ps[:, b:b + tiles, 0:T]

        def gain(layer, j, c):
            k = (layer * 6 + j) * NC + c
            return gains[:, k:k + 1]

        def pre_gain(s, c):
            return gain(s.layer, 2 * s.part, c)

        def post_gain(s, c):
            return gain(s.layer, 2 * s.part + 1, c)

        stores = {}

        def store(dma, signal, key):
            stores[key] = stores.get(key, 0) + 1
            dma.then_inc(signal, 16)

        KV_TILES = {"nsa": NSA_KVT, "diff": DIFF_KVT}
        BATCHES = {k: [(tt, j) for tt in range(3) for j in range(KV_TILES[k] // 4)] for k in KV_TILES}
        TASKS = {"nsa": [(qt, br, g) for qt in range(2) for br in (0, 1) for g in range(GROUPS)],
                 "diff": [(qt, 0, g) for qt in range(2) for g in range(GROUPS)]}
        ROUNDS = {"nsa": ["cmp", "sel", "win"], "diff": ["diff"]}
        PIECES = {"nsa": 2, "diff": 4}
        PLACES = {"nsa": (1, 3), "diff": (0, 1, 2, 3)}
        piece0 = {"nsa": 0, "diff": PIECES["nsa"] * 2 * DEC}

        def piece_at(kind, n, place_in_task):
            if n >= len(TASKS[kind]) or place_in_task not in PLACES[kind]:
                return None
            return n * PIECES[kind] + PLACES[kind].index(place_in_task)

        def pieces_to(n):
            past = 2 * DEC
            return PIECES["nsa"] * (n + 1) if n < past else piece0["diff"] + PIECES["diff"] * (n - past + 1)

        batch0 = {"nsa": 0, "diff": len(BATCHES["nsa"])}
        task0 = {"nsa": 0, "diff": len(TASKS["nsa"])}
        round0 = {"nsa": 0, "diff": len(ROUNDS["nsa"])}
        n_units = subs[-1].outs[-1].end
        unit_shape = {}
        for s in subs:
            for g in s.ins + s.outs:
                for k, n in enumerate(g.units):
                    unit_shape[g.unit0 + k] = (n, g.tiles * P)

        def norm_bank(norm):
            s = subs[norm // 2]
            return 4 * s.outs[1].set if norm % 2 else 4 * s.ins[1].set + 3

        tok_stores = {"nsa": 6, "diff": 9}

        def wide(k, kind):
            return pt_wide[1 if k == 2 else 0]

        def round_bank(name):
            return {"cmp": 4, "sel": 5, "win": 6, "diff": 5}[name]

        def round_cols(name):
            return DEC * GROUPS * N_CMP if name == "cmp" else SEQ + DEC * GROUPS

        def value_tile(kind, br):
            return (64 + 128 * (br + 1), 384, HEAD) if kind == "nsa" else (128, 256, P)

        def value_home(s):
            free = (s.outs[0].unit0 + 2) % RING
            assert free % 2 == 0
            return w_at + free * slot_bytes, w_at + (RING + free) * slot_bytes

        homes = {}
        for s in subs:
            if s.kind == "nsa":
                a, b = value_home(s)
                homes["sel"] = place("v_sel", [P, DEC, 2, GROUPS, HEAD], at=a)
                homes["win"] = place("v_win", [P, DEC, 2, GROUPS, HEAD], at=b)
            if s.kind == "diff":
                a, b = value_home(s)
                homes["diff"] = [place("v_diff_a", [P, 4, 2, GROUPS, P], at=a),
                                 place("v_diff_b", [P, 4, 2, GROUPS, P], at=b)]

        @block.gpsimd
        def _(pool):
            fill = lambda t, v: nc.gpsimd.memset(t, v).then_inc(pool_step, 1)
            fill(ident[:, :], 0.0)
            pool.wait_ge(pool_step, 1)
            nc.gpsimd.affine_select(out=ident[:, :], in_=ident[:, :], compare_op=ALU.not_equal, fill=1.0, base=0,
                                    pattern=[[-1, P]], channel_multiplier=1).then_inc(ident_ready, 1)
            fill(cmp_ok[:, :, :], 1.0)
            fill(head_of_row[:, :], 1.0)
            fill(block_of_row[:, :], 1.0)
            fill(tmp[:, 0, 0:256], 0.0)
            fill(tmp[:, 1, 0:256], 0.0)
            fill(tmp[:, 2, 0:32], 0.0)
            fill(mean_col[:, 0:1], 1.0 / D_MODEL)
            fill(mean_col[:, 1:2], 1.0 / P)
            fill(minus_half[:, :], -0.5)
            fill(var[:, :], 1.0)
            fill(small[:, :], 1.0)
            fill(even_tmp[:, :], 0.0)
            n = [13]
            pool.wait_ge(pool_step, n[0])

            def select(t, pattern, op, fill, base, mult):
                nc.gpsimd.affine_select(out=t, in_=t, compare_op=op, fill=fill, base=base,
                                        pattern=pattern, channel_multiplier=mult).then_inc(pool_step, 1)
                n[0] += 1
                pool.wait_ge(pool_step, n[0])

            def copy(dst, src):
                nc.gpsimd.tensor_copy(dst, src).then_inc(consts_ready, 1)

            pool.wait_ge(ident_ready, 1)
            copy(ident_b[:, :], ident[:, :])
            copy(ident_r[:, :], ident[:, :])
            select(tmp[:, 0, 0:P], [[-1, P]], ALU.is_ge, NEG, 0, 1)
            copy(causal[:, :], tmp[:, 0, 0:P])
            select(cmp_ok[:, :, :], [[P, 2], [-CMP_BLOCK, N_CMP]], ALU.is_ge, 0.0, -(CMP_BLOCK - 1), 1)
            nc.gpsimd.tensor_scalar(cmp_bias[:, :, :], cmp_ok[:, :, :], -1.0, -NEG, ALU.add, ALU.mult)\
                .then_inc(consts_ready, 1)
            select(head_of_row[:, :], [[-N_CMP, 16]], ALU.is_ge, 0.0, 0, 1)
            select(head_of_row[:, :], [[N_CMP, 16]], ALU.is_ge, 0.0, N_CMP - 1, -1)
            select(block_of_row[:, :], [[-CMP_BLOCK, 4]], ALU.is_ge, 0.0, 0, 1)
            select(block_of_row[:, :], [[CMP_BLOCK, 4]], ALU.is_ge, 0.0, CMP_BLOCK - 1, -1)
            fill(block_strip[:, :], 0.0)
            n[0] += 1
            pool.wait_ge(pool_step, n[0])
            copy(block_strip[:, 28:32], block_of_row[:, :])
            select(even_tmp[:, :], [[-2, 64]], ALU.not_equal, 1.0, 0, 1)
            view = tmp[:, 1, 0:256].rearrange("p (j n) -> p j n", n=N_CMP)
            select(view, [[-4, 32], [0, N_CMP]], ALU.is_ge, NEG, 0, 1)
            select(view, [[4, 32], [0, N_CMP]], ALU.is_ge, NEG, 3, -1)
            copy(own_cmp[:, :, :], view)
            view = tmp[:, 2, 0:32].rearrange("p (g b) -> p g b", b=DEC)
            select(view, [[-4, GROUPS], [-16, DEC]], ALU.is_ge, NEG, 0, 1)
            select(view, [[4, GROUPS], [16, DEC]], ALU.is_ge, NEG, 3, -1)
            copy(own_new[:, :, :], view)
            for norm in range(2 * len(subs)):
                s = subs[norm // 2]
                if norm % 2 == 0:
                    for c in range(1, NC):
                        pool.wait_ge(x_squared, NC * s.i + c + 1)
                        if c > 1:
                            pool.wait_ge(pre_summed, (NC - 1) * s.i + c - 1)
                        nc.gpsimd.tensor_tensor(sum_pre[:, :], sum_pre[:, :] if c > 1 else sq[:, 0, :], sq[:, c, :],
                                                ALU.add).then_inc(pre_summed, 1)
                if s.kind == "nsa" and norm % 2:
                    for b in range(s.cache_units):
                        t = stage_of["c", s.cache0 + b]
                        pool.wait_ge(loaded[t % RING], 32 * (t // RING + 1))
                        if b == 0:
                            pool.wait_ge(dec_q, s.attend + 1)
                        if b >= 2:
                            pool.wait_ge(cache_turned, pieces_to(s.cache0 + b - 2))
                        if b < DEC:
                            page = wstage[:, t % RING, :, :].rearrange("p (t g) (h c) -> p t (g h) c", t=2, c=256)
                            keys = page[:, :, :, 128:192]
                        else:
                            keys = wstage[:, t % RING, 0:2, :].rearrange("p t (g c) -> p t g c", g=GROUPS)[:, :, :, 0:HEAD]
                        nc.gpsimd.tensor_copy(k_pairs[:, b % 2, :, :, :], keys).then_inc(keys_paired, 1)
                if s.cache_units and norm % 2:
                    pool.wait_ge(at_scaled, task0[s.kind] + len(TASKS[s.kind]))
                    pool.wait_ge(tok_stored, 16 * tok_stores[s.kind])
                    nc.gpsimd.memset(pt_wide[0][:, :, :], 0.0).then_inc(wide_zeroed, 1)
                    if s.kind == "nsa":
                        pool.wait_ge(cache_scored, pieces_to(2 * DEC - 1))
                        nc.gpsimd.memset(pt_wide[1][:, :, :], 0.0).then_inc(wide_zeroed, 1)
                if s.kind == "diff" and norm % 2:
                    pool.wait_ge(sub_var, 1)
                    nc.gpsimd.tensor_tensor(sub_r, sub_v, minus_half[:, 0:16], ALU.pow).then_inc(sub_rs, 1)
                    pool.wait_ge(sub_var, 2)
                    nc.gpsimd.tensor_tensor(s_nmx[0][0:64, :], s_mx[0][0:64, :], minus_half[0:64, 0:1], ALU.pow)\
                        .then_inc(sub_rs, 1)
                pool.wait_ge(var_ready, 2 * norm + 2)
                nc.gpsimd.tensor_tensor(rs[:, :], var[:, :], minus_half[:, 0:3], ALU.pow).then_inc(rs_ready, 1)
                pool.wait_ge(rs_ready, 3 * norm + 1)
                nc.gpsimd.tensor_copy(rs_hi[:, :], rs[:, :]).then_inc(rs_ready, 1)
                pool.wait_ge(rs_ready, 3 * norm + 2)
                nc.gpsimd.tensor_tensor(rs_lo[:, :], rs[:, :], rs_hi[:, :].bitcast(F32), ALU.subtract)\
                    .then_inc(rs_ready, 1)

        @block.scalar
        def _(act):
            split = [0]

            def split_to(upto):
                while split[0] < upto:
                    u = split[0]
                    t = stage_of["w", u]
                    act.wait_ge(loaded[t % RING], 32 * (t // RING + 1))
                    if u >= RING:
                        act.wait_ge(unit_used, u - RING + 1)
                    n, cols = unit_shape[u]
                    nc.scalar.activation(w_high_ring[:, u % RING, 0:n, 0:cols], wstage[:, t % RING, 0:n, 0:cols],
                                         ACT.Copy).then_inc(w_high, 1)
                    split[0] += 1

            def ffn_drain(gate, piece, chunk):
                act.wait_ge(gate_scaled, gate)
                nc.scalar.activation(tanh_t, gate_t, ACT.Tanh, scale=0.5).then_inc(tanh_done, 1)
                act.wait_ge(h_full, piece)
                nc.scalar.activation(h_hi[:, chunk, :], prod_t, ACT.Copy).then_inc(h_high, 1)

            def new_x(s, chunks=range(NC)):
                for c in chunks:
                    act.wait_ge(x_updated, NC * s.i + c + 1)
                    nc.scalar.activation(x_hi[:, c, :], x[:, c, :], ACT.Copy, scale=pre_gain(s, c)).then_inc(x_high, 1)
                    nc.scalar.activation(sq[:, c, :], x[:, c, :], ACT.Square).then_inc(x_squared, 1)

            def attend(s):
                kind = s.kind
                tiles, b0, n0 = KV_TILES[kind], batch0[kind], task0[kind]
                if kind == "nsa":
                    act.wait_ge(lam_summed, 2)
                    nc.scalar.activation(lam_e, lam_s, ACT.Exp).then_inc(lam_exp, 1)
                    act.wait_ge(gates_turned, 1)
                    g_ps = ps[:, 7, 0:3 * P].rearrange("p (t c) -> p t c", t=3)[:, :, P - 48:P]
                    nc.scalar.activation(gates[:, 0:2, :], g_ps[:, 0:2, :], ACT.Tanh, scale=0.5).then_inc(gates_tanh, 1)
                    nc.scalar.activation(gates[0:DEC, 2, :], g_ps[0:DEC, 2, :], ACT.Tanh, scale=0.5)\
                        .then_inc(gates_tanh, 1)
                act.wait_ge(conv_stored, 16 * stores["conv_stored"])
                for n, (tt, j) in enumerate(BATCHES[kind]):
                    rows_n = TOK[tt][1]
                    dst = kv_tok[:, tt, 512 * j:512 * j + 512] if tt < 2 else kv_sample[:, 512 * j:512 * j + 512]
                    act.wait_ge(tok_turned, b0 + n + 1)
                    nc.scalar.activation(dst, ps[0:rows_n, n % 6, :], ACT.Copy).then_inc(tok_copied, 1)
                act.wait_ge(tok_copied, b0 + len(BATCHES[kind]))
                if kind == "nsa":
                    act.wait_ge(gates_ready, 2)
                    store(act.dma_start(gate_scratch, gates[0:DEC, 2, :]), gates_out, "gates_out")
                width = 384 if kind == "nsa" else 256
                outs = (new_nsa_kv_prompt, new_nsa_kv_sample) if kind == "nsa" else (new_diff_kv_prompt, new_diff_kv_sample)
                for tt in range(2):
                    kv = kv_tok[:, tt, 0:4 * width].rearrange("p (g c) -> p g c", g=GROUPS)
                    store(act.dma_start(outs[0][0, 0, P * tt:P * tt + P], kv[:, :, 0:256]), tok_stored, "tok_stored")
                    if kind == "nsa":
                        store(act.dma_start(new_nsa_win_prompt[0, 0, P * tt:P * tt + P], kv[:, :, 256:384]), tok_stored, "tok_stored")
                kv = kv_sample[:, 0:4 * width].rearrange("p (g c) -> p g c", g=GROUPS)
                store(act.dma_start(outs[1][0].rearrange("b t g c -> (b t) g c"), kv[:, :, 0:256]), tok_stored, "tok_stored")
                if kind == "nsa":
                    store(act.dma_start(new_nsa_win_sample[0, :, SEQ - 1], kv[:, :, 256:384]), tok_stored, "tok_stored")
                    act.wait_ge(gates_out, 16)
                    act.dma_start(gate_rows, gate_scratch.rearrange("b (r k) -> (b r) k", k=3))\
                        .then_inc(gate_rows_loaded, 16)
                    act.wait_ge(cmp_shifted, 1)
                    nc.scalar.activation(cmp_e[:, :, :, :], cmp_s[:, :, :, :], ACT.Exp, scale=SCALE).then_inc(cmp_exp, 1)
                    act.wait_ge(cmp_pt_done, 1)
                    nc.scalar.activation(cmp_pt[:, :, :].rearrange("p a b -> p (a b)"), ps[:, 7, 0:2 * P],
                                         ACT.Copy).then_inc(cmp_pt_copied, 1)
                    act.wait_ge(cmp_out, 1)
                    nc.scalar.activation(z_prompt[:, :, :].rearrange("p a b -> p (a b)"),
                                         ps[:, 0:4, :].rearrange("p a b -> p (a b)"), ACT.Copy).then_inc(cmp_added, 1)

                r0 = round0[kind]

                def keep_values(b):
                    n = s.cache0 + b
                    t = stage_of["c", n]
                    act.wait_ge(loaded[t % RING], 32 * (t // RING + 1))
                    page = wstage[:, t % RING, :, :].rearrange("p (t g) (h c) -> p t (g h) c", t=2, c=256)
                    if kind == "diff":
                        dst, src = homes["diff"][b // 4][:, b % 4, :, :, :], page[:, :, :, 128:256]
                    elif b < DEC:
                        dst, src = homes["sel"][:, b, :, :, :], page[:, :, :, 192:256]
                    else:
                        win = wstage[:, t % RING, 0:2, :].rearrange("p t (g c) -> p t g c", g=GROUPS)
                        dst, src = homes["win"][:, b - DEC, :, :, :], win[:, :, :, 64:128]
                    nc.scalar.activation(dst, src, ACT.Copy).then_inc(cache_kept, 1)

                tasks = TASKS[kind]
                for n in range(len(tasks) + 1):
                    if n < len(tasks):
                        m, keys = n0 + n, P * (tasks[n][0] + 1)
                        act.wait_ge(at_max, m + 1)
                        if m >= 2:
                            act.wait_ge(at_turned, m - 1)
                        for i in range(4):
                            nc.scalar.activation(probs[:, m % 2, i, 0:keys],
                                                 ps[:, 2 * (m % 2) + i // 2, 256 * (i % 2):256 * (i % 2) + keys],
                                                 ACT.Exp, bias=nmx[:, m % 4, i:i + 1], scale=SCALE,
                                                 accum_out=esum[:, m % 4, i:i + 1]).then_inc(at_exp, 1)
                    if n >= 1:
                        m, tiles_n = n0 + n - 1, tasks[n - 1][0] + 1
                        act.wait_ge(at_turned, m + 1)
                        if m >= 2:
                            act.wait_ge(at_pv, m - 1)
                        heads = 4 if kind == "nsa" else 2
                        nc.scalar.activation(probs_t[:, m % 2, 0:heads, 0:tiles_n, :],
                                             ps[:, 4:4 + heads // 2, :].rearrange("p a (i t q) -> p (a i) t q", i=2, t=2)[:, :, 0:tiles_n, :],
                                             ACT.Copy).then_inc(at_copied, 1)
                    if n < len(tasks):
                        keep_values(n)
                rounds = ROUNDS[kind]
                if kind == "nsa":
                    act.wait_ge(kc_turned, 1)
                    by_block = kc_dec[:, :].rearrange("p (b h g k n) -> p g k h b n", b=DEC, h=2, g=2, k=2)
                    for g in range(2):
                        for kt in range(2):
                            nc.scalar.activation(by_block[:, g, kt, :, :, :],
                                                 ps[:, 6, P * g + 64 * kt:P * g + 64 * kt + 64]
                                                 .rearrange("p (h b n) -> p h b n", h=2, b=DEC),
                                                 ACT.Copy).then_inc(kc_copied, 1)
                for k, name in enumerate(rounds):
                    bank, cols = round_bank(name), round_cols(name)
                    act.wait_ge(dec_max, r0 + k + 1)
                    nc.scalar.activation(p_dec[:, k, 0:cols], ps[:, bank, 0:cols], ACT.Exp, bias=s_nmx[k], scale=SCALE,
                                         accum_out=s_sum[k]).then_inc(dec_exp, 1)
                scale = 1.0 if kind == "nsa" else sub_gain
                act.wait_ge(tok_stored, 16 * stores["tok_stored"])
                assert stores["tok_stored"] == tok_stores[kind]
                if kind == "nsa":
                    act.wait_ge(dec_scores, r0 + len(rounds))
                    z = z_prompt[:, :, :]
                else:
                    act.wait_ge(z_turned, 1)
                    z = ps[:, 0:4, :].rearrange("p a (b t) -> p (a b) t", b=2)
                nc.scalar.activation(h_hi[:, 0:NC, 0:SEQ], z, ACT.Copy, scale=scale).then_inc(z_high, 1)
                act.wait_ge(dec_placed, s.attend + 1)
                nc.scalar.activation(h_hi[:, 0:NC, SEQ:T], z_dec[:, :, :], ACT.Copy, scale=scale).then_inc(z_high, 1)

            act.wait_ge(pool_step, 12)
            nc.scalar.activation(warm, minus_half[:, 0:1], ACT.Exp)
            act.wait_ge(xs_loaded, 32)
            small_in = lambda dst, src: act.dma_start(dst, src).then_inc(small_loaded, 16)
            small_in(lam_in[:, :, :].rearrange("p a d -> p (a d)"),
                     diff_lambda.rearrange("a b d -> a (b d)").broadcast_to([P, 4 * HEAD]))
            small_in(state_tok[:, :], state_conv.rearrange("v b s n -> (v b s) n"))
            small_in(cmp_tok[:, :].rearrange("l (k d) -> l k d", k=2), nsa_w_cmp[0].rearrange("k l d -> l k d"))
            for n in range(4):
                small_in(cmp_w_tok[32 * n:32 * n + 32, :].rearrange("l (k d) -> l k d", k=2),
                         nsa_w_cmp[0].rearrange("k l d -> l k d"))
            small_in(pages[:, :], page_table.rearrange("(a b) n -> a (b n)", a=1))
            split_to(1)
            act.wait_ge(gains_copied, 1)
            new_x(subs[0], range(0, 4))
            split_to(2)
            new_x(subs[0], range(4, NC))
            for s in subs:
                if s.kind == "ffn":
                    gates0, pieces0 = s.ffn * (NF // 2), s.h_before
                    split_to(s.ins[0].end + 2)
                    ffn_drain(gates0 + 1, pieces0 + 1, slice(0, 2))
                    u0 = split[0]
                    with act.Fori(0, (NF // 2 - 1) // 2) as i:
                        for k in range(2):
                            for j in range(2):
                                u = u0 + 2 * k + j
                                t = stage_of["w", u]
                                act.wait_ge(loaded[t % RING], i * 32 + 32 * (t // RING + 1))
                                act.wait_ge(unit_used, i * 4 + (u - RING + 1))
                                nc.scalar.activation(w_high_ring[:, u % RING, :, :], wstage[:, t % RING, :, :],
                                                     ACT.Copy).then_inc(w_high, 1)
                            ffn_drain(i * 2 + (gates0 + 2 + k), i * 2 + (pieces0 + 2 + k), bass.ds(i * 4 + (2 + 2 * k), 2))
                    split[0] = u0 + 4 * ((NF // 2 - 1) // 2)
                else:
                    for g in s.ins:
                        split_to(g.end + 2)
                        if g.kind == "conv_b":
                            act.wait_ge(h_full, s.h_before + g.n - 3)
                            nc.scalar.activation(h_hi[:, 4 * (g.n - 4):4 * (g.n - 4) + 4, :], tmp4, ACT.Copy)\
                                .then_inc(h_high, 1)
                if s.cache_units:
                    attend(s)
                g = s.outs[0]
                split_to(g.end + 2)
                act.wait_ge(unit_used, g.end)
                nc.scalar.activation(y[:, 0:GT, :], gset(g), ACT.Copy).then_inc(y_copied, 1)
                nc.scalar.activation(sq[:, 0:GT, :], gset(g), ACT.Square).then_inc(y_squared, 1)
                g = s.outs[1]
                split_to(min(g.end + 2, n_units))
                for tile in range(GT):
                    if tile < GT - 1:
                        act.wait_ge(tile_done, (GT - 1) * s.i + tile + 1)
                    else:
                        act.wait_ge(unit_used, g.end)
                    nc.scalar.activation(sq[:, GT + tile, :], gset(g)[:, tile, :], ACT.Square).then_inc(y_squared, 1)
                    if tile == GT - 1:
                        act.wait_ge(psum_drained, g.index)
                    nc.scalar.activation(y[:, GT + tile, :], gset(g)[:, tile, :], ACT.Copy)\
                        .then_inc(y_copied if tile < GT - 1 else psum_drained, 1)
                if s.kind == "conv":
                    act.wait_ge(conv_turned, s.conv + 1)
                    b = 4 * s.outs[0].set
                    nc.scalar.activation(conv_tok[:, :].rearrange("p (a n) -> p a n", a=2), ps[0:18, b:b + 2, :],
                                         ACT.Copy).then_inc(conv_copied, 1)
                    act.wait_ge(conv_copied, s.conv + 1)
                    store(act.dma_start(new_conv_prompt[s.conv, 0], conv_tok[0:2, :]), conv_stored, "conv_stored")
                    store(act.dma_start(new_conv_sample[s.conv].rearrange("b s n -> (b s) n"), conv_tok[2:18, :]),
                          conv_stored, "conv_stored")
                if s.i + 1 < len(subs):
                    new_x(subs[s.i + 1])
            for c in range(6):
                tt, half = c // 2, c % 2
                n = TOK[tt][1]
                act.wait_ge(y_turned, c + 1)
                nc.scalar.activation(y_tok[0:n, tt, 512 * half:512 * half + 512], ps[0:n, c, :], ACT.Copy)\
                    .then_inc(y_out, 1)
            act.wait_ge(y_out, 6)
            store(act.dma_start(y_prompt[0].rearrange("(t p) n -> p t n", p=P), y_tok[:, 0:2, :]), y_stored, "y_stored")
            store(act.dma_start(y_sample.rearrange("b t n -> (b t) n"), y_tok[0:DEC, 2, :]), y_stored, "y_stored")
        @block.vector
        def _(dve):
            V = nc.vector
            split = [0]

            def low_part(u, n, cols):
                V.tensor_tensor(w_low_ring[:, u % RING, 0:n, 0:cols],
                                wstage[:, stage_of["w", u] % RING, 0:n, 0:cols],
                                w_high_ring[:, u % RING, 0:n, 0:cols].bitcast(F32), ALU.subtract).then_inc(w_low, 1)

            def split_to(upto):
                while split[0] < upto:
                    u = split[0]
                    dve.wait_ge(w_high, u + 1)
                    low_part(u, *unit_shape[u])
                    split[0] += 1

            steps = {}

            def chain(ins, signal):
                steps[signal.name] = steps.get(signal.name, 0) + 1
                ins.then_inc(signal, 1)
                dve.wait_ge(signal, steps[signal.name])

            def ffn_drain(psum_set, end, before, gates, pieces, chunk):
                dve.wait_ge(unit_used, end)
                V.tensor_tensor(gate_t, ps[:, 4 * psum_set:4 * psum_set + 2, 0:T], b3(r_pre[:, :], 2), ALU.mult)\
                    .then_inc(gate_scaled, 1)
                V.scalar_tensor_tensor(out=up_t, in0=ps[:, 4 * psum_set + 2:4 * psum_set + 4, 0:T], scalar=0.5,
                                       in1=b3(r_pre[:, :], 2), op0=ALU.mult, op1=ALU.mult).then_inc(psum_drained, 1)
                dve.wait_ge(gate_scaled, gates + 1)
                dve.wait_ge(psum_drained, before + 1)
                V.tensor_tensor(up_t, gate_t, up_t, ALU.mult).then_inc(prod_ready, 1)
                dve.wait_ge(tanh_done, gates + 1)
                dve.wait_ge(prod_ready, gates + 1)
                V.scalar_tensor_tensor(out=prod_t, in0=tanh_t, scalar=1.0, in1=up_t, op0=ALU.add, op1=ALU.mult)\
                    .then_inc(h_full, 1)
                dve.wait_ge(h_high, pieces + 1)
                V.tensor_tensor(h_lo[:, chunk, :], prod_t, h_hi[:, chunk, :].bitcast(F32), ALU.subtract)\
                    .then_inc(h_low, 1)

            def norm_var(norm):
                dve.wait_ge(stats_done, norm + 1)
                b = norm_bank(norm)
                V.tensor_scalar(var[:, 0:2], ps[:, b, 0:2], EPS, None, ALU.add).then_inc(var_ready, 1)
                V.tensor_scalar(var[0:DEC, 2:3], ps[0:DEC, b, 2:3], EPS, None, ALU.add).then_inc(var_ready, 1)

            def norm_copy(s):
                dve.wait_ge(bcast_done, 2 * s.i + 1)
                V.tensor_copy(r_pre[:, :], ps[:, norm_bank(2 * s.i), 8:8 + T]).then_inc(rstd_ready, 1)
                dve.wait_ge(rstd_ready, s.i + 1)

            def low_x(s, c):
                dve.wait_ge(x_updated, NC * s.i + c + 1)
                dve.wait_ge(x_high, NC * s.i + c + 1)
                V.scalar_tensor_tensor(out=x_lo[:, c, :], in0=x[:, c, :], scalar=pre_gain(s, c),
                                       in1=x_hi[:, c, :].bitcast(F32), op0=ALU.mult, op1=ALU.subtract)\
                    .then_inc(x_low, 1)

            def copy_x(c):
                dve.wait_ge(x_turned, c + 1)
                V.tensor_copy(x[:, c, :], ps[:, c % 7, 0:T]).then_inc(x_updated, 1)

            for c in range(NC - 1):
                copy_x(c)
            dve.wait_ge(gains_turned, 1)
            V.tensor_copy(gains[:, :], ps[:, 7, 0:gain_rows]).then_inc(gains_copied, 1)
            copy_x(NC - 1)
            dve.wait_ge(gains_copied, 1)
            halves = gains[:, 0:n_norm].rearrange("p (l j c) -> p l j c", l=DEPTH, j=6)
            V.tensor_scalar(halves[:, :, 1, :], halves[:, :, 1, :], 0.5, None, ALU.mult).then_inc(gains_copied, 1)
            V.tensor_scalar(halves[:, :, 5, :], halves[:, :, 5, :], 0.5, None, ALU.mult).then_inc(gains_copied, 1)
            dve.wait_ge(gains_copied, 3)
            split_to(1)
            for c in range(4):
                low_x(subs[0], c)
            split_to(2)
            for c in range(4, NC):
                low_x(subs[0], c)

            def take_small():
                dve.wait_ge(init_turned, 1)
                V.tensor_copy(cmp_w[:, :], ps[:, 6, 256:288]).then_inc(init_copied, 1)
                V.tensor_copy(conv_state[:, :, :], ps[:, 6, 0:256].rearrange("p (c r) -> p c r", c=NC))\
                    .then_inc(init_copied, 1)
                dve.wait_ge(small_loaded, 128)
                dve.wait_ge(consts_ready, 7)
                V.tensor_tensor(lam_p[:, :, :], lam_in[:, 0:4:2, :], lam_in[:, 1:4:2, :], ALU.mult).then_inc(lam_summed, 1)
                dve.wait_ge(lam_summed, 1)
                V.tensor_reduce(lam_s, lam_p[:, :, :], AX_X, ALU.add).then_inc(lam_summed, 1)
                V.tensor_reduce(even_row, even_tmp[:, :], AX_X, ALU.max).then_inc(dve_const, 1)
                steps["dve_const"] = 1
                dve.wait_ge(lam_summed, 2)
                dve.wait_ge(dve_const, 1)

            def conv_tap(s, j, c):
                k = n_norm + (3 * s.conv + j) * NC + c
                return gains[:, k:k + 1]

            def conv_filter(s, c):
                for dst, taps in ((y[:, c, 0:SEQ], [u_prompt[:, c, j:j + SEQ] for j in range(3)]),
                                  (y[:, c, SEQ:T], [u_sample[:, c, j, :] for j in range(3)])):
                    chain(V.tensor_scalar(dst, taps[0], conv_tap(s, 0, c), None, ALU.mult), conv_step)
                    for j in (1, 2):
                        chain(V.scalar_tensor_tensor(out=dst, in0=taps[j], scalar=conv_tap(s, j, c), in1=dst,
                                                     op0=ALU.mult, op1=ALU.add), conv_step)

            def drain(s, g):
                dve.wait_ge(unit_used, g.end)
                if g.kind in ("q", "kv"):
                    dst = (q_t if g.kind == "q" else kv_t)
                    n = g.n if g.kind == "q" else g.n - 2
                    V.tensor_tensor(dst[:, 4 * n:4 * n + 4, :], gset(g), b3(r_pre[:, :], 4), ALU.mult)\
                        .then_inc(psum_drained, 1)
                elif g.kind == "gate":
                    V.tensor_tensor(gate_t1[:, :], gset(g)[:, 0, :], r_pre[:, :], ALU.mult).then_inc(psum_drained, 1)
                elif g.kind == "conv_cv":
                    if g.n == 0:
                        chain(V.memset(u_prompt[:, :, 0:2], 0.0), conv_step)
                        kept = conv_state[:, :, 16 * s.conv:16 * s.conv + 16].rearrange("p c (b s) -> p c s b", s=2)
                        for j in range(2):
                            chain(V.tensor_copy(u_sample[:, :, j, :], kept[:, :, j, :]), conv_step)
                    view = gset(g)
                    chain(V.tensor_tensor(gate_t, view[:, 0:2, :], b3(r_pre[:, :], 2), ALU.mult), conv_step)
                    V.tensor_tensor(up_t, view[:, 2:4, :], b3(r_pre[:, :], 2), ALU.mult).then_inc(psum_drained, 1)
                    dve.wait_ge(psum_drained, g.index + 1)
                    c = 2 * g.n
                    chain(V.tensor_tensor(u_prompt[:, c:c + 2, 2:SEQ + 2], gate_t[:, :, 0:SEQ], up_t[:, :, 0:SEQ],
                                          ALU.mult), conv_step)
                    chain(V.tensor_tensor(u_sample[:, c:c + 2, 2, :], gate_t[:, :, SEQ:T], up_t[:, :, SEQ:T],
                                          ALU.mult), conv_step)
                    conv_filter(s, c)
                    conv_filter(s, c + 1)
                    if g.n == 3:
                        if s.conv:
                            dve.wait_ge(conv_turned, s.conv)
                        chain(V.tensor_copy(conv_new[:, :, 0:2], u_prompt[:, :, SEQ:SEQ + 2]), conv_step)
                        V.tensor_copy(conv_new[:, :, 2:18].rearrange("p c (b s) -> p c s b", s=2),
                                      u_sample[:, :, 1:3, :]).then_inc(conv_gathered, 1)
                elif g.kind == "conv_b":
                    c = 4 * (g.n - 4)
                    if g.n > 4:
                        dve.wait_ge(h_low, s.h_before + g.n - 4)
                    V.tensor_tensor(tmp4, gset(g), b3(r_pre[:, :], 4), ALU.mult).then_inc(psum_drained, 1)
                    dve.wait_ge(psum_drained, g.index + 1)
                    V.tensor_tensor(tmp4, tmp4, y[:, c:c + 4, :], ALU.mult).then_inc(h_full, 1)
                    dve.wait_ge(h_high, s.h_before + g.n - 3)
                    V.tensor_tensor(h_lo[:, c:c + 4, :], tmp4, h_hi[:, c:c + 4, :].bitcast(F32), ALU.subtract)\
                        .then_inc(h_low, 1)

            def attend(s):
                kind = s.kind
                n0, tasks = task0[kind], TASKS[kind]

                def step(ins):
                    chain(ins, att_step)

                def decode_queries():
                    src = q_t[:, :, SEQ:T]
                    dst = q_dec[:, :].rearrange("p (b c k) -> p c b k", b=DEC, k=2)
                    if kind == "diff":
                        step(V.memset(q_dec[:, :], 0.0))
                        step(V.tensor_copy(dst[0:64, :, :, 0], src[0:64]))
                        step(V.tensor_copy(dst[64:128, :, :, 1], src[64:128]))
                        step(V.memset(q_wide[kind][:, :, :], 0.0))
                        V.tensor_copy(q_wide[kind].rearrange("p a (j c) -> p a j c", c=36)[:, :, :, 0:4],
                                      q_dec[:, :].rearrange("p (a j c) -> p a j c", a=4, c=4)).then_inc(dec_q, 1)
                    else:
                        step(V.memset(q_pair[:, :], 0.0))
                        step(V.tensor_copy(dst[0:64, :, :, 0], src[0:64]))
                        step(V.tensor_copy(dst[0:64, :, :, 1], src[64:128]))
                        by_pair = lambda t: t.rearrange("p (j e h) -> p j e h", e=2, h=4)
                        step(V.tensor_copy(by_pair(q_pair[0:64, :])[:, :, 0, :], by_pair(q_dec[0:64, :])[:, :, 0, :]))
                        step(V.tensor_copy(by_pair(q_pair[64:128, :])[:, :, 1, :], by_pair(q_dec[0:64, :])[:, :, 1, :]))
                        step(V.memset(q_wide[kind][:, :, :], 0.0))
                        V.tensor_copy(q_wide[kind].rearrange("p a (j c) -> p a j c", c=40)[:, :, :, 0:8],
                                      q_pair[:, :].rearrange("p (a j c) -> p a j c", a=4, c=8)).then_inc(dec_q, 1)

                if kind == "nsa":
                    dve.wait_ge(lam_exp, 1)
                    chain(V.tensor_tensor(lam, lam_e[:, 0:1], lam_e[:, 1:2], ALU.subtract), dve_const)
                    chain(V.tensor_scalar(lam, lam, lam_init(2), None, ALU.add), dve_const)
                    chain(V.tensor_scalar(dec_sign, lam, 1.0, None, ALU.add), dve_const)
                    chain(V.tensor_tensor(dec_sign, dec_sign, even_row, ALU.mult), dve_const)
                    chain(V.tensor_tensor(dec_sign, dec_sign, lam, ALU.subtract), dve_const)
                    chain(V.tensor_scalar(sub_gain, gains[:, gain_rows - 1:gain_rows], 1.0 - lam_init(2), None, ALU.mult),
                          dve_const)
                dve.wait_ge(psum_drained, s.ins[-1].index + 1)
                if kind == "nsa":
                    groups_t = kv_t[:, :, :].rearrange("p (g k) t -> p g k t", k=3)
                    step(V.tensor_tensor(cmp_prod[:, :, :, :],
                                         groups_t[:, :, 0, 0:SEQ].rearrange("p g (n l) -> p g n l", l=CMP_BLOCK),
                                         cmp_w[:, :].unsqueeze(1).unsqueeze(1).broadcast_to(
                                             [P, GROUPS, N_CMP, CMP_BLOCK]), ALU.mult))
                    step(V.tensor_reduce(kc_t[:, :, :], cmp_prod[:, :, :, :], AX_X, ALU.add))
                    step(V.memset(kc_diag[:, :, :, :], 0.0))
                    step(V.tensor_copy(kc_diag[0:64, :, 0, :], kc_t[0:64, :, :]))
                    step(V.tensor_copy(kc_diag[64:128, :, 1, :], kc_t[0:64, :, :]))
                    V.tensor_copy(vc_rep[64:128, :, :, :], kc_t[64:128, :, :].unsqueeze(2).broadcast_to(
                        [64, GROUPS, 4, N_CMP])).then_inc(cmp_keys, 1)
                    V.tensor_copy(k_odd[64:128, :, 0, :], groups_t[0:64, :, 1, 0:SEQ]).then_inc(keys_odd, 1)
                    V.tensor_copy(k_odd[64:128, :, 1, :], groups_t[0:64, :, 2, 0:SEQ]).then_inc(keys_odd, 1)
                    dve.wait_ge(gates_tanh, 2)
                    for t, n in ((slice(0, 2), P), (slice(2, 3), DEC)):
                        V.tensor_scalar(gates[0:n, t, :], gates[0:n, t, :], 0.5, 0.5, ALU.mult, ALU.add)\
                            .then_inc(gates_ready, 1)
                    dve.wait_ge(cmp_turned, 1)
                    V.tensor_tensor(vc_diag[:, :, :], ps[:, 6, 0:HEAD].unsqueeze(1).broadcast_to([P, 16, HEAD]),
                                    head_of_row[:, :].unsqueeze(2).broadcast_to([P, 16, HEAD]), ALU.mult)\
                        .then_inc(cmp_vals, 1)
                    dve.wait_ge(cmp_scores, 1)
                    step(V.tensor_tensor(cmp_s[:, :, :, :],
                                         ps[:, 4, 0:256].rearrange("p (q h n) -> p q h n", q=2, n=N_CMP),
                                         cmp_bias[:, :, :].unsqueeze(2).broadcast_to([P, 2, 16, N_CMP]), ALU.add))
                    step(V.tensor_reduce(cmp_m[:, :, :], cmp_s[:, :, :, :], AX_X, ALU.max))
                    m_all = cmp_m[:, :, :].unsqueeze(3).broadcast_to([P, 2, 16, N_CMP])
                    V.tensor_tensor(cmp_s[:, :, :, :], cmp_s[:, :, :, :], m_all, ALU.subtract)\
                        .then_inc(cmp_shifted, 1)
                    dve.wait_ge(cmp_exp, 1)
                    step(V.tensor_tensor(cmp_e[:, :, :, :], cmp_e[:, :, :, :],
                                         cmp_ok[:, :, :].unsqueeze(2).broadcast_to([P, 2, 16, N_CMP]), ALU.mult))
                    step(V.tensor_reduce(cmp_m[:, :, :], cmp_e[:, :, :, :], AX_X, ALU.add))
                    step(V.tensor_scalar(cmp_m[:, :, :], cmp_m[:, :, :], TINY, None, ALU.max))
                    step(V.reciprocal(cmp_m[:, :, :], cmp_m[:, :, :]))
                    dve.wait_ge(gates_ready, 2)
                    step(V.tensor_tensor(cmp_m[:, :, :], cmp_m[:, :, :],
                                         gates[:, 0:2, :].rearrange("p q (h k) -> p q h k", k=3)[:, :, :, 0], ALU.mult))
                    V.tensor_tensor(cmp_e[:, :, :, :], cmp_e[:, :, :, :], m_all, ALU.mult).then_inc(cmp_probs, 1)

                def task_max(n):
                    m, keys = n0 + n, P * (tasks[n][0] + 1)
                    dve.wait_ge(at_scores, m + 1)
                    b = 2 * (m % 2)
                    step(V.tensor_reduce(mx[:, m % 4, :].rearrange("p (a i) -> p a i", a=2),
                                         ps[:, b:b + 2, :].rearrange("p a (i k) -> p a i k", i=2)[:, :, :, 0:keys],
                                         AX_X, ALU.max))
                    V.tensor_scalar(nmx[:, m % 4, :], mx[:, m % 4, :], -SCALE, None, ALU.mult).then_inc(at_max, 1)

                def task_mix(n):
                    m, (qt, br, g) = n0 + n, tasks[n]
                    keys = P * (qt + 1)
                    dve.wait_ge(at_exp, 4 * (m + 1))
                    cf = coef[:, m % 4, :]
                    step(V.reciprocal(cf, esum[:, m % 4, :]))
                    maps = probs[:, m % 2, :, 0:keys]
                    mix = lambda: V.tensor_tensor(maps, maps, cf.unsqueeze(2).broadcast_to([P, 4, keys]), ALU.mult)
                    if kind == "nsa":
                        k = 12 * g
                        step(V.tensor_tensor(cf.rearrange("p (k a) -> p k a", k=2), cf.rearrange("p (k a) -> p k a", k=2),
                                             gates[:, qt, k:k + 12].rearrange("p (a k t) -> p k a t", k=2, t=3)[:, :, :, br + 1],
                                             ALU.mult))
                        mix().then_inc(at_mixed, 1)
                    else:
                        step(V.tensor_scalar(cf[:, 2:4], cf[:, 2:4], lam, -1.0, ALU.mult, ALU.mult))
                        step(mix())
                        V.tensor_tensor(maps[:, 0:2, :], maps[:, 0:2, :], maps[:, 2:4, :], ALU.add).then_inc(at_mixed, 1)

                def task_add(n):
                    m, (qt, br, g) = n0 + n, tasks[n]
                    dve.wait_ge(at_pv, m + 1)
                    if kind == "diff":
                        V.tensor_copy(o_tok[:, qt, 256 * g:256 * g + 256], ps[:, 6, 0:256]).then_inc(at_scaled, 1)
                        return
                    if n == 0:
                        dve.wait_ge(cmp_added, 1)
                    else:
                        dve.wait_ge(at_scaled, m)
                    z = z_prompt[:, 2 * g:2 * g + 2, P * qt:P * qt + P]
                    V.tensor_tensor(z, z, ps[:, 6, 0:256].rearrange("p (a q) -> p a q", a=2), ALU.add)\
                        .then_inc(at_scaled, 1)

                decode_queries()
                p0, r0 = piece0[kind], round0[kind]

                def add_scores(piece):
                    u, q = piece // PIECES[kind], piece % PIECES[kind]
                    kt, b, k = q * 2 // PIECES[kind], u % DEC, u // DEC
                    quad = slice(32 * (b // 2), 32 * (b // 2) + 32)
                    dst, src = s_rows[quad, k, P * kt:P * kt + P], ps[quad, 7, 256 + P * kt:256 + P * kt + P]
                    dve.wait_ge(cache_scored, p0 + piece + 1)
                    if p0 + piece:
                        dve.wait_ge(rows_added, p0 + piece)
                    if b % 2 or (kind == "diff" and q % 2):
                        V.tensor_tensor(dst, src, dst, ALU.add).then_inc(rows_added, 1)
                    else:
                        V.tensor_copy(dst, src).then_inc(rows_added, 1)

                def copy_piece(n, where):
                    piece = piece_at(kind, n, where)
                    if piece is None:
                        return
                    m = p0 + piece
                    dve.wait_ge(cache_turned, m + 1)
                    if piece:
                        add_scores(piece - 1)
                    V.tensor_copy(kt_dec[:, m % 2, :, :].rearrange("p a k -> p (a k)"), ps[:, 7, 0:2 * P])\
                        .then_inc(cache_keys, 1)

                def compress(n):
                    t = stage_of["c", n]
                    dve.wait_ge(loaded[t % RING], 32 * (t // RING + 1))
                    if n:
                        dve.wait_ge(cache_summed, n)
                    page = wstage[:, t % RING, :, :].rearrange("p (t g) (h c) -> p (t g h) c", t=2, c=256)
                    V.tensor_tensor(prod_dec[:, :, :, :].rearrange("p t g c -> p (t g) c"), page[:, :, 0:P],
                                    cmp_w_tok[:, :].unsqueeze(1).broadcast_to([P, 8, P]), ALU.mult)\
                        .then_inc(cache_prod, 1)

                for n in range(len(tasks) + 2):
                    if 1 <= n <= len(tasks):
                        task_mix(n - 1)
                    copy_piece(n, 0)
                    if n < len(tasks):
                        task_max(n)
                    copy_piece(n, 1)
                    if kind == "nsa" and 1 <= n <= DEC:
                        dve.wait_ge(cache_summed, n)
                        if n > 1:
                            dve.wait_ge(blocks_added, n - 1)
                        flat = kc_rows[:, :, :].rearrange("p g c -> p (g c)")
                        (V.tensor_copy(flat, ps[:, 6, 256:512]) if n == 1 else
                         V.tensor_tensor(flat, ps[:, 6, 256:512], flat, ALU.add)).then_inc(blocks_added, 1)
                    copy_piece(n, 2)
                    if n >= 2:
                        task_add(n - 2)
                    copy_piece(n, 3)
                    if kind == "nsa" and n < DEC:
                        compress(s.cache0 + n)
                add_scores(PIECES[kind] * len(tasks) - 1)
                rounds = ROUNDS[kind]
                for k, name in enumerate(rounds):
                    dve.wait_ge(dec_scores, r0 + k + 1)
                    step(V.tensor_reduce(s_mx[k], ps[:, round_bank(name), 0:round_cols(name)], AX_X, ALU.max))
                    V.tensor_scalar(s_nmx[k], s_mx[k], -SCALE, None, ALU.mult).then_inc(dec_max, 1)
                for k, name in enumerate(rounds):
                    cols = round_cols(name)
                    factor = gate_rows[:, k:k + 1] if kind == "nsa" else dec_sign
                    if name == "cmp":
                        dve.wait_ge(gate_rows_loaded, 16)
                    dve.wait_ge(dec_exp, r0 + k + 1)
                    step(V.tensor_scalar(s_sum[k], s_sum[k], TINY, None, ALU.max))
                    step(V.reciprocal(s_coef[k], s_sum[k]))
                    step(V.tensor_tensor(s_coef[k], s_coef[k], factor, ALU.mult))
                    V.tensor_scalar(p_dec[:, k, 0:cols], p_dec[:, k, 0:cols], s_coef[k], None, ALU.mult)\
                        .then_inc(dec_probs, 1)
                    dve.wait_ge(dec_turned, r0 + k + 1)
                    if name == "cmp":
                        V.tensor_copy(pt_dec[:, :, :].rearrange("p a b -> p (a b)"), ps[:, 7, 0:2 * P])\
                            .then_inc(dec_copied, 1)
                        V.tensor_copy(vc_dec[:, :, :].rearrange("p a b -> p (a b)"), ps[:, 4, 0:P])\
                            .then_inc(dec_copied, 1)
                    else:
                        dve.wait_ge(wide_zeroed, (max(k, 1) if kind == "nsa" else 3))
                        V.tensor_copy(wide(k, kind).rearrange("p a (j c) -> p a j c", c=36)[:, :, :, 0:4],
                                      ps[:, 7, 0:2 * P].rearrange("p (a j c) -> p a j c", j=8, c=4))\
                            .then_inc(dec_copied, 1)
                        V.tensor_copy(ptn_dec[:, k % 2, :, :].rearrange("p a b -> p (a b)"), ps[0:DEC, 4, :])\
                            .then_inc(dec_copied, 1)

                def z_low_part(k, src, t):
                    dve.wait_ge(z_high, 2 * s.attend + k + 1)
                    hi, lo = h_hi[:, 0:NC, t].bitcast(F32), h_lo[:, 0:NC, t]
                    if kind == "nsa":
                        V.tensor_tensor(lo, src, hi, ALU.subtract).then_inc(z_low, 1)
                    else:
                        V.scalar_tensor_tensor(out=lo, in0=src, scalar=sub_gain, in1=hi, op0=ALU.mult,
                                               op1=ALU.subtract).then_inc(z_low, 1)

                def copy_rows():
                    dve.wait_ge(dec_pv, r0 + len(rounds))
                    d = HEAD if kind == "nsa" else P
                    V.tensor_copy(o_rows[:, 0:d], ps[:, 5, 0:d]).then_inc(dec_rows, 1)
                    dve.wait_ge(dec_back, s.attend + 1)

                def prompt_low():
                    dve.wait_ge(tok_stored, 16 * tok_stores[kind])
                    z_low_part(0, z_prompt[:, :, :] if kind == "nsa" else
                               ps[:, 0:4, :].rearrange("p a (b t) -> p (a b) t", b=2), slice(0, SEQ))

                dve.wait_ge(at_scaled, n0 + len(tasks))
                if kind == "nsa":
                    prompt_low()
                    copy_rows()
                    pairs = ps[0:64, 5, 0:P].rearrange("p (b c k) -> p c b k", b=DEC, k=2)
                    step(V.tensor_copy(z_dec[0:64, :, :], pairs[:, :, :, 0]))
                    V.tensor_copy(z_dec[64:128, :, :], pairs[:, :, :, 1]).then_inc(dec_placed, 1)
                else:
                    heads = lambda t: t.rearrange("p q (h d) -> p (q h) d", d=P)
                    step(V.tensor_tensor(o_square[:, :, :], o_tok[:, :, :], o_tok[:, :, :], ALU.mult))
                    step(V.tensor_reduce(sub_v, heads(o_square[:, :, :]), AX_X, ALU.add))
                    V.tensor_scalar(sub_v, sub_v, 1.0 / P, EPS, ALU.mult, ALU.add).then_inc(sub_var, 1)
                    dve.wait_ge(sub_rs, 1)
                    V.tensor_tensor(heads(o_tok[:, :, :]), heads(o_tok[:, :, :]),
                                    sub_r.unsqueeze(2).broadcast_to([P, 16, P]), ALU.mult).then_inc(o_normed, 1)
                    copy_rows()
                    V.tensor_copy(o_dec[:, :], ps[:, 5, 0:P]).then_inc(dec_added, 1)
                    dve.wait_ge(dec_added, 1)
                    pairs = o_dec[:, :].rearrange("p (b c k) -> p c b k", b=DEC, k=2)
                    step(V.tensor_tensor(z_dec[:, :, :], pairs[:, :, :, 0], pairs[:, :, :, 1], ALU.add))
                    z_rows = z_dec[:, :, :].rearrange("p c b -> p (c b)")
                    V.tensor_tensor(o_dec[:, 0:64], z_rows, z_rows, ALU.mult).then_inc(sub_squared, 1)
                    dve.wait_ge(sub_stats, 1)
                    V.tensor_scalar(s_mx[0][0:64, :], ps[0:64, 6, 0:1], EPS, None, ALU.add).then_inc(sub_var, 1)
                    prompt_low()
                    dve.wait_ge(sub_bcast, 1)
                    V.tensor_tensor(z_rows, ps[:, 6, 64:128], z_rows, ALU.mult).then_inc(dec_placed, 1)
                dve.wait_ge(dec_placed, s.attend + 1)
                z_low_part(1, z_dec[:, :, :], slice(SEQ, T))

            for s in subs:
                pre, post = 2 * s.i, 2 * s.i + 1
                split_to(s.ins[0].end + 1)
                if s.i == 0:
                    take_small()
                norm_var(pre)
                split_to(s.ins[0].end + 2)
                norm_copy(s)
                if s.kind == "ffn":
                    gates0, pieces0, g1 = s.ffn * (NF // 2), s.h_before, s.ins[1]
                    ffn_drain(s.ins[0].set, s.ins[0].end, s.ins[0].index, gates0, pieces0, slice(0, 2))
                    u0 = split[0]
                    with dve.Fori(0, (NF // 2 - 1) // 2) as i:
                        for k in range(2):
                            for j in range(2):
                                u = u0 + 2 * k + j
                                dve.wait_ge(w_high, i * 4 + (u + 1))
                                low_part(u, HC, GC)
                            ffn_drain(s.ins[1 + k].set, i * 4 + s.ins[1 + k].end, i * 2 + (g1.index + k), i * 2 + (gates0 + 1 + k),
                                      i * 2 + (pieces0 + 1 + k), bass.ds(i * 4 + (2 + 2 * k), 2))
                    split[0] = u0 + 4 * ((NF // 2 - 1) // 2)
                else:
                    drain(s, s.ins[0])
                    for g in s.ins[1:]:
                        split_to(g.end + 2)
                        drain(s, g)
                if s.cache_units:
                    attend(s)
                split_to(s.outs[0].end + 2)
                dve.wait_ge(y_squared, (GT + 1) * s.i + 1)
                V.tensor_reduce(sum_post[:, :], sq[:, 0:GT, :].rearrange("p c t -> p t c"),
                                AX_X, ALU.add).then_inc(psum_drained, 1)
                dve.wait_ge(psum_drained, s.outs[0].index + 1)
                split_to(min(s.outs[1].end + 2, n_units))
                for tile in range(GT - 1):
                    dve.wait_ge(y_squared, (GT + 1) * s.i + tile + 2)
                    if tile:
                        dve.wait_ge(post_added, (GT - 1) * s.i + tile)
                    V.tensor_tensor(sum_post[:, :], sum_post[:, :], sq[:, GT + tile, :], ALU.add)\
                        .then_inc(post_added, 1)
                norm_var(post)
                dve.wait_ge(psum_drained, s.outs[1].index + 1)
                dve.wait_ge(bcast_done, post + 1)
                r_post = ps[:, norm_bank(post), 8:8 + T]
                def scale_y(c):
                    V.scalar_tensor_tensor(out=y[:, c, :], in0=y[:, c, :], scalar=post_gain(s, c),
                                           in1=r_post, op0=ALU.mult, op1=ALU.mult).then_inc(y_scaled, 1)

                scale_y(0)
                for c in range(NC):
                    dve.wait_ge(y_scaled, NC * s.i + c + 1)
                    V.tensor_tensor(x[:, c, :], x[:, c, :], y[:, c, :], ALU.add).then_inc(x_updated, 1)
                    if c + 1 < NC:
                        scale_y(c + 1)
                    if c and s.i + 1 < len(subs):
                        low_x(subs[s.i + 1], c - 1)
                if s.i + 1 < len(subs):
                    dve.wait_ge(x_updated, NC * (s.i + 2))
                    low_x(subs[s.i + 1], NC - 1)

        @block.tensor
        def _(pe):
            MM = nc.tensor.matmul
            TR = nc.tensor.transpose

            def products(psum_bank, u, k, tile, hi, lo, first, last):
                wh = w_high_ring[:, u % RING, k, tile * P:tile * P + P]
                wl = w_low_ring[:, u % RING, k, tile * P:tile * P + P]
                out = ps[:, psum_bank, 0:T]
                MM(out, wh, hi, start=first, stop=False)
                MM(out, wh, lo, start=False, stop=False)
                return MM(out, wl, hi, start=False, stop=last)

            def norm_stats(norm, squares, first=True, last=True):
                b = norm_bank(norm)
                for tt, (t0, n) in enumerate(TOK):
                    mm = MM(ps[0:n, b, tt:tt + 1], squares[:, t0:t0 + n], mean_col[:, 0:1], start=(first and tt == 0),
                            stop=last, skip_group_check=True)
                if last:
                    mm.then_inc(stats_done, 1)

            def norm_bcast(norm):
                pe.wait_ge(rs_ready, 3 * (norm + 1))
                b = norm_bank(norm)
                for tt, (t0, n) in enumerate(TOK):
                    out = ps[:, b, 8 + t0:8 + t0 + n]
                    MM(out, rs_hi[0:n, tt:tt + 1].broadcast_to([n, P]), ident_r[0:n, 0:n], start=(tt == 0), stop=False,
                       skip_group_check=True)
                    mm = MM(out, rs_lo[0:n, tt:tt + 1].broadcast_to([n, P]), ident_r[0:n, 0:n], start=False, stop=True,
                            skip_group_check=True)
                mm.then_inc(bcast_done, 1)

            def group_units(s, g):
                first_of_sub, second = g is s.ins[0], g is s.ins[1]
                if g.index >= 2:
                    pe.wait_ge(psum_drained, g.index - 1)
                for k, u in enumerate(range(g.unit0, g.end)):
                    pe.wait_ge(w_low, u + 1)
                    if second and k == 0:
                        for tile in range(GT):
                            if tile == 1:
                                norm_bcast(2 * s.i)
                            if tile == 2 and s.i == 0:
                                pe.wait_ge(init_copied, 2)
                            if tile == GT - 1:
                                pe.wait_ge(rstd_ready, s.i + 1)
                            for c in range(HC):
                                mm = products(4 * g.set + tile, u, c, tile, x_hi[:, c, :], x_lo[:, c, :], c == 0, False)
                    else:
                        for j in range(HC):
                            c = HC * k + j
                            if first_of_sub:
                                w = lambda ring, tile: ring[:, u % RING, j, tile * P:tile * P + P]
                                out = lambda tile: ps[:, 4 * g.set + tile, 0:T]
                                pe.wait_ge(x_high, NC * s.i + c + 1)
                                for tile in range(g.tiles):
                                    MM(out(tile), w(w_high_ring, tile), x_hi[:, c, :], start=(c == 0), stop=False)
                                    MM(out(tile), w(w_low_ring, tile), x_hi[:, c, :], start=False, stop=False)
                                pe.wait_ge(x_low, NC * s.i + c + 1)
                                for tile in range(g.tiles):
                                    mm = MM(out(tile), w(w_high_ring, tile), x_lo[:, c, :], start=False,
                                            stop=(c == NC - 1))
                                continue
                            for tile in range(g.tiles):
                                mm = products(4 * g.set + tile, u, j, tile, x_hi[:, c, :], x_lo[:, c, :],
                                              c == 0, c == NC - 1)
                    mm.then_inc(unit_used, 1)

            def turn_x(c):
                for tt, (t0, n) in enumerate(TOK):
                    mm = TR(ps[:, c % 7, t0:t0 + n], tok_in[0:n, tt, c * P:c * P + P], ident[0:n, 0:n])
                mm.then_inc(x_turned, 1)

            pe.wait_ge(ident_ready, 1)
            pe.wait_ge(xs_loaded, 32)
            for c in range(NC - 1):
                turn_x(c)
            pe.wait_ge(gains_loaded, 64)
            TR(ps[:, 7, 0:P], gain_a[:, :], ident[:, :])
            TR(ps[:, 7, P:P + cols_b], gain_b[:, :], ident[0:cols_b, 0:cols_b]).then_inc(gains_turned, 1)
            pe.wait_ge(x_updated, 1)
            turn_x(NC - 1)
            pe.wait_ge(x_updated, NC)
            pe.wait_ge(consts_ready, 7)

            def turn_small():
                pe.wait_ge(small_loaded, 128)
                TR(ps[:, 6, 256:288], cmp_tok[:, :], ident[0:32, 0:32])
                for c in range(NC):
                    mm = TR(ps[:, 6, 32 * c:32 * c + 32], state_tok[:, c * P:c * P + P], ident[0:32, 0:32])
                mm.then_inc(init_turned, 1)

            def attend(s):
                kind = s.kind
                n0, b0, tasks = task0[kind], batch0[kind], TASKS[kind]
                pe.wait_ge(psum_drained, s.ins[-1].index + 1)
                if kind == "nsa":
                    for tt, (t0, n) in enumerate(TOK):
                        mm = TR(ps[0:n, 7, P * tt:P * tt + P], gate_t1[:, t0:t0 + n], ident[:, :])
                    mm.then_inc(gates_turned, 1)
                for n, (tt, j) in enumerate(BATCHES[kind]):
                    t0, rows_n = TOK[tt]
                    if n >= 6:
                        pe.wait_ge(tok_copied, b0 + n - 5)
                    for i in range(4):
                        mm = TR(ps[0:rows_n, n % 6, P * i:P * i + P], kv_t[:, 4 * j + i, t0:t0 + rows_n], ident[:, :])
                    mm.then_inc(tok_turned, 1)
                pe.wait_ge(tok_copied, b0 + len(BATCHES[kind]))
                if kind == "nsa":
                    pe.wait_ge(cmp_keys, 1)
                    TR(ps[:, 6, 0:HEAD], vc_rep[64:128, :, :, :].rearrange("p g h n -> p (g h n)"),
                       ident[64:128, 64:128]).then_inc(cmp_turned, 1)
                    for qt in range(2):
                        for c in range(NC):
                            col = P * qt + 2 * N_CMP * c
                            mm = MM(ps[:, 4, col:col + 2 * N_CMP], q_t[:, c, P * qt:P * qt + P],
                                    kc_diag[:, c // 2, :, :].rearrange("p k n -> p (k n)"), start=True, stop=True,
                                    skip_group_check=True)
                    mm.then_inc(cmp_scores, 1)
                    pe.wait_ge(cmp_probs, 1)
                    pe.wait_ge(gates_tanh, 2)
                    for qt in range(2):
                        mm = TR(ps[:, 7, P * qt:P * qt + P], cmp_e[:, qt, :, :].rearrange("p h n -> p (h n)"), ident[:, :])
                    mm.then_inc(cmp_pt_done, 1)
                    pe.wait_ge(cmp_pt_copied, 1)
                    pe.wait_ge(cmp_vals, 1)
                    for c in range(NC):
                        mm = MM(ps[:, c // 2, 256 * (c % 2):256 * (c % 2) + 256],
                                vc_diag[:, 2 * c:2 * c + 2, :].rearrange("p h d -> p (h d)"),
                                cmp_pt[:, :, :].rearrange("p t q -> p (t q)"), start=True, stop=True,
                                skip_group_check=True)
                    mm.then_inc(cmp_out, 1)
                    pe.wait_ge(cmp_added, 1)
                    pe.wait_ge(keys_odd, 2)

                def task_scores(n):
                    m, (qt, br, g) = n0 + n, tasks[n]
                    if n >= 2:
                        pe.wait_ge(at_exp, 4 * (m - 1))
                    keys = P * (qt + 1)
                    for i in range(4):
                        odd, a = i // 2, i % 2
                        if kind == "nsa":
                            k = k_odd[64:128, g, br, 0:keys] if odd else kv_t[0:64, 3 * g + 1 + br, 0:keys]
                        else:
                            k = kv_t[64 * odd:64 * odd + 64, 2 * g, 0:keys]
                        bank, col = 2 * (m % 2) + odd, 256 * a
                        MM(ps[:, bank, col:col + keys], q_t[64 * odd:64 * odd + 64, 2 * g + a, P * qt:P * qt + P], k,
                           start=(a == 0), stop=False, skip_group_check=True)
                    for odd in range(2):
                        diagonal = ps[:, 2 * (m % 2) + odd, :].rearrange("p (a k) -> p a k", a=2)[:, :, P * qt:P * qt + P]
                        mm = MM(diagonal, ident_b[:, :], causal[:, :].unsqueeze(1).broadcast_to([P, 2, P]),
                                start=False, stop=True, skip_group_check=True)
                    mm.then_inc(at_scores, 1)

                def task_turn(n):
                    m, (qt, br, g) = n0 + n, tasks[n]
                    pe.wait_ge(at_mixed, m + 1)
                    if n >= 1:
                        pe.wait_ge(at_copied, m)
                    for i in range(4 if kind == "nsa" else 2):
                        for kt in range(qt + 1):
                            col = 256 * (i % 2) + P * kt
                            mm = TR(ps[:, 4 + i // 2, col:col + P], probs[:, m % 2, i, P * kt:P * kt + P], ident[:, :])
                    mm.then_inc(at_turned, 1)

                def task_values(n):
                    m, (qt, br, g) = n0 + n, tasks[n]
                    v0, vstep, d = value_tile(kind, br)
                    pe.wait_ge(at_copied, m + 1)
                    if n >= 1:
                        pe.wait_ge(at_scaled, m)
                    first = True
                    for odd in range(2 if kind == "nsa" else 0):
                        for kt in range(qt + 1):
                            mm = MM(ps[64 * odd:64 * odd + 64, 6, 0:256], kv_tok[:, kt, v0 + vstep * g:v0 + vstep * g + d],
                                    probs_t[:, m % 2, 2 * odd:2 * odd + 2, kt, :], start=(kt == 0), stop=(kt == qt),
                                    skip_group_check=True)
                    for i in range(0 if kind == "nsa" else 2):
                        for kt in range(qt + 1):
                            mm = MM(ps[:, 6, d * i:d * i + d], probs_t[:, m % 2, i, kt, :],
                                    kv_tok[:, kt, v0 + vstep * g:v0 + vstep * g + d], start=first, stop=(kt == qt),
                                    skip_group_check=True)
                            first = False
                    mm.then_inc(at_pv, 1)

                p0, kd = piece0[kind], (64 if kind == "nsa" else P)

                def piece_tiles(piece):
                    u, q = piece // PIECES[kind], piece % PIECES[kind]
                    tiles = [(q, 0), (q, 1)] if kind == "nsa" else [(q // 2, 2 * (q % 2)), (q // 2, 2 * (q % 2) + 1)]
                    return u, stage_of["c", s.cache0 + u], tiles

                def turn_piece(piece):
                    u, t, tiles = piece_tiles(piece)
                    if kind == "nsa":
                        pe.wait_ge(keys_paired, u + 1)
                    else:
                        pe.wait_ge(loaded[t % RING], 32 * (t // RING + 1))
                    for i, (kt, e) in enumerate(tiles):
                        if kind == "nsa":
                            keys = k_pairs[:, u % 2, kt, 2 * e:2 * e + 2, :].rearrange("p g d -> p (g d)")
                        else:
                            page = wstage[:, t % RING, 2 * kt:2 * kt + 2, :].rearrange("p a (g c) -> p (a g) c", g=2)
                            keys = page[:, e, 0:P]
                        mm = TR(ps[:, 7, P * i:P * i + P], keys, ident[:, :])
                    mm.then_inc(cache_turned, 1)

                def score_piece(piece):
                    u, t, tiles = piece_tiles(piece)
                    pe.wait_ge(cache_keys, p0 + piece + 1)
                    b, n = u % DEC, (2 if kind == "nsa" else 4)
                    quad = b // 2
                    for i, (kt, e) in enumerate(tiles):
                        j = n * (b % 2) + e
                        mm = MM(ps[32 * quad:32 * quad + 32, 7, 256 + P * kt:256 + P * kt + P],
                                q_wide[kind][:, quad, 32 * j:32 * j + 32], kt_dec[:, (p0 + piece) % 2, i, :],
                                start=(i == 0), stop=(i == 1), skip_group_check=True)
                    mm.then_inc(cache_scored, 1)

                def piece_step(n, where):
                    piece = piece_at(kind, n, where)
                    if piece is None:
                        return
                    if piece:
                        score_piece(piece - 1)
                    else:
                        pe.wait_ge(dec_q, s.attend + 1)
                    turn_piece(piece)

                def sum_blocks(b):
                    pe.wait_ge(cache_prod, b + 1)
                    for i in range(4):
                        kt, pair = i // 2, i % 2
                        mm = MM(ps[32 * i:32 * i + 32, 6, 256:512], block_strip[:, 28 - 4 * b:60 - 4 * b],
                                prod_dec[:, kt, 2 * pair:2 * pair + 2, :].rearrange("p g c -> p (g c)"),
                                start=True, stop=True, skip_group_check=True)
                    mm.then_inc(cache_summed, 1)

                for n in range(len(tasks) + 2):
                    piece_step(n, 0)
                    if n < len(tasks):
                        task_scores(n)
                    piece_step(n, 1)
                    if kind == "nsa" and 1 <= n <= DEC:
                        if n >= 3:
                            pe.wait_ge(at_scaled, n0 + n - 2)
                        sum_blocks(n - 1)
                    if 1 <= n <= len(tasks):
                        task_turn(n - 1)
                    piece_step(n, 2)
                    if kind == "nsa" and 1 <= n <= DEC:
                        pe.wait_ge(blocks_added, n)
                    if n >= 2:
                        task_values(n - 2)
                    piece_step(n, 3)
                    if n == len(tasks):
                        score_piece(PIECES[kind] * n - 1)
                pe.wait_ge(at_scaled, n0 + len(tasks))

                r0, rounds = round0[kind], ROUNDS[kind]

                def page_scores(k, bank, new_tile):
                    pe.wait_ge(rows_added, pieces_to(s.cache0 + DEC * (k + 1) - 1))
                    MM(ps[:, bank, 0:SEQ], ident[:, :], s_rows[:, k, :], start=True, stop=True, skip_group_check=True)
                    for g in range(GROUPS):
                        MM(ps[:, bank, 256 + DEC * g:256 + DEC * g + DEC], q_dec[0:kd, :], kv_t[0:kd, new_tile(g), SEQ:T],
                           start=False, stop=False, skip_group_check=True)
                    MM(ps[:, bank, 256:288], ident_b[:, :], own_new[:, :, :].rearrange("p g b -> p (g b)"),
                       start=False, stop=True, skip_group_check=True).then_inc(dec_scores, 1)

                def turn_probs(k):
                    pe.wait_ge(dec_probs, r0 + k + 1)
                    if k:
                        pe.wait_ge(dec_copied, 2 * (r0 + k))
                    for kt in range(2):
                        mm = TR(ps[:, 7, P * kt:P * kt + P], p_dec[:, k, P * kt:P * kt + P], ident[:, :])
                    if rounds[k] == "cmp":
                        for kt in range(2):
                            mm = TR(ps[:, 4, HEAD * kt:HEAD * kt + HEAD], kc_dec[64:128, P * kt:P * kt + P],
                                    ident[64:128, 64:128])
                    else:
                        for g in range(GROUPS):
                            mm = TR(ps[0:DEC, 4, P * g:P * g + P], p_dec[:, k, 256 + DEC * g:256 + DEC * g + DEC], ident[:, :])
                    mm.then_inc(dec_turned, 1)

                def round_values(k, br, values):
                    v0, vstep, d = value_tile(kind, br)
                    pe.wait_ge(dec_copied, 2 * (r0 + k + 1))
                    for g in range(GROUPS):
                        MM(ps[:, 5, 0:d], ptn_dec[:, k % 2, g, :], kv_sample[:, v0 + vstep * g:v0 + vstep * g + d],
                           start=(g == 0 and k == 0), stop=False, skip_group_check=True)
                    for b in range(DEC):
                        for kt in range(2):
                            for g in range(GROUPS):
                                quad, j = b // 2, 4 * (b % 2) + g
                                mm = MM(ps[32 * quad:32 * quad + 32, 5, 0:d],
                                        wide(k, kind)[:, 4 * kt + quad, 32 * j:32 * j + 32], values(b, kt, g),
                                        start=False, stop=True, skip_group_check=True)
                    mm.then_inc(dec_pv, 1)

                def turn_rows():
                    d = HEAD if kind == "nsa" else P
                    pe.wait_ge(dec_rows, s.attend + 1)
                    TR(ps[0:d, 5, 0:P], o_rows[:, 0:d], ident[:, :]).then_inc(dec_back, 1)

                def turn_prompt():
                    for qt in range(2):
                        for c in range(NC):
                            col = 256 * (c % 2) + P * qt
                            mm = TR(ps[:, c // 2, col:col + P], o_tok[:, qt, P * c:P * c + P], ident[:, :])
                    mm.then_inc(z_turned, 1)

                if kind == "nsa":
                    for g in range(2):
                        mm = TR(ps[:, 6, P * g:P * g + P], kc_rows[:, g, :], ident[:, :])
                    mm.then_inc(kc_turned, 1)
                    pe.wait_ge(kc_copied, 4)
                    MM(ps[:, 4, 0:256], q_dec[0:64, :], kc_dec[0:64, :], start=True, stop=False, skip_group_check=True)
                    MM(ps[:, 4, 0:256], ident_b[:, :], own_cmp[:, :, :].rearrange("p j n -> p (j n)"),
                       start=False, stop=True, skip_group_check=True).then_inc(dec_scores, 1)
                    page_scores(0, 5, lambda g: 3 * g + 1)
                    page_scores(1, 6, lambda g: 3 * g + 2)
                    turn_probs(0)
                    turn_probs(1)
                    pe.wait_ge(dec_exp, r0 + 2)
                    for kt in range(2):
                        mm = MM(ps[:, 5, 0:HEAD], pt_dec[:, kt, :], vc_dec[:, kt, :], start=(kt == 0), stop=False,
                                skip_group_check=True)
                    mm.then_inc(dec_pv, 1)
                    turn_probs(2)
                    round_values(1, 0, lambda b, kt, g: homes["sel"][:, b, kt, g, :])
                    round_values(2, 1, lambda b, kt, g: homes["win"][:, b, kt, g, :])
                    turn_rows()
                else:
                    page_scores(0, 5, lambda g: 2 * g)
                    turn_probs(0)
                    round_values(0, 0, lambda b, kt, g: homes["diff"][b // 4][:, b % 4, kt, g, :])
                    pe.wait_ge(o_normed, 1)
                    turn_prompt()
                    turn_rows()
                    pe.wait_ge(sub_squared, 1)
                    MM(ps[0:64, 6, 0:1], o_dec[:, 0:64], mean_col[:, 1:2], start=True, stop=True).then_inc(sub_stats, 1)
                    pe.wait_ge(sub_rs, 2)
                    MM(ps[:, 6, 64:128], s_nmx[0][0:64, :].broadcast_to([64, P]), ident[0:64, 0:64], start=True, stop=True)\
                        .then_inc(sub_bcast, 1)

            for s in subs:
                g0, g1 = s.ins[0], s.ins[1]
                group_units(s, g0)
                pe.wait_ge(pre_summed, (NC - 1) * (s.i + 1))
                pe.wait_ge(psum_drained, g0.index)
                norm_stats(2 * s.i, sum_pre)
                if s.i == 0:
                    turn_small()
                group_units(s, g1)
                if s.kind == "ffn":
                    with pe.Fori(0, (NF // 2 - 3) // 2) as i:
                        for k in range(2):
                            g = s.ins[2 + k]
                            pe.wait_ge(psum_drained, i * 2 + (g.index - 1))
                            for j in range(2):
                                u = g.unit0 + j
                                pe.wait_ge(w_low, i * 4 + (u + 1))
                                for cc in range(HC):
                                    c = HC * j + cc
                                    for tile in range(GT):
                                        mm = products(4 * g.set + tile, u, cc, tile, x_hi[:, c, :], x_lo[:, c, :],
                                                      c == 0, c == NC - 1)
                                mm.then_inc(unit_used, 1)
                    group_units(s, s.ins[-1])
                else:
                    for g in s.ins[2:]:
                        group_units(s, g)
                if s.cache_units:
                    attend(s)
                for g in s.outs:
                    pe.wait_ge(psum_drained, g.index - 1)
                    if s.cache_units:
                        pe.wait_ge(z_low, 2 * (s.attend + 1))
                    chunk0, n_chunks = 0, sum(g.units)
                    for k, u in enumerate(range(g.unit0, g.end)):
                        pe.wait_ge(w_low, u + 1)
                        if g.n == 1 and u == g.end - 1:
                            for tile in range(GT):
                                for j in range(g.units[k]):
                                    c = chunk0 + j
                                    mm = products(4 * g.set + tile, u, j, tile, h_hi[:, c, :], h_lo[:, c, :],
                                                  c == 0, c == n_chunks - 1)
                                mm.then_inc(tile_done if tile < GT - 1 else unit_used, 1)
                            break
                        for j in range(g.units[k]):
                            c = chunk0 + j
                            if not s.cache_units and g.n == 0 and c % s.h_piece == 0:
                                pe.wait_ge(h_low, s.h_before + c // s.h_piece + 1)
                            for tile in range(GT):
                                mm = products(4 * g.set + tile, u, j, tile, h_hi[:, c, :], h_lo[:, c, :],
                                              c == 0, c == n_chunks - 1)
                        mm.then_inc(unit_used, 1)
                        chunk0 += g.units[k]
                pe.wait_ge(post_added, (GT - 1) * (s.i + 1))
                pe.wait_ge(y_copied, GT * s.i + 2)
                norm_stats(2 * s.i + 1, sum_post, last=False)
                pe.wait_ge(y_squared, (GT + 1) * (s.i + 1))
                norm_stats(2 * s.i + 1, sq[:, NC - 1, :], first=False)
                norm_bcast(2 * s.i + 1)
                if s.kind == "conv":
                    pe.wait_ge(conv_gathered, s.conv + 1)
                    b = 4 * s.outs[0].set
                    pe.wait_ge(psum_drained, s.outs[0].index + 1)
                    for c in range(NC):
                        mm = TR(ps[0:18, b + c // 4, P * (c % 4):P * (c % 4) + P], conv_new[:, c, :], ident[:, :])
                    mm.then_inc(conv_turned, 1)
                    pe.wait_ge(conv_copied, s.conv + 1)
            pe.wait_ge(x_updated, NC * (len(subs) + 1))
            for c in range(6):
                tt, half = c // 2, c % 2
                t0, n = TOK[tt]
                for j in range(4):
                    mm = TR(ps[0:n, c, P * j:P * j + P], x[:, 4 * half + j, t0:t0 + n], ident[:, :])
                mm.then_inc(y_turned, 1)

        @block.sync
        def _(sp):
            for half in range(2):
                sp.dma_start(wstage[:, 0, :, 256 * half:256 * half + 256],
                             rows(ffn_w_in[0, 0])[:, 0:HC, D_FF * half:D_FF * half + 256]).then_inc(loaded[0], 16)
            sp.dma_start(tok_in[:, 0:2, :], x_prompt[0].rearrange("(t p) n -> p t n", p=P)).then_inc(xs_loaded, 16)
            sp.dma_start(tok_in[0:DEC, 2, :], x_sample.rearrange("b t n -> (b t) n")).then_inc(xs_loaded, 16)
            g2 = norm_g.rearrange("l j (c p) -> (l j c) p", p=P)
            sp.dma_start(gain_a[:, :], g2[0:P, :]).then_inc(gains_loaded, 16)
            sp.dma_start(gain_b[0:n_norm - P, :], g2[P:n_norm, :]).then_inc(gains_loaded, 16)
            sp.dma_start(gain_b[n_norm - P:cols_b - 1, :], conv_w.rearrange("v j (c p) -> (v j c) p", p=P))\
                .then_inc(gains_loaded, 16)
            sp.dma_start(gain_b[cols_b - 1:cols_b, :], diff_subln_g).then_inc(gains_loaded, 16)

            def slot_free(t):
                if t < RING:
                    return
                kind, n = stage_order[t - RING]
                if kind == "w":
                    sp.wait_ge(w_low, n + 1)
                else:
                    if n < 2 * DEC:
                        sp.wait_ge(keys_paired, n + 1)
                    else:
                        sp.wait_ge(cache_turned, pieces_to(n))
                    sp.wait_ge(cache_kept, n + 1)
                    if n < DEC:
                        sp.wait_ge(cache_prod, n + 1)

            def load(t, *parts):
                for dst, src in parts:
                    sp.dma_start(dst, src).then_inc(loaded[t % RING], 16)

            def chunks(t, w, k0, n, c0, cols=GC):
                h, v = n // 2, rows(w)
                load(t, (wstage[:, t % RING, 0:h, 0:cols], v[:, k0:k0 + h, c0:c0 + cols]),
                     (wstage[:, t % RING, h:n, 0:cols], v[:, k0 + h:k0 + n, c0:c0 + cols]))

            def pair(t, w, k0, c0, c1):
                v = rows(w)
                load(t, (wstage[:, t % RING, :, 0:256], v[:, k0:k0 + HC, c0:c0 + 256]),
                     (wstage[:, t % RING, :, 256:512], v[:, k0:k0 + HC, c1:c1 + 256]))

            for s in subs:
                w_in = {"ffn": ffn_w_in[s.layer, s.part // 2] if s.kind == "ffn" else None,
                        "conv": conv_w_in[s.conv % 2], "nsa": nsa_w_in[0], "diff": diff_w_in[0]}[s.kind]
                w_out = {"ffn": ffn_w_out[s.layer, s.part // 2] if s.kind == "ffn" else None,
                         "conv": conv_w_out[s.conv % 2], "nsa": nsa_w_out[0], "diff": diff_w_out[0]}[s.kind]

                def load_in(g):
                    for k, u in enumerate(range(g.unit0, g.end)):
                        t = stage_of["w", u]
                        slot_free(t)
                        if t == 0:
                            continue
                        if g.kind == "ffn_in":
                            pair(t, w_in, HC * k, 256 * g.n, D_FF + 256 * g.n)
                        elif g.kind == "conv_cv":
                            pair(t, w_in, HC * k, 256 * g.n, 2 * D_MODEL + 256 * g.n)
                        elif g.kind == "conv_b":
                            chunks(t, w_in, HC * k, HC, D_MODEL + GC * (g.n - 4))
                        elif g.kind == "gate":
                            chunks(t, w_in, HC * k, HC, NSA_IN - P, P)
                        else:
                            chunks(t, w_in, HC * k, HC, GC * g.n)

                if s.kind == "ffn":
                    load_in(s.ins[0])
                    load_in(s.ins[1])
                    g2 = s.ins[2]
                    cols = w_in.rearrange("(c p) (m n) -> m p c n", p=P, n=256)
                    with sp.Fori(0, (NF // 2 - 3) // 2) as i:
                        for k in range(4):
                            t0 = stage_of["w", g2.unit0 + k]
                            sp.wait_ge(w_low, i * 4 + (g2.unit0 + k - RING + 1))
                            for half, off in ((0, 0), (1, NF // 2)):
                                m = i * 2 + (2 + k // 2 + off)
                                sp.dma_start(wstage[:, t0 % RING, :, 256 * half:256 * half + 256],
                                             cols[bass.ds(m, 1), :, HC * (k % 2):HC * (k % 2) + HC, :]
                                             .rearrange("m p c n -> (m p) c n")).then_inc(loaded[t0 % RING], 16)
                    load_in(s.ins[-1])
                else:
                    for g in s.ins:
                        load_in(g)

                def load_out(g, k):
                    u = g.unit0 + k
                    t = stage_of["w", u]
                    slot_free(t)
                    chunks(t, w_out, HC * k, g.units[k], GC * g.n)

                outs = [(g, k) for g in s.outs for k in range(len(g.units))]
                for g, k in outs[:2]:
                    load_out(g, k)
                if s.cache_units:
                    cache = cache_nsa[0] if s.kind == "nsa" else cache_diff[0]
                    cv = cache.rearrange("g p h n -> g p (h n)")
                    if s.kind == "nsa":
                        sp.wait_ge(small_loaded, 128)
                    for b in range(DEC):
                        t = stage_of["c", s.cache0 + b]
                        slot_free(t)
                        for pg in range(N_PAGES):
                            page = sp.value_load(pages[0:1, 2 * b + pg:2 * b + pg + 1], min_val=0,
                                                 max_val=cache.shape[0] - 1)
                            sp.dma_start(wstage[:, t % RING, 2 * pg:2 * pg + 2, :].rearrange("p a n -> p (a n)"),
                                         cv[bass.ds(page, 1), :, :].rearrange("g p n -> (g p) n"))\
                                .then_inc(loaded[t % RING], 16)
                    for b in range(DEC if s.kind == "nsa" else 0):
                        t = stage_of["c", s.cache0 + DEC + b]
                        slot_free(t)
                        win = state_nsa_win[0, b].rearrange("(t p) h n -> p t (h n)", p=P)
                        for kt in range(2):
                            sp.dma_start(wstage[:, t % RING, kt, :], win[:, kt, :]).then_inc(loaded[t % RING], 16)
                for g, k in outs[2:]:
                    load_out(g, k)
                if s.kind == "nsa":
                    store(sp.dma_start(new_nsa_win_sample[0, :, 0:SEQ - 1].rearrange("b t h n -> b (t h n)"),
                                       state_nsa_win[0, :, 1:SEQ].rearrange("b t h n -> b (t h n)")),
                          win_moved, "win_moved")
            for signal in (gates_out, tok_stored, conv_stored, win_moved, y_stored):
                sp.wait_ge(signal, 16 * stores[signal.name])


_INS = ['x_prompt', 'x_sample', 'state_conv', 'cache_nsa', 'state_nsa_win', 'cache_diff', 'page_table', 'norm_g',
        'ffn_w_in', 'ffn_w_out', 'conv_w_in', 'conv_w', 'conv_w_out', 'nsa_w_in', 'nsa_w_cmp', 'nsa_w_out',
        'diff_w_in', 'diff_lambda', 'diff_subln_g', 'diff_w_out']
_OUTS = [(1, SEQ, D_MODEL), (DEC, 1, D_MODEL), (2, 1, 2, D_MODEL), (2, DEC, 2, D_MODEL), (1, 1, SEQ, 4, 256),
         (1, DEC, 1, 4, 256), (1, 1, SEQ, 4, 128), (1, DEC, SEQ, 4, 128), (1, 1, SEQ, 4, 256), (1, DEC, 1, 4, 256)]


def kernel(**inputs):
    import numpy as _np
    import concourse.bacc as _bacc
    from concourse import mybir as _mybir
    from concourse.bass_utils import run_bass_kernel_spmd as _run

    nc = _bacc.Bacc("TRN2", target_bir_lowering=False, num_devices=1)
    arrays, args = {}, []
    for name in _INS:
        a = _np.ascontiguousarray(inputs[name])
        arrays[f"in_{name}_dram"] = a
        args.append(nc.dram_tensor(f"in_{name}_dram", a.shape, _mybir.dt.from_np(a.dtype), kind="ExternalInput").ap())
    for i, shape in enumerate(_OUTS):
        args.append(nc.dram_tensor(f"out_{i}_dram", shape, _mybir.dt.float32, kind="ExternalOutput").ap())
    trunk_kernel(nc, *args)
    r = _run(nc, [arrays], core_ids=[0])
    return tuple(r.results[0][f"out_{i}_dram"] for i in range(len(_OUTS)))
```
